# Optimizing a Trainium2 kernel written in Bass

```python
import math
import jax, jax.numpy as jnp
from jax import lax
import numpy as np

D_MODEL = 1024
BATCH = 1
SEQ = 1024
DEPTH = 1

CHUNK = 64
N_META = 16
D_MIX = D_MODEL
D_A = D_MIX // 2
HEAD_A = 64
H_A = D_A // HEAD_A
LORA_W = 64
LORA_A = 64
LORA_G = 128
DECAY_SCALE = math.exp(-0.5)
GN_EPS_A = 64e-5
D_B = D_MIX - D_A
H_B = 4
HEAD_B = D_B // H_B
ROPE_BASE = 10000.0
GN_EPS_B = 1e-5
P_A = 3 * D_A + LORA_W + LORA_A + LORA_G
P_B = 4 * D_B
P_IN = P_A + P_B
N_GROUPS = 4
EXPERTS_PER_GROUP = 8
N_EXPERTS = N_GROUPS * EXPERTS_PER_GROUP
TOP_K = 2
D_EXPERT = 512
MOE_BLOCK = 128
NORM_EPS = 1e-6

kernel_name = 'hybrid_rwkv7_retention_hmoe'

def rmsnorm(x, g):
    xf = x.astype(jnp.float32)
    y = xf * lax.rsqrt(jnp.mean(xf * xf, axis=-1, keepdims=True) + NORM_EPS)
    return (y * g.astype(jnp.float32)).astype(x.dtype)

def head_norm(y, eps):
    mean = jnp.mean(y, axis=-1, keepdims=True)
    var = jnp.mean(jnp.square(y - mean), axis=-1, keepdims=True)
    return (y - mean) * lax.rsqrt(var + eps)

def rwkv7_mix(z, mu, decay_w0, decay_up, iclr_a0, iclr_up, gate_up, k_k, k_a, r_k, ln_w, ln_b):
    zf = z.astype(jnp.float32)
    z_prev = jnp.pad(zf, ((0, 0), (1, 0), (0, 0)))[:, :-1]
    zs = zf + (z_prev - zf) * mu
    offs = [D_A, 2 * D_A, 3 * D_A, 3 * D_A + LORA_W, 3 * D_A + LORA_W + LORA_A]
    r, k, v, w_lo, a_lo, g_lo = jnp.split(zs, offs, axis=-1)
    log_w = -DECAY_SCALE * jax.nn.sigmoid(decay_w0 + jnp.tanh(w_lo) @ decay_up)
    a = jax.nn.sigmoid(iclr_a0 + a_lo @ iclr_up)
    g = jax.nn.sigmoid(g_lo) @ gate_up
    B_, L_, _ = r.shape
    hs = lambda t: t.reshape(B_, L_, H_A, HEAD_A)
    r, k, v, a, log_w = hs(r), hs(k), hs(v), hs(a), hs(log_w)
    kk = k * k_k.reshape(H_A, HEAD_A)
    kk = kk / jnp.maximum(jnp.sqrt(jnp.sum(kk * kk, axis=-1, keepdims=True)), 1e-12)
    k = k * (1.0 + (a - 1.0) * k_a.reshape(H_A, HEAD_A))
    w = jnp.exp(log_w)

    def step(S, inp):
        r_t, w_t, k_t, v_t, kk_t, b_t = inp
        S = (S * w_t[:, :, None, :]
             + jnp.einsum('bhvk,bhk->bhv', S, -kk_t)[..., None] * b_t[:, :, None, :]
             + v_t[..., None] * k_t[:, :, None, :])
        return S, jnp.einsum('bhvk,bhk->bhv', S, r_t)

    xs = tuple(jnp.moveaxis(t, 1, 0) for t in (r, w, k, v, kk, kk * a))
    S0 = jnp.zeros((B_, H_A, HEAD_A, HEAD_A), jnp.float32)
    _, y = lax.scan(step, S0, xs)
    y = jnp.moveaxis(y, 0, 1)
    y = head_norm(y, GN_EPS_A).reshape(B_, L_, D_A) * ln_w + ln_b
    bonus = jnp.sum(r * k * r_k.reshape(H_A, HEAD_A), axis=-1, keepdims=True) * v
    return (y + bonus.reshape(B_, L_, D_A)) * g

def retention_mix(z, gn_w):
    zf = z.astype(jnp.float32)
    q, k, v, g = jnp.split(zf, 4, axis=-1)
    B_, L_, _ = q.shape
    q = q.reshape(B_, L_, H_B, HEAD_B)
    k = k.reshape(B_, L_, H_B, HEAD_B)
    v = v.reshape(B_, L_, H_B, HEAD_B)
    pos = jnp.arange(L_, dtype=jnp.float32)
    inv_freq = ROPE_BASE ** (-jnp.arange(0, HEAD_B, 2, dtype=jnp.float32) / HEAD_B)
    ang = pos[:, None] * inv_freq[None, :]
    cos = jnp.cos(ang)[None, :, None, :]
    sin = jnp.sin(ang)[None, :, None, :]

    def rope(t):
        t1, t2 = jnp.split(t, 2, axis=-1)
        return jnp.concatenate([t1 * cos - t2 * sin, t1 * sin + t2 * cos], axis=-1)

    q = rope(q)
    k = rope(k) * (HEAD_B ** -0.5)
    pad = (-L_) % CHUNK
    n_chunks = (L_ + pad) // CHUNK

    def chunked(t):
        t = jnp.pad(t, ((0, 0), (pad, 0), (0, 0), (0, 0)))
        return t.reshape(B_, n_chunks, CHUNK, H_B, HEAD_B).transpose(1, 0, 3, 2, 4)

    qc, kc, vc = chunked(q), chunked(k), chunked(v)
    log_gamma = jnp.log1p(-jnp.exp2(-5.0 - jnp.arange(H_B, dtype=jnp.float32)))
    idx = jnp.arange(CHUNK)
    rel = idx[:, None] - idx[None, :]
    decay_in = jnp.where(rel >= 0, jnp.exp(log_gamma[:, None, None] * jnp.maximum(rel, 0).astype(jnp.float32)), 0.0)
    q_decay = jnp.exp(log_gamma[:, None] * (idx + 1).astype(jnp.float32))
    k_decay = jnp.exp(log_gamma[:, None] * (CHUNK - 1 - idx).astype(jnp.float32))
    chunk_decay = jnp.exp(log_gamma * CHUNK)
    scores = jnp.einsum('nbhcd,nbhmd->nbhcm', qc, kc) * decay_in
    inner = jnp.einsum('nbhcm,nbhme->nbhce', scores, vc)

    def step(R, inp):
        q_c, k_c, v_c = inp
        cross = jnp.einsum('bhcd,bhde->bhce', q_c, R) * q_decay[None, :, :, None]
        R = R * chunk_decay[None, :, None, None] + jnp.einsum('bhmd,bhme->bhde', k_c * k_decay[None, :, :, None], v_c)
        return R, cross

    R0 = jnp.zeros((B_, H_B, HEAD_B, HEAD_B), jnp.float32)
    _, cross = lax.scan(step, R0, (qc, kc, vc))
    y = (inner + cross).transpose(1, 0, 3, 2, 4).reshape(B_, n_chunks * CHUNK, H_B, HEAD_B)[:, pad:]
    y = head_norm(y, GN_EPS_B).reshape(B_, L_, D_B) * gn_w
    return y * jax.nn.silu(g)

def hier_moe(u, w_rg, b_rg, w_re, b_re, w_gate, w_up, w_down):
    B_, L_, D_ = u.shape
    T = B_ * L_
    uf = u.reshape(T, D_)
    group_prob = jax.nn.softmax((uf @ w_rg).astype(jnp.float32) + b_rg.astype(jnp.float32), axis=-1)
    g_p, g_idx = lax.top_k(group_prob, 1)
    exp_logits = ((uf @ w_re).astype(jnp.float32) + b_re.astype(jnp.float32)).reshape(T, N_GROUPS, EXPERTS_PER_GROUP)
    exp_logits = exp_logits[jnp.arange(T), g_idx[:, 0]]
    e_p, e_idx = lax.top_k(jax.nn.softmax(exp_logits, axis=-1), TOP_K)
    weight = g_p * e_p / jnp.sum(e_p, axis=-1, keepdims=True)
    expert = g_idx * EXPERTS_PER_GROUP + e_idx
    n_assign = T * TOP_K
    e_flat = expert.reshape(-1).astype(jnp.int32)
    w_flat = weight.reshape(-1)
    tok_flat = jnp.repeat(jnp.arange(T, dtype=jnp.int32), TOP_K)
    order = jnp.argsort(e_flat)
    e_s, w_s, tok_s = e_flat[order], w_flat[order], tok_flat[order]
    counts = jnp.zeros((N_EXPERTS,), jnp.int32).at[e_flat].add(1)
    padded = (counts + MOE_BLOCK - 1) // MOE_BLOCK * MOE_BLOCK
    pad_end = jnp.cumsum(padded)
    pad_start = pad_end - padded
    raw_start = jnp.cumsum(counts) - counts
    dest = pad_start[e_s] + jnp.arange(n_assign, dtype=jnp.int32) - raw_start[e_s]
    n_blocks = -(-(n_assign + N_EXPERTS * (MOE_BLOCK - 1)) // MOE_BLOCK)
    n_rows = n_blocks * MOE_BLOCK
    row_tok = jnp.zeros((n_rows,), jnp.int32).at[dest].set(tok_s)
    row_w = jnp.zeros((n_rows,), jnp.float32).at[dest].set(w_s)
    block_expert = jnp.minimum(jnp.searchsorted(pad_end, jnp.arange(n_blocks, dtype=jnp.int32) * MOE_BLOCK, side='right'), N_EXPERTS - 1)
    x_rows = uf[row_tok].reshape(n_blocks, MOE_BLOCK, D_)

    def run_block(args):
        xb, e = args
        hid = jax.nn.silu(xb @ w_gate[e]) * (xb @ w_up[e])
        return hid @ w_down[e]

    y_rows = lax.map(run_block, (x_rows, block_expert)).reshape(n_rows, D_)
    out = jnp.zeros((T, D_), u.dtype).at[row_tok].add(y_rows * row_w[:, None].astype(u.dtype))
    return out.reshape(B_, L_, D_)

def setup_inputs(seed: int = 0) -> dict:
    key = jax.random.key(seed)
    ks = iter(jax.random.split(key, 32))
    f32 = jnp.float32
    nrm = lambda shape, scale: jax.random.normal(next(ks), shape, f32) * scale
    D = D_MODEL
    return {
        'x': nrm((BATCH, SEQ, D), 1.0),
        'meta_tokens': nrm((N_META, D), 1.0),
        'norm_mix': 1.0 + nrm((DEPTH, D), 0.02),
        'w_in': nrm((DEPTH, D, P_IN), D ** -0.5),
        'shift_mu': jax.random.uniform(next(ks), (DEPTH, P_A), f32, 0.1, 0.9),
        'decay_w0': jax.random.uniform(next(ks), (DEPTH, D_A), f32, -3.0, 3.0),
        'decay_up': nrm((DEPTH, LORA_W, D_A), 0.5 * LORA_W ** -0.5),
        'iclr_a0': nrm((DEPTH, D_A), 0.5),
        'iclr_up': nrm((DEPTH, LORA_A, D_A), 0.5 * LORA_A ** -0.5),
        'gate_up': nrm((DEPTH, LORA_G, D_A), LORA_G ** -0.5),
        'k_k': 0.85 + nrm((DEPTH, D_A), 0.05),
        'k_a': 1.0 + nrm((DEPTH, D_A), 0.05),
        'r_k': nrm((DEPTH, D_A), 0.1),
        'ln_w_a': 1.0 + nrm((DEPTH, D_A), 0.02),
        'ln_b_a': nrm((DEPTH, D_A), 0.02),
        'gn_w_b': 1.0 + nrm((DEPTH, D_B), 0.02),
        'w_out': nrm((DEPTH, D_MIX, D), D_MIX ** -0.5),
        'norm_ffn': 1.0 + nrm((DEPTH, D), 0.02),
        'router_group_w': nrm((DEPTH, D, N_GROUPS), D ** -0.5),
        'router_group_b': nrm((DEPTH, N_GROUPS), 0.01),
        'router_expert_w': nrm((DEPTH, D, N_EXPERTS), D ** -0.5),
        'router_expert_b': nrm((DEPTH, N_EXPERTS), 0.01),
        'moe_w_gate': nrm((DEPTH, N_EXPERTS, D, D_EXPERT), D ** -0.5),
        'moe_w_up': nrm((DEPTH, N_EXPERTS, D, D_EXPERT), D ** -0.5),
        'moe_w_down': nrm((DEPTH, N_EXPERTS, D_EXPERT, D), D_EXPERT ** -0.5),
        'norm_final': 1.0 + nrm((D,), 0.02),
    }

def reference(x, meta_tokens, norm_mix, w_in, shift_mu, decay_w0, decay_up, iclr_a0, iclr_up, gate_up,
              k_k, k_a, r_k, ln_w_a, ln_b_a, gn_w_b, w_out, norm_ffn, router_group_w, router_group_b,
              router_expert_w, router_expert_b, moe_w_gate, moe_w_up, moe_w_down, norm_final):
    B_ = x.shape[0]
    meta = jnp.broadcast_to(meta_tokens[None].astype(x.dtype), (B_, N_META, x.shape[-1]))
    h = jnp.concatenate([meta, x], axis=1)
    for i in range(DEPTH):
        u = rmsnorm(h, norm_mix[i])
        z = u @ w_in[i]
        y_a = rwkv7_mix(z[..., :P_A], shift_mu[i], decay_w0[i], decay_up[i], iclr_a0[i], iclr_up[i], gate_up[i],
                        k_k[i], k_a[i], r_k[i], ln_w_a[i], ln_b_a[i])
        y_b = retention_mix(z[..., P_A:], gn_w_b[i])
        mixed = jnp.concatenate([y_a, y_b], axis=-1).astype(h.dtype)
        h = h + mixed @ w_out[i]
        u = rmsnorm(h, norm_ffn[i])
        h = h + hier_moe(u, router_group_w[i], router_group_b[i], router_expert_w[i], router_expert_b[i],
                         moe_w_gate[i], moe_w_up[i], moe_w_down[i])
    return rmsnorm(h, norm_final)[:, N_META:]


_drawn_inputs = setup_inputs


def setup_inputs(seed=0):
    import zlib

    import numpy as np

    out = dict(_drawn_inputs(seed))
    spreads = {}
    factors = {'k_k': 12.132,
     'ln_w_a': 11.381,
     'ln_b_a': 12.337,
     'gn_w_b': 9.553,
     'router_group_b': 19.445,
     'router_expert_b': 21.707,
     'norm_final': 7.85,
     'norm_ffn': 3.857}
    for name, (base, spread) in spreads.items():
        noise = np.random.default_rng([zlib.crc32(name.encode()), seed]).standard_normal(out[name].shape)
        drawn = base * np.exp(spread * noise) if base else spread * noise
        out[name] = __import__('jax').numpy.asarray(drawn.astype(out[name].dtype))
    for name, factor in factors.items():
        out[name] = (out[name] * factor).astype(out[name].dtype)
    return out
```

```python
from contextlib import ExitStack
import math

import numpy as np

import concourse.bass as bass
from concourse import mybir

F32, F32R, I32 = mybir.dt.float32, mybir.dt.float32r, mybir.dt.int32
ACT = mybir.ActivationFunctionType
ALU = mybir.AluOpType
X = mybir.AxisListType.X

P = 128
D = 1024
KD = D // P
SEQ = 1024
N_META = 16
NT = SEQ // P + 1
PAD = P - N_META
ROWS = NT * P
C = 64
DA, HA, HEAD_A = 512, 8, 64
DB, HB, HEAD_B = 512, 4, 128
PA, PB = 3 * DA + 256, 4 * DB
PIN = PA + PB
GROUP_COLS = 480
NGRP = PIN // GROUP_COLS
N_GROUPS, PER_GROUP, NE = 4, 8, 32
NR = N_GROUPS + NE
DE = 512
KE = DE // P
DECAY = math.exp(-0.5)
EXTRA = (2 * SEQ - 1) // P
NBLK = NE + EXTRA
SUB = 16

CONST_PARTS = [
    ("ident", P), ("cum_in", P), ("cum_ex", P), ("after", P), ("chunk_of", 2),
    ("lt_sub", C), ("gt_sub", C), ("gt_off", C), ("lt", C), ("le", C), ("ident_c", C),
    ("before", P), ("ones", P),
    ("ret_mask", HB * C), ("q_decay", HB), ("k_decay", HB), ("r_decay", HB),
    ("group_prio", N_GROUPS), ("expert_prio", NE), ("slot_base", NE), ("before_e", NE * NE),
    ("thresholds", 8), ("block_no", EXTRA),
]
CONST_AT, _n = {}, 0
for _name, _w in CONST_PARTS:
    CONST_AT[_name] = (_n, _n + _w)
    _n += _w
NCONST = _n


def shape_constants():
    c = {}
    p = np.arange(P)[:, None]
    q = np.arange(P)[None, :]
    same = p // C == q // C
    c["ident"] = p == q
    c["cum_in"] = same & (p <= q)
    c["cum_ex"] = same & (p < q)
    c["after"] = same & (p > q)
    c["chunk_of"] = p // C == np.arange(2)[None, :]
    s = p % C
    t = np.arange(C)[None, :]
    sub = s // SUB == t // SUB
    c["lt_sub"] = (s < t) & sub
    c["gt_sub"] = (s > t) & sub
    c["gt_off"] = (s > t) & ~sub
    c["lt"] = s < t
    c["le"] = s <= t
    c["ident_c"] = s == t
    c["before"] = p < q
    c["ones"] = np.ones((P, P))
    lg = np.log1p(-np.exp2(-5.0 - np.arange(HB)))
    scale = HEAD_B ** -0.5
    rel = t - s
    c["ret_mask"] = np.concatenate([np.where(rel >= 0, np.exp(g * np.maximum(rel, 0)), 0.0) * scale for g in lg], 1)
    c["q_decay"] = np.exp(lg[None, :] * (s + 1))
    c["k_decay"] = np.exp(lg[None, :] * (C - 1 - s)) * scale
    c["r_decay"] = np.exp(lg * C)[None, :] + np.zeros((P, 1))
    c["group_prio"] = np.arange(N_GROUPS, 0, -1)[None, :] + np.zeros((P, 1))
    c["expert_prio"] = np.arange(NE, 0, -1)[None, :] + np.zeros((P, 1))
    c["slot_base"] = np.arange(NE)[None, :] * P + np.zeros((P, 1))
    e = np.arange(NE)
    c["before_e"] = (e[None, :] < e[:, None]).reshape(1, -1) + np.zeros((P, 1))
    c["thresholds"] = (np.arange(8) + 1)[None, :] * P + np.zeros((P, 1))
    c["block_no"] = np.arange(EXTRA)[None, :] + np.zeros((P, 1))
    table = np.zeros((P, NCONST), np.float32)
    for name, (a, b) in CONST_AT.items():
        table[:, a:b] = c[name]
    pos = np.maximum(np.arange(ROWS) - PAD, 0).astype(np.float32)
    inv = (np.float32(10000.0) ** (-np.arange(0, HEAD_B, 2, dtype=np.float32) / np.float32(HEAD_B))).astype(np.float32)
    ang = (pos[:, None] * inv[None, :]).astype(np.float32)
    rot = np.concatenate([np.cos(ang.astype(np.float64)), np.sin(ang.astype(np.float64))], 1).astype(np.float32)
    return table, rot


class Turn:
    def __init__(self, i, after):
        self.i, self.after = i, after
        self.has_before = not (isinstance(i, int) and i == 0)

    def lead(self, eng):
        if not isinstance(self.i, int):
            eng.wait_ge(self.loaded, 16)


def layer(nc, d, out):
    with ExitStack() as top:
        sems = {}

        def sem(name):
            if name not in sems:
                sems[name] = nc.alloc_semaphore(name=name)
            return sems[name]

        def free_sems():
            names = [n for n in sems if n != "consts_loaded"]
            nc.clear_and_free_semaphores([sems.pop(n) for n in names])
            nc.all_engine_barrier()

        def tile(stack, name, shape, dt=F32):
            return stack.enter_context(nc.sbuf_tensor(name, shape, dt))

        scr = lambda name, shape, dt=F32: nc.dram_tensor(name, shape, dt, kind="Internal").ap()
        z_dram = scr("z_rows", (ROWS + 1, PIN))
        h2_dram = scr("h2_rows", (ROWS, D))
        u2_dram = scr("u2_rows", (ROWS, D))
        y_dram = scr("y_slots", (NBLK * P, D))
        slot_row_dram = scr("slot_rows", (NBLK * P, 1))

        ps = top.enter_context(nc.psum_tensor("ps", [P, 8, 512], F32))
        consts = tile(top, "consts", [P, NCONST])
        logits = tile(top, "logits", [P, NT, NR])
        half = tile(top, "minus_half", [P, 8])

        def cst(name):
            a, b = CONST_AT[name]
            return consts[:, a:b]

        ident = cst("ident")

        Turn.loaded = sem("consts_loaded")
        project(nc, d, locals())
        free_sems()
        mix(nc, d, locals())
        free_sems()
        dispatch_and_experts(nc, d, out, locals())


def project(nc, d, env):
    sem, tile, ps, ident, z_dram, consts, half = (env[k] for k in ("sem", "tile", "ps", "ident", "z_dram", "consts", "half"))
    y_dram = env["y_dram"]
    with ExitStack() as s:
        u_hi = tile(s, "u_hi", [P, KD, ROWS], F32R)
        u_lo = tile(s, "u_lo", [P, KD, ROWS], F32R)
        h_in = [tile(s, f"h_in{b}", [P, D]) for b in range(2)]
        u = [tile(s, f"u{b}", [P, D]) for b in range(2)]
        gain = tile(s, "norm_mix_rows", [P, D])
        stat = tile(s, "stat", [P, 3, 2])
        w_raw = [tile(s, f"w_raw{b}", [P, KD, GROUP_COLS]) for b in range(2)]
        w_hi = [tile(s, f"w_hi{b}", [P, KD, GROUP_COLS], F32R) for b in range(2)]
        w_lo = [tile(s, f"w_lo{b}", [P, KD, GROUP_COLS], F32R) for b in range(2)]
        z_out = [tile(s, f"z_out{b}", [P, GROUP_COLS]) for b in range(3)]
        zero_row = u[1]
        w_view = d["w_in"].rearrange("(k p) n -> p k n", p=P)
        x = d["x"]

        def run_tiles(eng, body):
            body(Turn(0, 1), 0, 0)
            with eng.Fori(0, (NT - 1) // 2) as i:
                n = [eng.snap(2 * i + 1), eng.snap(2 * i + 2), eng.snap(2 * i + 3)]
                body(Turn(n[0], n[1]), 1, i)
                body(Turn(n[1], n[2]), 0, i + 1)

        def run_groups(eng, body):
            body(0, 0, 0, False)
            with eng.Fori(0, NGRP // 2 - 1) as i:
                body(2 * i + 1, 1, i, False)
                body(2 * i + 2, 0, i + 1, False)
            body(NGRP - 1, 1, NGRP // 2 - 1, True)

        with nc.Block() as block:
            @block.sync
            def _(sp):
                sp.dma_start(consts[:], d["consts"]).then_inc(sem("consts_loaded"), 16)
                sp.dma_start(gain[:], d["norm_mix"].partition_broadcast(P)).then_inc(sem("gain_loaded"), 16)
                sp.dma_start(w_raw[0][:], w_view[:, :, 0:GROUP_COLS]).then_inc(sem("w_loaded0"), 16)

                def load_tile(t, b, n):
                    if isinstance(t.i, int):
                        sp.wait_ge(sem("h0_zeroed"), 1)
                        sp.dma_start(h_in[0][PAD:P, :], d["meta_tokens"]).then_inc(sem("h_loaded0"), 16)
                        return
                    sp.wait_ge(sem("u_ready"), t.i)
                    sp.dma_start(h_in[b][:], x[bass.ds((t.i - 1) * P, P), :]).then_inc(sem(f"h_loaded{b}"), 16)
                run_tiles(sp, load_tile)
                sp.wait_ge(sem("zero_row_ready"), 1)
                for i in range(PIN // 960):
                    sp.dma_start(z_dram[0:1, i * 960:(i + 1) * 960], zero_row[0:1, 0:960]).then_inc(sem("zero_stored"), 16)

                for i in range(EXTRA):
                    sp.dma_start(y_dram[(NE + i) * P:(NE + i + 1) * P, :], zero_row[:]).then_inc(sem("zero_stored"), 16)

                def group(g, b, n, last):
                    if not last:
                        if not (isinstance(g, int) and g == 0):
                            sp.wait_ge(sem("w_lo_ready"), g)
                        sp.dma_start(w_raw[1 - b][:], w_view[:, :, bass.ds((g + 1) * GROUP_COLS, GROUP_COLS)]
                                     ).then_inc(sem(f"w_loaded{1 - b}"), 16)
                    for t in range(NT):
                        sp.wait_ge(sem("z_evacuated"), g * NT + t + 1)
                        sp.dma_start(z_dram[1 + t * P:1 + (t + 1) * P, bass.ds(g * GROUP_COLS, GROUP_COLS)],
                                     z_out[t % 3][:]).then_inc(sem(f"z_stored{t % 3}"), 16)
                run_groups(sp, group)
                for r in range(3):
                    sp.wait_ge(sem(f"z_stored{r}"), 16 * (NT // 3) * NGRP)
                sp.wait_ge(sem("zero_stored"), 16 * (PIN // 960 + EXTRA))

            @block.scalar
            def _(act):
                def square(t, b, n):
                    act.wait_ge(sem(f"h_loaded{b}"), 16 * (n + 1))
                    if not isinstance(t.i, int):
                        act.wait_ge(sem("u_ready"), t.i)
                        act.wait_ge(sem("u_turned"), t.i)
                    act.activation(u[b][:], h_in[b][:], ACT.Square, scale=D ** -0.5,
                                   accum_out=stat[:, 0, b:b + 1]).then_inc(sem("mean_square"), 1)
                    act.wait_ge(sem("u_turned"), t.after)
                    act.activation(u_hi[:, :, bass.ds(t.i * P, P)],
                                   ps[:, 2 * b:2 * b + 2, :].rearrange("p a (k t) -> p (a k) t", t=P),
                                   ACT.Copy).then_inc(sem("u_hi_ready"), 1)
                run_tiles(act, square)

                def split(g, b, n):
                    act.wait_ge(sem(f"w_loaded{b}"), 16 * (n + 1))
                    if not (isinstance(g, int) and g < 2):
                        act.wait_ge(sem("z_ready"), (g - 1) * NT)
                    act.activation(w_hi[b][:], w_raw[b][:], ACT.Copy).then_inc(sem("w_hi_ready"), 1)
                split(0, 0, 0)

                def group(g, b, n, last):
                    if not last:
                        split(g + 1, 1 - b, n + b)
                    for t in range(NT):
                        act.wait_ge(sem("z_ready"), g * NT + t + 1)
                        if not (isinstance(g, int) and g == 0 and t < 3):
                            act.wait_ge(sem(f"z_stored{t % 3}"), 16 * (g * (NT // 3) + t // 3))
                        act.activation(z_out[t % 3][:], ps[:, 4 + t % 3, 0:GROUP_COLS], ACT.Copy
                                       ).then_inc(sem("z_evacuated"), 1)
                run_groups(act, group)

            @block.gpsimd
            def _(pool):
                pool.memset(half[:], -0.5).then_inc(sem("half_ready"), 1)
                pool.wait_ge(sem("half_ready"), 1)

                def rstd(t, b, n):
                    pool.wait_ge(sem("mean_eps"), t.after)
                    pool.tensor_tensor(stat[:, 2, b:b + 1], stat[:, 1, b:b + 1], half[:, 0:1], ALU.pow
                                       ).then_inc(sem("rstd_ready"), 1)
                run_tiles(pool, rstd)

            @block.vector
            def _(dve):
                dve.memset(h_in[0][:], 0.0).then_inc(sem("h0_zeroed"), 1)
                dve.wait_ge(sem("gain_loaded"), 16)

                def norm(t, b, n):
                    dve.wait_ge(sem("mean_square"), t.after)
                    dve.tensor_scalar(stat[:, 1, b:b + 1], stat[:, 0, b:b + 1], 1e-6, None, ALU.add
                                      ).then_inc(sem("mean_eps"), 1)
                    dve.wait_ge(sem("rstd_ready"), t.after)
                    dve.scalar_tensor_tensor(u[b][:], h_in[b][:], stat[:, 2, b:b + 1], gain[:], ALU.mult, ALU.mult
                                             ).then_inc(sem("u_ready"), 1)
                    dve.wait_ge(sem("u_hi_ready"), t.after)
                    dve.tensor_tensor(u_lo[:, :, bass.ds(t.i * P, P)],
                                      ps[:, 2 * b:2 * b + 2, :].rearrange("p a (k t) -> p (a k) t", t=P),
                                      u_hi[:, :, bass.ds(t.i * P, P)].bitcast(F32), ALU.subtract
                                      ).then_inc(sem("u_lo_ready"), 1)
                run_tiles(dve, norm)
                dve.wait_ge(sem("u_turned"), NT)
                dve.memset(zero_row[:], 0.0).then_inc(sem("zero_row_ready"), 1)

                def low(g, b, n):
                    dve.wait_ge(sem("w_hi_ready"), g + 1)
                    dve.tensor_tensor(w_lo[b][:], w_raw[b][:], w_hi[b][:].bitcast(F32), ALU.subtract
                                      ).then_inc(sem("w_lo_ready"), 1)
                low(0, 0, 0)
                low(1, 1, 0)
                with dve.Fori(1, NGRP // 2) as i:
                    low(2 * i, 0, i)
                    low(2 * i + 1, 1, i)

            @block.tensor
            def _(pe):
                pe.wait_ge(sem("consts_loaded"), 16)

                def turn(t, b, n):
                    if t.has_before:
                        pe.wait_ge(sem("u_lo_ready"), t.i)
                    t.lead(pe)
                    pe.wait_ge(sem("u_ready"), t.after)
                    for k in range(KD):
                        last = pe.transpose(ps[:, 2 * b + k // 4, (k % 4) * P:(k % 4 + 1) * P],
                                            u[b][:, k * P:(k + 1) * P], ident)
                    last.then_inc(sem("u_turned"), 1)
                run_tiles(pe, turn)
                pe.wait_ge(sem("u_lo_ready"), NT)

                def group(g, b, n, last):
                    pe.wait_ge(sem("w_hi_ready"), g + 1)
                    pe.wait_ge(sem("w_lo_ready"), g + 1)
                    for t in range(NT):
                        if not (isinstance(g, int) and g == 0 and t < 3):
                            pe.wait_ge(sem("z_evacuated"), g * NT + t - 2)
                        acc = ps[:, 4 + t % 3, 0:GROUP_COLS]
                        for k in range(KD):
                            for a, w, n3 in ((u_hi, w_hi, 0), (u_hi, w_lo, 1), (u_lo, w_hi, 2)):
                                mm = pe.matmul(acc, a[:, k, t * P:(t + 1) * P], w[b][:, k, :],
                                               start=(k == 0 and n3 == 0), stop=(k == KD - 1 and n3 == 2))
                        mm.then_inc(sem("z_ready"), 1)
                run_groups(pe, group)


def mix(nc, d, env):
    sem, tile, ps, ident, cst = (env[k] for k in ("sem", "tile", "ps", "ident", "cst"))
    z_dram, h2_dram, u2_dram, consts, half, logits = (
        env[k] for k in ("z_dram", "h2_dram", "u2_dram", "consts", "half", "logits"))
    with ExitStack() as s:
        def sb(name, *shape):
            return tile(s, name, [P, *shape])

        mu = sb("mu", PA)
        rows = {n: sb(n + "_rows", DA) for n in ("decay_w0", "iclr_a0", "k_k", "k_a", "r_k", "ln_w_a", "ln_b_a", "gn_w_b")}
        gain = sb("norm_ffn_rows", D)
        router_b = sb("router_b", NR)
        lora_up = sb("lora_up", DA)
        gate_up = sb("gate_up", DA)
        w_out = sb("w_out", KD, D)
        router_w = sb("router_w", KD, NR)

        z_cur, z_prev, z_ret = sb("z_cur", PA), sb("z_prev", PA), sb("z_ret", PB)
        rot, h_in = sb("rot", 2 * C), sb("h_res", D)
        zs = sb("zs", PA)
        r, k, v = (zs[:, i * DA:(i + 1) * DA] for i in range(3))

        lora_t, gate_t = sb("lora_t", P), sb("gate_t", P)
        log_w, iclr, gate, kk, k2, b_row, e_in, e_neg, e_ex, e_after, r_d, k_d, b_d, a_d, r_t, a_t, tmp = (
            sb(n, DA) for n in ("log_w", "iclr", "gate", "kk", "k2", "b_row", "e_in", "e_neg", "e_ex", "e_after",
                                "r_d", "k_d", "b_d", "a_d", "r_t", "a_t", "tmp"))
        after_pair, turned_pair = sb("after_pair", D), sb("turned_pair", D)
        k_h, b_h = after_pair[:, 0:DA], after_pair[:, DA:D]
        k_t, b_t = turned_pair[:, 0:DA], turned_pair[:, DA:D]
        stat = sb("mix_stat", 10, HA)
        decay_c = sb("decay_c", HA)
        ld_t, ld, lo = e_in, e_neg, e_ex
        ak_t, rb_t, rk_t = sb("ak_t", DA), sb("rb_t", DA), sb("rk_t", DA)
        l2, l2_t, l4, l4_t, l8 = log_w, kk, b_row, r_d, k_d
        inv = sb("inv", DA)
        x_m, x_t, x2_t, q_m = e_after, e_in, e_neg, b_d
        z0, z1, w_m = sb("z0", 2, DA), sb("z1", 2, DA), sb("w_m", 2, DA)
        diag_c = iclr[:].rearrange("p (c k) -> p c k", c=2)
        m_t = z1
        n_m = sb("n_m", 2, DA // 2)
        state = [sb(f"state{i}", DA // 2) for i in range(2)]
        rz_t, y = l4_t, inv
        bonus = sb("bonus", DA)

        z_cos, z_sin, qk = sb("z_cos", D), sb("z_sin", D), sb("qk", D)
        q_t, kr_t, k_dec, s_t = sb("q_t", DB), sb("kr_t", DB), sb("k_dec", DB), sb("s_t", HB * C)
        memory = [sb(f"memory{i}", DB) for i in range(2)]
        memory_d = a_t
        in_s, y_ret, ret_gate = sb("in_s", DB), sb("y_ret", DB), sb("ret_gate", DB)
        ret_tmp = tmp
        mixed_t = z_cos[:].rearrange("p (k t) -> p k t", t=P)
        h2, u2 = after_pair, z_sin
        u2_t = h_in[:].rearrange("p (k t) -> p k t", t=P)

        def heads(ap, n=HA):
            return ap.rearrange("p (h c) -> p h c", h=n)

        def per_head(small, n=HA):
            return small.unsqueeze(2).to_broadcast([P, n, DA // n])

        def parity(ap):
            return ap.rearrange("p (q a c) -> p a q c", a=2, c=C)

        def bank_pair(b, at=0):
            return ps[:, b:b + 2, at:at + 256].rearrange("p a (q c) -> p a q c", c=C)

        def all_heads(mask):
            return mask.unsqueeze(1).to_broadcast([P, HA, C])

        def all_pairs(mask):
            return mask.unsqueeze(1).unsqueeze(1).to_broadcast([P, 2, 4, C])

        def run(eng, body):
            body(Turn(0, 1))
            with eng.Fori(2, NT) as v_:
                body(Turn(v_ - 1, v_))
            body(Turn(NT - 1, NT))

        def at(t, n=P):
            return slice(t.i * n, (t.i + 1) * n) if isinstance(t.i, int) else bass.ds(t.i * n, n)

        with nc.Block() as block:
            @block.sync
            def _(sp):
                def row(dst, name):
                    sp.dma_start(dst, d[name].partition_broadcast(P)).then_inc(sem("mix_params"), 16)
                row(mu[:], "shift_mu")
                for n, t_ in rows.items():
                    row(t_[:], n)
                row(gain[:], "norm_ffn")
                row(router_b[:, 0:N_GROUPS], "router_group_b")
                row(router_b[:, N_GROUPS:NR], "router_expert_b")
                load = lambda dst, src: sp.dma_start(dst, src).then_inc(sem("mix_params"), 16)
                load(lora_up[0:C, :], d["decay_up"])
                load(lora_up[C:P, :], d["iclr_up"])
                load(gate_up[:], d["gate_up"])
                load(w_out[:], d["w_out"].rearrange("(k p) n -> p k n", p=P))
                load(router_w[:, :, 0:N_GROUPS], d["router_group_w"].rearrange("(k p) n -> p k n", p=P))
                load(router_w[:, :, N_GROUPS:NR], d["router_expert_w"].rearrange("(k p) n -> p k n", p=P))
                sp.wait_ge(sem("h_res_zeroed"), 1)

                def store(n):
                    sp.wait_ge(sem("h2_ready"), n)
                    sp.dma_start(h2_dram[bass.ds((n - 1) * P, P), :], h2[:]).then_inc(sem("h2_stored"), 16)
                    sp.wait_ge(sem("u2_ready"), n)
                    sp.dma_start(u2_dram[bass.ds((n - 1) * P, P), :], u2[:]).then_inc(sem("u2_stored"), 16)

                def body(t):
                    if t.has_before:
                        sp.wait_ge(sem("zs_ready"), t.i)
                        sp.wait_ge(sem("zs_k_ready"), t.i)
                    sp.dma_start(z_cur[:], z_dram[bass.ds(t.i * P + 1, P), 0:PA]).then_inc(sem("z_cur_loaded"), 16)
                    sp.dma_start(z_prev[:], z_dram[bass.ds(t.i * P, P), 0:PA]).then_inc(sem("z_prev_loaded"), 16)
                    if t.has_before:
                        sp.wait_ge(sem("mixed_b_ready"), t.i)
                    sp.dma_start(z_ret[:], z_dram[bass.ds(t.i * P + 1, P), PA:PIN]).then_inc(sem("z_ret_loaded"), 16)
                    sp.dma_start(rot[:], d["rotation"][bass.ds(t.i * P, P), :]).then_inc(sem("rot_loaded"), 16)
                    if isinstance(t.i, int) and t.i == 0:
                        sp.dma_start(h_in[PAD:P, :], d["meta_tokens"]).then_inc(sem("h_res_loaded"), 16)
                    else:
                        store(t.i)
                        sp.wait_ge(sem("router_done"), t.i)
                        sp.dma_start(h_in[:], d["x"][bass.ds((t.i - 1) * P, P), :]).then_inc(sem("h_res_loaded"), 16)
                run(sp, body)
                store(NT)
                sp.wait_ge(sem("h2_stored"), 16 * NT)
                sp.wait_ge(sem("u2_stored"), 16 * NT)

            @block.gpsimd
            def _(pool):
                for ap in (state[0], memory[0]):
                    pool.memset(ap[:], 0.0).then_inc(sem("states_zeroed"), 1)
                pool.wait_ge(sem("mix_params"), 16 * 17)

                def head_a_rstd(n):
                    pool.wait_ge(sem("head_a_rstd_in"), n)
                    pool.tensor_tensor(stat[:, 4, :], stat[:, 3, :], half[:, 0:HA], ALU.pow).then_inc(sem("head_a_rstd"), 1)

                def h2_rstd(n):
                    pool.wait_ge(sem("h2_rstd_in"), n)
                    pool.tensor_tensor(stat[:, 7, 1:2], stat[:, 7, 0:1], half[:, 0:1], ALU.pow).then_inc(sem("h2_rstd"), 1)

                def r_and_v(ap):
                    return ap[:, 0:4 * DA].rearrange("p (a c) -> p a c", c=2 * DA)[:, :, 0:DA]

                def body(t):
                    pool.wait_ge(sem("z_cur_loaded"), t.after * 16)
                    pool.wait_ge(sem("z_prev_loaded"), t.after * 16)
                    pool.tensor_tensor(z_prev[:], z_prev[:], z_cur[:], ALU.subtract).then_inc(sem("shift_diff"), 1)
                    pool.wait_ge(sem("shift_diff"), t.after)
                    pool.tensor_tensor(z_prev[:], z_prev[:], mu[:], ALU.mult).then_inc(sem("shift_scaled"), 1)
                    pool.wait_ge(sem("shift_scaled"), t.after)
                    if t.has_before:
                        pool.wait_ge(sem("y0_done"), t.i)
                        pool.wait_ge(sem("bonus_ready"), t.i)
                    pool.tensor_tensor(zs[:, 0:DA], z_prev[:, 0:DA], z_cur[:, 0:DA], ALU.add).then_inc(sem("zs_r_ready"), 1)
                    pool.tensor_tensor(v, z_prev[:, 2 * DA:3 * DA], z_cur[:, 2 * DA:3 * DA], ALU.add).then_inc(sem("zs_ready"), 1)
                    if t.has_before:
                        head_a_rstd(t.i)
                    pool.wait_ge(sem("kk_rnorm_in"), t.after)
                    pool.tensor_tensor(stat[:, 1, :], stat[:, 0, :], half[:, 0:HA], ALU.pow).then_inc(sem("kk_rnorm"), 1)
                    pool.wait_ge(sem("decay_c_ready"), t.after)
                    pool.wait_ge(sem("b_d_ready"), t.after)
                    pool.tensor_tensor(diag_c.rearrange("p c (q k) -> p c q k", k=C),
                                       all_pairs(cst("ident_c")),
                                       decay_c[:].rearrange("p (q c) -> p c q", c=2).unsqueeze(3).to_broadcast([P, 2, 4, C]),
                                       ALU.mult).then_inc(sem("diag_c_ready"), 1)
                    if t.has_before:
                        h2_rstd(t.i)
                    pool.wait_ge(sem("z_ret_loaded"), t.after * 16)
                    pool.wait_ge(sem("rot_loaded"), t.after * 16)
                    if t.has_before:
                        pool.wait_ge(sem("proj_done"), t.i)
                        pool.wait_ge(sem("u2_turned1"), t.i)
                        pool.wait_ge(sem("u2_stored"), t.i * 16)
                    zq = z_ret[:, 0:D].rearrange("p (h c) -> p h c", c=C)
                    halves = lambda ap: ap[:].rearrange("p (h a c) -> p h a c", a=2, c=C)
                    pool.tensor_tensor(z_cos[:].rearrange("p (h c) -> p h c", c=C), zq,
                                       rot[:, 0:C].unsqueeze(1).to_broadcast([P, 16, C]), ALU.mult
                                       ).then_inc(sem("z_cos_ready"), 1)
                    pool.tensor_tensor(z_sin[:].rearrange("p (h c) -> p h c", c=C), zq,
                                       rot[:, C:2 * C].unsqueeze(1).to_broadcast([P, 16, C]), ALU.mult
                                       ).then_inc(sem("z_sin_ready"), 1)
                    pool.wait_ge(sem("z_cos_ready"), t.after)
                    pool.wait_ge(sem("z_sin_ready"), t.after)
                    pool.tensor_tensor(halves(qk)[:, :, 0, :], halves(z_cos)[:, :, 0, :], halves(z_sin)[:, :, 1, :],
                                       ALU.subtract).then_inc(sem("rot_first"), 1)
                    pool.tensor_tensor(halves(qk)[:, :, 1, :], halves(z_sin)[:, :, 0, :], halves(z_cos)[:, :, 1, :],
                                       ALU.add).then_inc(sem("qk_ready"), 1)
                    pool.wait_ge(sem("rot_first"), t.after)
                    pool.wait_ge(sem("qk_ready"), t.after)
                    pool.tensor_tensor(heads(k_dec[:], HB), heads(qk[:, DB:D], HB), per_head(cst("k_decay"), HB), ALU.mult
                                       ).then_inc(sem("k_dec_ready"), 1)
                    pool.wait_ge(sem("head_b_rstd_in"), t.after)
                    pool.tensor_tensor(stat[:, 6, 0:HB], stat[:, 5, 0:HB], half[:, 0:HB], ALU.pow).then_inc(sem("head_b_rstd"), 1)
                run(pool, body)
                head_a_rstd(NT)
                h2_rstd(NT)

            @block.scalar
            def _(act):
                act.wait_ge(sem("consts_loaded"), 16)

                def mixed_t0(n):
                    act.wait_ge(sem("mixed_turned0"), n)
                    act.activation(mixed_t[:, 0:4, :], ps[:, 3, :], ACT.Copy).then_inc(sem("mixed_t0_ready"), 1)

                def mean_square(n):
                    act.wait_ge(sem("h2_ready"), n)
                    act.activation(z0[:].rearrange("p a c -> p (a c)"), h2[:], ACT.Square,
                                   scale=D ** -0.5, accum_out=stat[:, 7, 2:3]).then_inc(sem("h2_mean_square"), 1)

                def u2_t0(n):
                    act.wait_ge(sem("u2_turned0"), n)
                    act.activation(u2_t[:, 0:4, :], ps[:, 6, :], ACT.Copy).then_inc(sem("u2_t0_ready"), 1)

                def body(t):
                    act.wait_ge(sem("lora_turned"), t.after)
                    act.activation(lora_t[0:C, :], ps[0:C, 4, 0:P], ACT.Tanh).then_inc(sem("lora_tanh"), 1)
                    act.activation(lora_t[C:P, :], ps[C:P, 4, 0:P], ACT.Copy).then_inc(sem("lora_t_ready"), 1)
                    act.activation(gate_t[:], ps[:, 4, P:2 * P], ACT.Tanh, scale=0.5).then_inc(sem("gate_tanh"), 1)
                    act.wait_ge(sem("decay_in"), t.after)
                    act.activation(log_w[:], log_w[:], ACT.Tanh, scale=0.5).then_inc(sem("decay_tanh"), 1)
                    act.wait_ge(sem("iclr_in"), t.after)
                    act.activation(iclr[:], iclr[:], ACT.Tanh, scale=0.5).then_inc(sem("iclr_tanh"), 1)
                    if t.has_before:
                        mixed_t0(t.i)
                    act.wait_ge(sem("cum_in_done"), t.after)
                    act.activation(e_in[:], ps[:, 0, :], ACT.Exp).then_inc(sem("e_in_ready"), 1)
                    act.activation(e_neg[:], ps[:, 0, :], ACT.Exp, scale=-1.0).then_inc(sem("e_neg_ready"), 1)
                    act.wait_ge(sem("cum_ex_done"), t.after)
                    act.activation(e_ex[:], ps[:, 1, :], ACT.Exp).then_inc(sem("e_ex_ready"), 1)
                    act.wait_ge(sem("chunk_sum_done"), t.after)
                    act.activation(decay_c[:], ps[:, 2, 0:HA], ACT.Exp).then_inc(sem("decay_c_ready"), 1)
                    act.wait_ge(sem("after_done"), t.after)
                    act.activation(e_after[:], ps[:, 5, :], ACT.Exp).then_inc(sem("e_after_ready"), 1)
                    act.wait_ge(sem("gate_up_done"), t.after)
                    if t.has_before:
                        act.wait_ge(sem("mixed_a_ready"), t.i)
                    act.activation(gate[:], ps[:, 4, :], ACT.Copy).then_inc(sem("gate_ready"), 1)
                    act.wait_ge(sem("b_turned"), t.after)
                    act.activation(b_t[:], ps[:, 1, :], ACT.Copy).then_inc(sem("b_t_ready"), 1)
                    act.wait_ge(sem("k_turned"), t.after)
                    act.activation(k_t[:], ps[:, 2, :], ACT.Copy).then_inc(sem("k_t_ready"), 1)
                    if t.has_before:
                        mean_square(t.i)
                        u2_t0(t.i)
                    act.wait_ge(sem("l2_t_done"), t.after)
                    act.activation(l2_t[:], ps[:, 5, :], ACT.Copy).then_inc(sem("l2_t_ready"), 1)
                    act.wait_ge(sem("l4_done"), t.after)
                    act.wait_ge(sem("b_h_ready"), t.after)
                    act.activation(l4[:], ps[:, 0, :], ACT.Copy).then_inc(sem("l4_ready"), 1)
                    act.wait_ge(sem("l4_t_done"), t.after)
                    act.activation(l4_t[:], ps[:, 1, :], ACT.Copy).then_inc(sem("l4_t_ready"), 1)
                    act.wait_ge(sem("q_m_done"), t.after)
                    act.activation(q_m[:], ps[:, 5, :], ACT.Copy).then_inc(sem("q_m_ready"), 1)
                    act.wait_ge(sem("l8_done"), t.after)
                    act.activation(l8[:], ps[:, 3, :], ACT.Copy).then_inc(sem("l8_ready"), 1)
                    act.wait_ge(sem("z_ret_loaded"), t.after * 16)
                    act.activation(ret_gate[:], z_ret[:, 3 * DB:4 * DB], ACT.Tanh, scale=0.5).then_inc(sem("ret_tanh"), 1)
                    act.wait_ge(sem("q_turned"), t.after)
                    act.activation(q_t[:], ps[:, 6, :], ACT.Copy).then_inc(sem("q_t_ready"), 1)
                    act.wait_ge(sem("kr_turned"), t.after)
                    act.activation(kr_t[:], ps[:, 7, :], ACT.Copy).then_inc(sem("kr_t_ready"), 1)
                    act.wait_ge(sem("x_t_done"), t.after)
                    act.activation(x_t[:], ps[:, 0, :], ACT.Copy).then_inc(sem("x_t_ready"), 1)
                    act.wait_ge(sem("z0_a_done"), t.after)
                    act.activation(z0[:, 0, :], ps[:, 4, :], ACT.Copy).then_inc(sem("z0_a_ready"), 1)
                    act.wait_ge(sem("x2_t_done"), t.after)
                    act.activation(x2_t[:], ps[:, 2, :], ACT.Copy).then_inc(sem("x2_t_ready"), 1)
                    act.wait_ge(sem("inner_done"), t.after)
                    act.activation(in_s[:], ps[:, 6, :], ACT.Copy).then_inc(sem("in_s_ready"), 1)
                    act.wait_ge(sem("n_m_done"), t.after)
                    act.activation(n_m[:], ps[:, 0:2, 0:256], ACT.Copy).then_inc(sem("n_m_ready"), 1)
                    act.wait_ge(sem("mixed_turned1"), t.after)
                    act.activation(mixed_t[:, 4:8, :], ps[:, 7, :], ACT.Copy).then_inc(sem("mixed_t1_ready"), 1)
                    act.wait_ge(sem("y0_done"), t.after)
                    act.activation(y[:], ps[:, 0, :], ACT.Copy).then_inc(sem("y0_ready"), 1)
                run(act, body)
                mixed_t0(NT)
                mean_square(NT)
                u2_t0(NT)

            @block.vector
            def _(dve):
                dve.memset(h_in[:], 0.0).then_inc(sem("h_res_zeroed"), 1)
                dve.wait_ge(sem("mix_params"), 16 * 17)
                dve.wait_ge(sem("states_zeroed"), 2)

                OWN, OWN_END = 28, 8

                def centre(y_, n, tmp_, mean, var, done):
                    w = DA // n
                    done(dve.tensor_reduce(mean, heads(y_[:], n), X, ALU.add))
                    done(dve.tensor_scalar(mean, mean, 1.0 / w, None, ALU.mult, ALU.bypass))
                    done(dve.tensor_tensor(heads(y_[:], n), heads(y_[:], n), per_head(mean, n), ALU.subtract))
                    done(dve.tensor_tensor(tmp_[:], y_[:], y_[:], ALU.mult))
                    done(dve.tensor_reduce(var, heads(tmp_[:], n), X, ALU.add))

                def end_steps(n):
                    n_own = [0]

                    def own(ins):
                        n_own[0] += 1
                        ins.then_inc(sem("dve_end"), 1)
                        dve.wait_ge(sem("dve_end"), (n - 1) * OWN_END + n_own[0])

                    def centre_a():
                        dve.wait_ge(sem("y1_done"), n)
                        dve.wait_ge(sem("y0_ready"), n)
                        own(dve.tensor_tensor(parity(y[:]), parity(y[:]), bank_pair(2), ALU.add))
                        dve.wait_ge(sem("s2_done"), n)
                        dve.tensor_tensor(state[0][:], n_m[:, 1, :], ps[:, 5, 0:256], ALU.add).then_inc(sem("state0_ready"), 1)
                        centre(y, HA, tmp, stat[:, 2, :], stat[:, 3, :], own)
                        dve.tensor_scalar(stat[:, 3, :], stat[:, 3, :], 1.0 / HEAD_A, 64e-5, ALU.mult, ALU.add
                                          ).then_inc(sem("head_a_rstd_in"), 1)

                    def gate_a():
                        dve.wait_ge(sem("head_a_rstd"), n)
                        own(dve.tensor_tensor(heads(y[:]), heads(y[:]), per_head(stat[:, 4, :]), ALU.mult))
                        own(dve.tensor_tensor(y[:], y[:], gate[:], ALU.mult))
                        dve.tensor_tensor(y[:], y[:], bonus[:], ALU.add).then_inc(sem("mixed_a_ready"), 1)

                    def residual():
                        dve.wait_ge(sem("h_res_loaded"), n * 16)
                        dve.wait_ge(sem("proj_done"), n)
                        dve.tensor_tensor(h2[:], h_in[:], ps[:, 6:8, :].rearrange("p a c -> p (a c)"), ALU.add).then_inc(sem("h2_ready"), 1)

                    def mean_eps():
                        dve.wait_ge(sem("h2_mean_square"), n)
                        dve.tensor_scalar(stat[:, 7, 0:1], stat[:, 7, 2:3], 1e-6, None, ALU.add, ALU.bypass).then_inc(sem("h2_rstd_in"), 1)

                    def norm():
                        dve.wait_ge(sem("h2_ready"), n)
                        dve.wait_ge(sem("h2_rstd"), n)
                        dve.scalar_tensor_tensor(u2[:], h2[:], stat[:, 7, 1:2], gain[:], ALU.mult, ALU.mult).then_inc(sem("u2_ready"), 1)

                    def u2_t1():
                        dve.wait_ge(sem("u2_turned1"), n)
                        dve.tensor_copy(u2_t[:, 4:8, :], ps[:, 7, :]).then_inc(sem("u2_t1_ready"), 1)

                    def logits_of():
                        dve.wait_ge(sem("router_done"), n)
                        dve.tensor_tensor(logits[:, bass.ds(n - 1, 1), :].rearrange("p a c -> p (a c)"), ps[:, 6, 0:NR],
                                          router_b[:], ALU.add).then_inc(sem("logits_ready"), 1)
                        assert n_own[0] == OWN_END, n_own[0]
                    return centre_a, gate_a, residual, mean_eps, norm, u2_t1, logits_of

                def body(t):
                    n_own = [0]

                    def own(ins):
                        n_own[0] += 1
                        ins.then_inc(sem("dve_own"), 1)
                        dve.wait_ge(sem("dve_own"), t.i * OWN + n_own[0])

                    if t.has_before:
                        centre_a, gate_a, residual, mean_eps, norm, u2_t1, logits_of = end_steps(t.i)
                    dve.wait_ge(sem("shift_scaled"), t.after)
                    if t.has_before:
                        dve.wait_ge(sem("y0_done"), t.i)
                    dve.tensor_tensor(zs[:, 3 * DA:PA], z_prev[:, 3 * DA:PA], z_cur[:, 3 * DA:PA], ALU.add).then_inc(sem("zs_lora_ready"), 1)
                    dve.tensor_tensor(k, z_prev[:, DA:2 * DA], z_cur[:, DA:2 * DA], ALU.add).then_inc(sem("zs_k_ready"), 1)
                    if t.has_before:
                        centre_a()
                    dve.wait_ge(sem("gate_tanh"), t.after)
                    dve.tensor_scalar(gate_t[:], gate_t[:], 0.5, 0.5, ALU.mult, ALU.add).then_inc(sem("gate_t_ready"), 1)
                    dve.wait_ge(sem("decay_up_done"), t.after)
                    dve.tensor_tensor(log_w[:], ps[:, 0, :], rows["decay_w0"][:], ALU.add).then_inc(sem("decay_in"), 1)
                    dve.wait_ge(sem("iclr_up_done"), t.after)
                    dve.tensor_tensor(iclr[:], ps[:, 1, :], rows["iclr_a0"][:], ALU.add).then_inc(sem("iclr_in"), 1)
                    if t.has_before:
                        gate_a()
                    dve.wait_ge(sem("zs_k_ready"), t.after)
                    own(dve.tensor_tensor(kk[:], k, rows["k_k"][:], ALU.mult))
                    dve.wait_ge(sem("decay_tanh"), t.after)
                    dve.tensor_scalar(log_w[:], log_w[:], -0.5 * DECAY, -0.5 * DECAY, ALU.mult, ALU.add).then_inc(sem("log_w_ready"), 1)
                    own(dve.tensor_tensor(tmp[:], kk[:], kk[:], ALU.mult))
                    own(dve.tensor_reduce(stat[:, 0, :], heads(tmp[:]), X, ALU.add))
                    dve.tensor_scalar(stat[:, 0, :], stat[:, 0, :], 1e-24, None, ALU.max, ALU.bypass).then_inc(sem("kk_rnorm_in"), 1)
                    dve.wait_ge(sem("iclr_tanh"), t.after)
                    own(dve.tensor_scalar(iclr[:], iclr[:], 0.5, 0.5, ALU.mult, ALU.add))
                    own(dve.scalar_tensor_tensor(k2[:], iclr[:], -1.0, rows["k_a"][:], ALU.add, ALU.mult))
                    own(dve.scalar_tensor_tensor(k2[:], k2[:], 1.0, k, ALU.add, ALU.mult))
                    dve.wait_ge(sem("kk_rnorm"), t.after)
                    own(dve.tensor_tensor(heads(kk[:]), heads(kk[:]), per_head(stat[:, 1, :]), ALU.mult))
                    dve.wait_ge(sem("e_ex_ready"), t.after)
                    dve.scalar_tensor_tensor(a_d[:], kk[:], -1.0, e_ex[:], ALU.mult, ALU.mult).then_inc(sem("a_d_ready"), 1)
                    own(dve.tensor_tensor(b_row[:], kk[:], iclr[:], ALU.mult))
                    dve.wait_ge(sem("e_neg_ready"), t.after)
                    dve.tensor_tensor(b_d[:], b_row[:], e_neg[:], ALU.mult).then_inc(sem("b_d_ready"), 1)
                    dve.tensor_tensor(k_d[:], k2[:], e_neg[:], ALU.mult).then_inc(sem("k_d_ready"), 1)
                    dve.wait_ge(sem("e_in_ready"), t.after)
                    dve.wait_ge(sem("zs_r_ready"), t.after)
                    dve.tensor_tensor(r_d[:], r, e_in[:], ALU.mult).then_inc(sem("r_d_ready"), 1)
                    dve.wait_ge(sem("a_turned"), t.after)
                    dve.tensor_copy(a_t[:], ps[:, 0, :]).then_inc(sem("a_t_ready"), 1)
                    dve.wait_ge(sem("r_turned"), t.after)
                    dve.tensor_copy(r_t[:], ps[:, 3, :]).then_inc(sem("r_t_ready"), 1)
                    if t.has_before:
                        residual()
                        mean_eps()
                    dve.wait_ge(sem("g_ab_done"), t.after)
                    dve.tensor_tensor(parity(ld_t[:]), bank_pair(4), all_pairs(cst("lt_sub")), ALU.mult).then_inc(sem("ld_t_ready"), 1)
                    dve.tensor_tensor(parity(ld[:]), bank_pair(4, 256), all_pairs(cst("gt_sub")), ALU.mult).then_inc(sem("ld_ready"), 1)
                    dve.tensor_tensor(parity(lo[:]), bank_pair(4, 256), all_pairs(cst("gt_off")), ALU.mult).then_inc(sem("lo_ready"), 1)
                    if t.has_before:
                        norm()
                    dve.wait_ge(sem("g_ak_done"), t.after)
                    own(dve.tensor_tensor(parity(ak_t[:]), bank_pair(0), all_pairs(cst("lt")), ALU.mult))
                    dve.tensor_tensor(parity(rb_t[:]), bank_pair(0, 256), all_pairs(cst("le")), ALU.mult).then_inc(sem("rb_t_ready"), 1)
                    dve.wait_ge(sem("g_rk_done"), t.after)
                    dve.tensor_tensor(parity(rk_t[:]), bank_pair(2), all_pairs(cst("le")), ALU.mult).then_inc(sem("rk_t_ready"), 1)
                    if t.has_before:
                        u2_t1()
                    dve.wait_ge(sem("e_after_ready"), t.after)
                    if t.has_before:
                        dve.wait_ge(sem("u2_ready"), t.i)
                        dve.wait_ge(sem("h2_stored"), t.i * 16)
                    dve.tensor_tensor(k_h[:], k2[:], e_after[:], ALU.mult).then_inc(sem("k_h_ready"), 1)
                    dve.tensor_tensor(b_h[:], b_row[:], e_after[:], ALU.mult).then_inc(sem("b_h_ready"), 1)
                    dve.wait_ge(sem("l2_done"), t.after)
                    dve.tensor_copy(l2[:], ps[:, 4, :]).then_inc(sem("l2_ready"), 1)
                    dve.wait_ge(sem("ld_t_ready"), t.after)
                    own(dve.tensor_tensor(heads(inv[:]), heads(ld_t[:]), all_heads(cst("ident_c")), ALU.add))
                    dve.wait_ge(sem("l2_t_ready"), t.after)
                    own(dve.tensor_tensor(inv[:], inv[:], l2_t[:], ALU.add))
                    if t.has_before:
                        logits_of()
                    dve.wait_ge(sem("l3_t_done"), t.after)
                    dve.tensor_tensor(inv[:], inv[:], ps[:, 2, :], ALU.add).then_inc(sem("inv_3"), 1)
                    dve.wait_ge(sem("zs_ready"), t.after)
                    own(dve.tensor_tensor(tmp[:], r, k2[:], ALU.mult))
                    own(dve.tensor_tensor(tmp[:], tmp[:], rows["r_k"][:], ALU.mult))
                    own(dve.tensor_reduce(stat[:, 8, :], heads(tmp[:]), X, ALU.add))
                    own(dve.tensor_tensor(heads(bonus[:]), heads(v), per_head(stat[:, 8, :]), ALU.mult))
                    dve.wait_ge(sem("inv_3"), t.after)
                    dve.wait_ge(sem("inv4_done"), t.after)
                    dve.tensor_tensor(inv[:], inv[:], ps[:, 4, :], ALU.add).then_inc(sem("inv_4"), 1)
                    own(dve.tensor_tensor(bonus[:], bonus[:], rows["ln_b_a"][:], ALU.add))
                    dve.wait_ge(sem("gate_ready"), t.after)
                    dve.tensor_tensor(bonus[:], bonus[:], gate[:], ALU.mult).then_inc(sem("bonus_ready"), 1)
                    dve.wait_ge(sem("inv_4"), t.after)
                    dve.wait_ge(sem("inv8_done"), t.after)
                    dve.tensor_tensor(inv[:], inv[:], ps[:, 5, :], ALU.add).then_inc(sem("inv_ready"), 1)
                    dve.wait_ge(sem("bonus_ready"), t.after)
                    own(dve.tensor_tensor(gate[:], gate[:], rows["ln_w_a"][:], ALU.mult))
                    own(dve.tensor_tensor(heads(memory_d[:], HB), heads(memory[0][:], HB), per_head(cst("r_decay"), HB), ALU.mult))
                    dve.wait_ge(sem("scores_done"), t.after)
                    dve.tensor_tensor(s_t[:], ps[:, 6, 0:HB * C], cst("ret_mask"), ALU.mult).then_inc(sem("s_t_ready"), 1)
                    dve.wait_ge(sem("kv0_done"), t.after)
                    dve.tensor_tensor(memory[1][:], memory_d[:], ps[:, 7, :], ALU.add).then_inc(sem("memory1_ready"), 1)
                    dve.wait_ge(sem("x_m_done"), t.after)
                    dve.tensor_copy(x_m[:], ps[:, 1, :]).then_inc(sem("x_m_ready"), 1)
                    dve.wait_ge(sem("z0_q_done"), t.after)
                    dve.tensor_copy(z0[:, 1, :], ps[:, 5, :]).then_inc(sem("z0_q_ready"), 1)
                    dve.wait_ge(sem("memory1_ready"), t.after)
                    own(dve.tensor_tensor(heads(memory_d[:], HB), heads(memory[1][:], HB), per_head(cst("r_decay"), HB), ALU.mult))
                    dve.wait_ge(sem("cross_done"), t.after)
                    own(dve.tensor_tensor(heads(ret_tmp[:], HB), heads(ps[:, 7, :], HB), per_head(cst("q_decay"), HB), ALU.mult))
                    dve.wait_ge(sem("in_s_ready"), t.after)
                    dve.tensor_tensor(y_ret[:], ret_tmp[:], in_s[:], ALU.add).then_inc(sem("y_ret_ready"), 1)
                    dve.wait_ge(sem("z0_q_ready"), t.after)
                    dve.wait_ge(sem("z1_done"), t.after)
                    dve.wait_ge(sem("z0_a_ready"), t.after)
                    dve.tensor_tensor(z1[:], z0[:], ps[:, 0:2, :], ALU.add).then_inc(sem("z1_ready"), 1)
                    dve.wait_ge(sem("kv1_done"), t.after)
                    dve.tensor_tensor(memory[0][:], memory_d[:], ps[:, 6, :], ALU.add).then_inc(sem("memory0_ready"), 1)
                    dve.wait_ge(sem("y_ret_ready"), t.after)
                    centre(y_ret, HB, ret_tmp, stat[:, 9, 0:HB], stat[:, 5, 0:HB], own)
                    dve.tensor_scalar(stat[:, 5, 0:HB], stat[:, 5, 0:HB], 1.0 / HEAD_B, 1e-5, ALU.mult, ALU.add
                                      ).then_inc(sem("head_b_rstd_in"), 1)
                    dve.wait_ge(sem("z1_ready"), t.after)
                    dve.wait_ge(sem("w_done"), t.after)
                    dve.tensor_tensor(w_m[:], z1[:], ps[:, 2:4, :], ALU.add).then_inc(sem("w_m_ready"), 1)
                    dve.wait_ge(sem("head_b_rstd"), t.after)
                    own(dve.tensor_tensor(heads(y_ret[:], HB), heads(y_ret[:], HB), per_head(stat[:, 6, 0:HB], HB), ALU.mult))
                    own(dve.tensor_tensor(y_ret[:], y_ret[:], rows["gn_w_b"][:], ALU.mult))
                    dve.wait_ge(sem("m_t_done"), t.after)
                    dve.wait_ge(sem("diag_c_ready"), t.after)
                    dve.tensor_tensor(m_t[:, :, 0:256], diag_c, ps[:, 4:6, 0:256], ALU.add).then_inc(sem("m_t_ready"), 1)
                    dve.wait_ge(sem("ret_tanh"), t.after)
                    own(dve.scalar_tensor_tensor(ret_gate[:], ret_gate[:], 1.0, z_ret[:, 3 * DB:4 * DB], ALU.add, ALU.mult))
                    dve.scalar_tensor_tensor(y_ret[:], ret_gate[:], 0.5, y_ret[:], ALU.mult, ALU.mult).then_inc(sem("mixed_b_ready"), 1)
                    dve.wait_ge(sem("rz_done"), t.after)
                    dve.tensor_tensor(rz_t[:].rearrange("p (q c k) -> p c q k", c=2, k=C), r_t[:].rearrange("p (q c k) -> p c q k", c=2, k=C), ps[:, 2:4, 0:256].rearrange("p c (q k) -> p c q k", k=C), ALU.add).then_inc(sem("rz_t_ready"), 1)
                    dve.wait_ge(sem("s1_done"), t.after)
                    dve.wait_ge(sem("n_m_ready"), t.after)
                    dve.tensor_tensor(state[1][:], n_m[:, 0, :], ps[:, 4, 0:256], ALU.add).then_inc(sem("state1_ready"), 1)
                    assert n_own[0] == OWN, n_own[0]
                run(dve, body)
                for step in end_steps(NT):
                    step()

            @block.tensor
            def _(pe):
                pe.wait_ge(sem("mix_params"), 16 * 17)

                def turn4(bank, src):
                    for j in range(4):
                        tr = pe.transpose(ps[:, bank, j * P:(j + 1) * P], src[:, j * P:(j + 1) * P], ident)
                    return tr

                def full(bank, lhs, rhs):
                    return pe.matmul(ps[:, bank, :], lhs, rhs, start=True, stop=True)

                def chunks(bank, pairs):
                    for h in range(HA):
                        for c in range(2):
                            p_ = slice(c * C, (c + 1) * C)
                            f = slice(h * C, (h + 1) * C)
                            for n, (lhs, rhs) in enumerate(pairs):
                                mm = pe.matmul(ps[p_, bank, f], lhs[p_, f], rhs[p_, f],
                                               start=(n == 0), stop=(n == len(pairs) - 1))
                    return mm

                def cross(banks, at_, lhs, rhs):
                    for a in range(2):
                        for q in range(4):
                            for c in range(2):
                                f = slice(q * P + c * C, q * P + (c + 1) * C)
                                mm = pe.matmul(ps[c * C:(c + 1) * C, banks + a, at_ + q * C:at_ + (q + 1) * C],
                                               lhs[a * C:(a + 1) * C, f], rhs[a * C:(a + 1) * C, f], start=True, stop=True)
                    return mm

                def to_features(banks, pairs):
                    for c in range(2):
                        p_ = slice(c * C, (c + 1) * C)
                        for h in range(HA):
                            a, q = h % 2, h // 2
                            f = slice(h * C, (h + 1) * C)
                            for n, (lhs, rhs) in enumerate(pairs):
                                mm = pe.matmul(ps[a * C:(a + 1) * C, banks + c, q * C:(q + 1) * C], lhs[p_, f], rhs[p_, f],
                                               start=(n == 0), stop=(n == len(pairs) - 1))
                    return mm

                def advance(bank, m, st):
                    for a in range(2):
                        p_ = slice(a * C, (a + 1) * C)
                        for q in range(4):
                            f = slice(q * C, (q + 1) * C)
                            mm = pe.matmul(ps[p_, bank, f], m[p_, f], st[p_, f], start=True, stop=True)
                    return mm

                def project_out(n, ks, first):
                    for k_ in ks:
                        mm = pe.matmul(ps[:, 6 + n, :], mixed_t[:, k_, :], w_out[:, k_, n * 512:(n + 1) * 512],
                                       start=(first and k_ == ks[0]), stop=(not first and k_ == ks[-1]))
                    return mm

                def end_steps(n, lead):
                    def retention_rows(cols):
                        lead()
                        pe.wait_ge(sem("mixed_t1_ready"), n)
                        pe.wait_ge(sem("memory0_ready"), n)
                        project_out(cols, range(4, 8), True)

                    def turn_rwkv_rows():
                        lead()
                        pe.wait_ge(sem("mixed_a_ready"), n)
                        turn4(3, y).then_inc(sem("mixed_turned0"), 1)

                    def rwkv_rows():
                        lead()
                        pe.wait_ge(sem("mixed_t0_ready"), n)
                        project_out(0, range(4), False)
                        project_out(1, range(4), False).then_inc(sem("proj_done"), 1)

                    def turn_u2():
                        lead()
                        pe.wait_ge(sem("u2_ready"), n)
                        turn4(6, u2[:, 0:512]).then_inc(sem("u2_turned0"), 1)
                        turn4(7, u2[:, 512:D]).then_inc(sem("u2_turned1"), 1)

                    def route():
                        lead()
                        pe.wait_ge(sem("u2_t0_ready"), n)
                        pe.wait_ge(sem("u2_t1_ready"), n)
                        for k_ in range(KD):
                            mm = pe.matmul(ps[:, 6, 0:NR], u2_t[:, k_, :], router_w[:, k_, :], start=(k_ == 0), stop=(k_ == KD - 1))
                        mm.then_inc(sem("router_done"), 1)
                    return retention_rows, turn_rwkv_rows, rwkv_rows, turn_u2, route

                def body(t):
                    if t.has_before:
                        retention_rows, turn_rwkv_rows, rwkv_rows, turn_u2, route = end_steps(t.i, lambda: t.lead(pe))
                    t.lead(pe)
                    pe.wait_ge(sem("zs_lora_ready"), t.after)
                    pe.transpose(ps[:, 4, 0:P], zs[:, 3 * DA:3 * DA + P], ident)
                    pe.transpose(ps[:, 4, P:2 * P], zs[:, 3 * DA + P:3 * DA + 2 * P], ident).then_inc(sem("lora_turned"), 1)
                    t.lead(pe)
                    pe.wait_ge(sem("lora_tanh"), t.after)
                    pe.wait_ge(sem("lora_t_ready"), t.after)
                    if t.has_before:
                        pe.wait_ge(sem("y0_ready"), t.i)
                    full(0, lora_t[0:C, :], lora_up[0:C, :]).then_inc(sem("decay_up_done"), 1)
                    full(1, lora_t[C:P, :], lora_up[C:P, :]).then_inc(sem("iclr_up_done"), 1)
                    if t.has_before:
                        retention_rows(0)
                    t.lead(pe)
                    pe.wait_ge(sem("gate_t_ready"), t.after)
                    full(4, gate_t[:], gate_up[:]).then_inc(sem("gate_up_done"), 1)
                    if t.has_before:
                        turn_rwkv_rows()
                    t.lead(pe)
                    pe.wait_ge(sem("log_w_ready"), t.after)
                    pe.wait_ge(sem("iclr_in"), t.after)
                    full(0, cst("cum_in"), log_w[:]).then_inc(sem("cum_in_done"), 1)
                    full(1, cst("cum_ex"), log_w[:]).then_inc(sem("cum_ex_done"), 1)
                    for q in range(4):
                        mm = pe.matmul(ps[:, 2, 2 * q:2 * q + 2], log_w[:, q * P:(q + 1) * P], cst("chunk_of"),
                                       start=True, stop=True)
                    mm.then_inc(sem("chunk_sum_done"), 1)
                    full(5, cst("after"), log_w[:]).then_inc(sem("after_done"), 1)
                    if t.has_before:
                        retention_rows(1)
                        t.lead(pe)
                        pe.wait_ge(sem("mixed_t0_ready"), t.i)
                    t.lead(pe)
                    pe.wait_ge(sem("a_d_ready"), t.after)
                    pe.wait_ge(sem("e_neg_ready"), t.after)
                    turn4(0, a_d).then_inc(sem("a_turned"), 1)
                    t.lead(pe)
                    pe.wait_ge(sem("b_d_ready"), t.after)
                    pe.wait_ge(sem("e_ex_ready"), t.after)
                    turn4(1, b_d).then_inc(sem("b_turned"), 1)
                    t.lead(pe)
                    pe.wait_ge(sem("k_d_ready"), t.after)
                    pe.wait_ge(sem("decay_c_ready"), t.after)
                    turn4(2, k_d).then_inc(sem("k_turned"), 1)
                    t.lead(pe)
                    pe.wait_ge(sem("r_d_ready"), t.after)
                    turn4(3, r_d).then_inc(sem("r_turned"), 1)
                    if t.has_before:
                        rwkv_rows()
                    t.lead(pe)
                    pe.wait_ge(sem("b_t_ready"), t.after)
                    pe.wait_ge(sem("a_t_ready"), t.after)
                    pe.wait_ge(sem("gate_ready"), t.after)
                    pe.wait_ge(sem("e_after_ready"), t.after)
                    cross(4, 0, b_t, a_t)
                    cross(4, 256, a_t, b_t).then_inc(sem("g_ab_done"), 1)
                    t.lead(pe)
                    pe.wait_ge(sem("k_t_ready"), t.after)
                    pe.wait_ge(sem("r_t_ready"), t.after)
                    cross(0, 0, k_t, a_t)
                    cross(0, 256, b_t, r_t).then_inc(sem("g_ak_done"), 1)
                    cross(2, 0, k_t, r_t).then_inc(sem("g_rk_done"), 1)
                    if t.has_before:
                        turn_u2()
                    t.lead(pe)
                    pe.wait_ge(sem("ld_t_ready"), t.after)
                    pe.wait_ge(sem("ld_ready"), t.after)
                    pe.wait_ge(sem("lo_ready"), t.after)
                    chunks(4, [(ld_t, ld)]).then_inc(sem("l2_done"), 1)
                    chunks(5, [(ld, ld_t)]).then_inc(sem("l2_t_done"), 1)
                    if t.has_before:
                        route()
                    t.lead(pe)
                    pe.wait_ge(sem("l2_ready"), t.after)
                    pe.wait_ge(sem("l2_t_ready"), t.after)
                    pe.wait_ge(sem("rb_t_ready"), t.after)
                    pe.wait_ge(sem("rk_t_ready"), t.after)
                    chunks(0, [(l2_t, l2)]).then_inc(sem("l4_done"), 1)
                    chunks(1, [(l2, l2_t)]).then_inc(sem("l4_t_done"), 1)
                    chunks(2, [(l2, ld_t)]).then_inc(sem("l3_t_done"), 1)
                    t.lead(pe)
                    pe.wait_ge(sem("zs_ready"), t.after)
                    chunks(5, [(ak_t, v)]).then_inc(sem("q_m_done"), 1)
                    t.lead(pe)
                    pe.wait_ge(sem("l4_ready"), t.after)
                    pe.wait_ge(sem("l4_t_ready"), t.after)
                    chunks(3, [(l4_t, l4)]).then_inc(sem("l8_done"), 1)
                    t.lead(pe)
                    pe.wait_ge(sem("inv_3"), t.after)
                    chunks(4, [(l4, inv)]).then_inc(sem("inv4_done"), 1)
                    if t.has_before:
                        t.lead(pe)
                        pe.wait_ge(sem("logits_ready"), t.i)
                    t.lead(pe)
                    pe.wait_ge(sem("qk_ready"), t.after)
                    turn4(6, qk[:, 0:DB]).then_inc(sem("q_turned"), 1)
                    turn4(7, qk[:, DB:D]).then_inc(sem("kr_turned"), 1)
                    t.lead(pe)
                    pe.wait_ge(sem("inv_4"), t.after)
                    pe.wait_ge(sem("l8_ready"), t.after)
                    pe.wait_ge(sem("q_m_ready"), t.after)
                    chunks(5, [(l8, inv)]).then_inc(sem("inv8_done"), 1)
                    t.lead(pe)
                    pe.wait_ge(sem("q_t_ready"), t.after)
                    pe.wait_ge(sem("kr_t_ready"), t.after)
                    pe.wait_ge(sem("k_dec_ready"), t.after)

                    def key_values(bank, c):
                        p_ = slice(c * C, (c + 1) * C)
                        for h in range(HB):
                            mm = pe.matmul(ps[:, bank, h * P:(h + 1) * P], k_dec[p_, h * P:(h + 1) * P],
                                           z_ret[p_, 2 * DB + h * P:2 * DB + (h + 1) * P], start=True, stop=True)
                        return mm
                    for c in range(2):
                        for h in range(HB):
                            f = slice(h * P + c * C, h * P + (c + 1) * C)
                            mm = pe.matmul(ps[c * C:(c + 1) * C, 6, h * C:(h + 1) * C], kr_t[:, f], q_t[:, f], start=True, stop=True)
                    mm.then_inc(sem("scores_done"), 1)
                    key_values(7, 0).then_inc(sem("kv0_done"), 1)
                    t.lead(pe)
                    pe.wait_ge(sem("inv_ready"), t.after)
                    chunks(0, [(lo, inv)]).then_inc(sem("x_t_done"), 1)
                    chunks(1, [(inv, lo)]).then_inc(sem("x_m_done"), 1)
                    chunks(4, [(inv, a_d)]).then_inc(sem("z0_a_done"), 1)
                    chunks(5, [(inv, q_m)]).then_inc(sem("z0_q_done"), 1)
                    t.lead(pe)
                    pe.wait_ge(sem("x_m_ready"), t.after)
                    pe.wait_ge(sem("x_t_ready"), t.after)
                    chunks(2, [(x_m, x_t)]).then_inc(sem("x2_t_done"), 1)
                    t.lead(pe)
                    pe.wait_ge(sem("s_t_ready"), t.after)
                    for c in range(2):
                        p_ = slice(c * C, (c + 1) * C)
                        for h in range(HB):
                            mm = pe.matmul(ps[p_, 6, h * P:(h + 1) * P], s_t[p_, h * C:(h + 1) * C],
                                           z_ret[p_, 2 * DB + h * P:2 * DB + (h + 1) * P], start=True, stop=True)
                    mm.then_inc(sem("inner_done"), 1)
                    t.lead(pe)
                    pe.wait_ge(sem("memory1_ready"), t.after)
                    for c in range(2):
                        for h in range(HB):
                            mm = pe.matmul(ps[c * C:(c + 1) * C, 7, h * P:(h + 1) * P], q_t[:, h * P + c * C:h * P + (c + 1) * C],
                                           memory[c][:, h * P:(h + 1) * P], start=True, stop=True)
                    mm.then_inc(sem("cross_done"), 1)
                    t.lead(pe)
                    pe.wait_ge(sem("x2_t_ready"), t.after)
                    pe.wait_ge(sem("z0_a_ready"), t.after)
                    pe.wait_ge(sem("z0_q_ready"), t.after)
                    chunks(0, [(x2_t, z0[:, 0, :])])
                    chunks(1, [(x2_t, z0[:, 1, :])]).then_inc(sem("z1_done"), 1)
                    t.lead(pe)
                    pe.wait_ge(sem("in_s_ready"), t.after)
                    key_values(6, 1).then_inc(sem("kv1_done"), 1)
                    t.lead(pe)
                    pe.wait_ge(sem("z1_ready"), t.after)
                    chunks(2, [(x_t, z1[:, 0, :])])
                    chunks(3, [(x_t, z1[:, 1, :])]).then_inc(sem("w_done"), 1)
                    t.lead(pe)
                    pe.wait_ge(sem("w_m_ready"), t.after)
                    pe.wait_ge(sem("k_h_ready"), t.after)
                    pe.wait_ge(sem("b_h_ready"), t.after)
                    wa, wq = w_m[:, 0, :], w_m[:, 1, :]
                    to_features(4, [(wa, b_h)]).then_inc(sem("m_t_done"), 1)
                    to_features(0, [(b_h, wq), (k_h, v)]).then_inc(sem("n_m_done"), 1)
                    to_features(2, [(wa, rb_t)]).then_inc(sem("rz_done"), 1)
                    t.lead(pe)
                    pe.wait_ge(sem("m_t_ready"), t.after)
                    if t.has_before:
                        pe.wait_ge(sem("state0_ready"), t.i)
                    advance(4, m_t[:, 0, :], state[0]).then_inc(sem("s1_done"), 1)
                    t.lead(pe)
                    pe.wait_ge(sem("mixed_b_ready"), t.after)
                    pe.wait_ge(sem("n_m_ready"), t.after)
                    turn4(7, y_ret).then_inc(sem("mixed_turned1"), 1)
                    chunks(0, [(rb_t, wq), (rk_t, v)]).then_inc(sem("y0_done"), 1)
                    t.lead(pe)
                    pe.wait_ge(sem("state1_ready"), t.after)
                    pe.wait_ge(sem("rz_t_ready"), t.after)
                    advance(5, m_t[:, 1, :], state[1]).then_inc(sem("s2_done"), 1)
                    for a in range(2):
                        p_ = slice(a * C, (a + 1) * C)
                        for q in range(4):
                            for c in range(2):
                                mm = pe.matmul(ps[c * C:(c + 1) * C, 2 + a, q * C:(q + 1) * C],
                                               rz_t[p_, q * P + c * C:q * P + (c + 1) * C],
                                               state[c][p_, q * C:(q + 1) * C], start=True, stop=True)
                    mm.then_inc(sem("y1_done"), 1)
                run(pe, body)
                retention_rows, turn_rwkv_rows, rwkv_rows, turn_u2, route = end_steps(NT, lambda: None)
                retention_rows(0)
                retention_rows(1)
                turn_rwkv_rows()
                rwkv_rows()
                turn_u2()
                route()


def dispatch_and_experts(nc, d, out, env):
    sem, tile, ps, ident, cst = (env[k] for k in ("sem", "tile", "ps", "ident", "cst"))
    h2_dram, u2_dram, y_dram, slot_row_dram, half, logits, free_sems = (
        env[k] for k in ("h2_dram", "u2_dram", "y_dram", "slot_row_dram", "half", "logits", "free_sems"))
    NTR = NT - 1
    BIG = 1e30
    with ExitStack() as outer:
        slots = tile(outer, "slots", [P, 2, NTR], I32)
        weight = tile(outer, "weight", [P, 2, NTR])
        slot_row = tile(outer, "slot_row", [P, NBLK], I32)
        extra = tile(outer, "extra", [1, 1 + EXTRA], I32)

        with ExitStack() as s:
            def sb(name, *shape, dt=F32):
                return tile(s, name, [P, *shape], dt)

            g_max, g_pick, g_hot, g_exp = sb("g_max", NTR), sb("g_pick", NTR, N_GROUPS), sb("g_hot", NTR, N_GROUPS), sb("g_exp", NTR, N_GROUPS)
            g_prob, e_max, e_gap, e_ratio = sb("g_prob", NTR), sb("e_max", 2, NTR), sb("e_gap", NTR), sb("e_ratio", NTR)
            e_log, e_pick = sb("e_log", 2, NTR, NE), sb("e_pick", NTR, NE)
            hot, load, rank = sb("hot", 2, NTR, NE), sb("load", NTR + 1, NE), sb("rank", NTR, NE)
            both = sb("both", NTR, NE)
            count, over, more, more_before, more_end, base_gap = (sb(n, NE) for n in (
                "count", "over_unused", "more", "more_before", "more_end", "base_gap"))
            cmp_t, cmp_e, cmp_b = sb("cmp_t", NE, 8), sb("cmp_e", NE, NE), sb("cmp_b", EXTRA, NE)
            blk = sb("blk", EXTRA)
            r_of, s_of, g_of = sb("r_of", NTR), sb("s_of", NTR), sb("g_of", NTR)
            slot_f = sb("slot_f", 2, NTR)
            row_id = sb("row_id", NTR, dt=I32)
            row_f = sb("row_f", NTR)
            blank = sb("blank", NBLK)
            by_block = tile(s, "by_block", [NBLK, P])

            gl = logits[:, 1:NT, 0:N_GROUPS]
            el = logits[:, 1:NT, N_GROUPS:NR]

            with nc.Block() as block:
                @block.vector
                def _(dve):
                    n = [0]

                    def step(ins, name=None):
                        if name:
                            ins.then_inc(sem(name), 1)
                            dve.wait_ge(sem(name), 1)
                        else:
                            n[0] += 1
                            ins.then_inc(sem("route_step"), 1)
                            dve.wait_ge(sem("route_step"), n[0])

                    def tt(dst, a, b, op, name=None):
                        step(dve.tensor_tensor(dst, a, b, op), name)

                    def red(dst, a, op, name=None):
                        step(dve.tensor_reduce(dst, a, X, op), name)

                    def over_last(ap, w):
                        return ap.unsqueeze(2).to_broadcast([P, NTR, w])

                    def first_of_max(dst, pick, top, values, prio, w):
                        red(top, values, ALU.max)
                        tt(pick, values, over_last(top, w), ALU.is_equal)
                        tt(pick, pick, prio.unsqueeze(1).to_broadcast([P, NTR, w]), ALU.mult)
                        red(s_of[:], pick, ALU.max)
                        tt(dst, pick, over_last(s_of[:], w), ALU.is_equal)

                    dve.memset(blank[:], 0.0).then_inc(sem("blank_ready"), 1)
                    dve.wait_ge(sem("blank_ready"), 1)
                    dve.wait_ge(sem("row_id_ready"), 1)
                    dve.tensor_copy(row_f[:], row_id[:]).then_inc(sem("row_f_ready"), 1)
                    dve.wait_ge(sem("row_f_ready"), 1)
                    first_of_max(g_hot[:], g_pick[:], g_max[:], gl, cst("group_prio"), N_GROUPS)
                    tt(g_exp[:], gl, over_last(g_max[:], N_GROUPS), ALU.subtract, "g_exp_in")
                    step(dve.tensor_scalar(g_pick[:], g_hot[:], BIG, -BIG, ALU.mult, ALU.add))
                    tt(e_log[:, 0].rearrange("p t (g e) -> p t g e", g=N_GROUPS), el.rearrange("p t (g e) -> p t g e", g=N_GROUPS),
                       g_pick[:].unsqueeze(3).to_broadcast([P, NTR, N_GROUPS, PER_GROUP]), ALU.add)
                    first_of_max(hot[:, 0], e_pick[:], e_max[:, 0], e_log[:, 0], cst("expert_prio"), NE)
                    step(dve.scalar_tensor_tensor(e_log[:, 1], hot[:, 0], -3.0 * BIG, e_log[:, 0], ALU.mult, ALU.add))
                    first_of_max(hot[:, 1], e_pick[:], e_max[:, 1], e_log[:, 1], cst("expert_prio"), NE)
                    tt(e_gap[:], e_max[:, 1], e_max[:, 0], ALU.subtract, "e_gap_ready")
                    dve.wait_ge(sem("g_exp_ready"), 1)
                    red(g_prob[:], g_exp[:], ALU.add)
                    dve.wait_ge(sem("e_ratio_ready"), 1)
                    step(dve.tensor_scalar(e_gap[:], e_ratio[:], 1.0, None, ALU.add, ALU.bypass))
                    tt(g_prob[:], g_prob[:], e_gap[:], ALU.mult)
                    step(dve.reciprocal(weight[:, 0], g_prob[:]))
                    tt(weight[:, 1], weight[:, 0], e_ratio[:], ALU.mult)
                    tt(both[:], hot[:, 0], hot[:, 1], ALU.add)
                    step(dve.memset(load[:, 0], 0.0))
                    for j in range(NTR):
                        tt(load[:, j + 1], load[:, j], both[:, j], ALU.add, "load_ready" if j == NTR - 1 else None)
                    dve.wait_ge(sem("rank_done"), 1)
                    step(dve.tensor_copy(rank[:].rearrange("p t e -> p (t e)"), ps[:, 0, 0:NTR * NE]))
                    step(dve.tensor_copy(count[:], ps[:, 1, 0:NE]))
                    tt(cmp_t[:], count[:].unsqueeze(2).to_broadcast([P, NE, 8]),
                       cst("thresholds").unsqueeze(1).to_broadcast([P, NE, 8]), ALU.is_gt)
                    red(more[:], cmp_t[:], ALU.add)
                    tt(cmp_e[:], cst("before_e").rearrange("p (a b) -> p a b", a=NE),
                       more[:].unsqueeze(1).to_broadcast([P, NE, NE]), ALU.mult)
                    red(more_before[:], cmp_e[:], ALU.add)
                    tt(more_end[:], more_before[:], more[:], ALU.add)
                    tt(cmp_b[:], more_end[:].unsqueeze(1).to_broadcast([P, EXTRA, NE]),
                       cst("block_no").unsqueeze(2).to_broadcast([P, EXTRA, NE]), ALU.is_le)
                    red(blk[:], cmp_b[:], ALU.add)
                    step(dve.tensor_scalar(blk[:], blk[:], float(NE - 1), None, ALU.min, ALU.bypass))
                    step(dve.tensor_copy(extra[0:1, 1:1 + EXTRA], blk[0:1, :]))
                    dve.tensor_copy(extra[0:1, 0:1], more_end[0:1, NE - 1:NE]).then_inc(sem("extra_ready"), 1)
                    dve.wait_ge(sem("extra_ready"), 1)
                    step(dve.tensor_scalar(base_gap[:], more_before[:], float(P), float((NE - 1) * P), ALU.mult, ALU.add))
                    tt(base_gap[:], base_gap[:], cst("slot_base"), ALU.subtract)
                    for j in range(2):
                        for dst, table in ((r_of, rank[:]), (s_of, cst("slot_base").unsqueeze(1).to_broadcast([P, NTR, NE])),
                                           (g_of, base_gap[:].unsqueeze(1).to_broadcast([P, NTR, NE]))):
                            tt(e_pick[:], hot[:, j], table, ALU.mult)
                            red(dst[:], e_pick[:], ALU.add)
                        tt(s_of[:], s_of[:], r_of[:], ALU.add)
                        step(dve.tensor_scalar(r_of[:], r_of[:], float(P), None, ALU.is_ge, ALU.bypass))
                        tt(g_of[:], g_of[:], r_of[:], ALU.mult)
                        tt(slot_f[:, j], s_of[:], g_of[:], ALU.add)
                    dve.tensor_copy(slots[:], slot_f[:]).then_inc(sem("slots_ready"), 1)
                    dve.wait_ge(sem("slots_ready"), 1)
                    dve.wait_ge(sem("slot_rows_turned"), 1)
                    dve.tensor_copy(slot_row[:], ps[:, 2, 0:NBLK]).then_inc(sem("slot_row_ready"), 1)
                    dve.wait_ge(sem("slot_row_ready"), 1)

                @block.scalar
                def _(act):
                    act.wait_ge(sem("g_exp_in"), 1)
                    act.activation(g_exp[:], g_exp[:], ACT.Exp).then_inc(sem("g_exp_ready"), 1)
                    act.wait_ge(sem("e_gap_ready"), 1)
                    act.activation(e_ratio[:], e_gap[:], ACT.Exp).then_inc(sem("e_ratio_ready"), 1)

                @block.tensor
                def _(pe):
                    pe.wait_ge(sem("load_ready"), 1)
                    flat = lambda ap: ap.rearrange("p t e -> p (t e)")
                    pe.matmul(ps[:, 0, 0:NTR * NE], cst("before"), flat(both[:]), start=True, stop=False)
                    pe.matmul(ps[:, 0, 0:NTR * NE], cst("ones"), flat(load[:, 0:NTR]), start=False, stop=True)
                    pe.matmul(ps[:, 1, 0:NE], cst("ones"), load[:, NTR], start=True, stop=True).then_inc(sem("rank_done"), 1)
                    pe.wait_ge(sem("by_block_loaded"), 16)
                    pe.transpose(ps[:, 2, 0:NBLK], by_block[:], ident[0:NBLK, 0:NBLK]).then_inc(sem("slot_rows_turned"), 1)

                @block.gpsimd
                def _(pool):
                    pool.iota(row_id[:], [[P, NTR]], base=P, channel_multiplier=1).then_inc(sem("row_id_ready"), 1)
                    pool.wait_ge(sem("blank_stored"), 16)
                    pool.wait_ge(sem("row_f_ready"), 1)
                    pool.wait_ge(sem("slots_ready"), 1)
                    for j in range(2):
                        for t in range(NTR):
                            pool.indirect_dma_start(slot_row_dram, bass.IndirectOffsetOnAxis(ap=slots[:, j, t:t + 1], axis=0),
                                                    row_f[:, t:t + 1], None).then_inc(sem("slot_rows_stored"), 16)

                @block.sync
                def _(sp):
                    sp.wait_ge(sem("blank_ready"), 1)
                    sp.dma_start(slot_row_dram.rearrange("(b p) o -> p (b o)", p=P), blank[:],
                                 allow_slow_non_contiguous=True).then_inc(sem("blank_stored"), 16)
                    sp.wait_ge(sem("slot_rows_stored"), 16 * 2 * NTR)
                    sp.dma_start(by_block[:], slot_row_dram.rearrange("(b p) o -> b (p o)", p=P)).then_inc(sem("by_block_loaded"), 16)
                    sp.wait_ge(sem("slot_row_ready"), 1)
        free_sems()

        with ExitStack() as s:
            def sb(name, *shape):
                return tile(s, name, [P, *shape])

            w_gate = [sb(f"w_gate{b}", KD, DE) for b in range(2)]
            w_up = [sb(f"w_up{b}", KD, DE) for b in range(2)]
            w_down = [sb(f"w_down{b}", KE, D) for b in range(2)]
            x_rows = [sb(f"x_rows{b}", D) for b in range(2)]
            x_t = [sb(f"x_t{b}", KD, P) for b in range(2)]
            act_t, hid, hid_t = sb("act_t", DE), sb("hid", DE), sb("hid_t", KE, P)
            y_out = [sb(f"y_out{b}", D) for b in range(2)]
            more_row = tile(s, "more_row", [P, 1], I32)
            y_in = [[sb(f"y_in{j}{b}", D) for b in range(2)] for j in range(2)]
            h_in = [sb(f"h_last{b}", D) for b in range(2)]
            gain = sb("norm_final_rows", D)
            rms = sb("rms", 3, 2)
            wg_v = d["moe_w_gate"].rearrange("e (k p) n -> e p k n", p=P)
            wu_v = d["moe_w_up"].rearrange("e (k p) n -> e p k n", p=P)
            wd_v = d["moe_w_down"].rearrange("e (k p) n -> e p k n", p=P)

            def one(view, e):
                return (view[e:e + 1] if isinstance(e, int) else view[bass.ds(e, 1)]).rearrange("a p k n -> p (a k) n")

            def run_pairs(eng, body, count):
                body(0, 0, 0, True, False)
                body(1, 1, 0, False, False)
                with eng.Fori(1, count // 2 - 1) as i:
                    body(2 * i, 0, i, False, False)
                    body(2 * i + 1, 1, i, False, False)
                body(count - 2, 0, count // 2 - 1, False, False)
                body(count - 1, 1, count // 2 - 1, False, True)

            def over_extra(eng, body):
                total = eng.value_load(extra[0:1, 0:1], min_val=0, max_val=EXTRA)
                with eng.If(total > 0):
                    with eng.Fori(1, total + 1) as n:
                        body(n)

            def is_first(e):
                return isinstance(e, int) and e == 0

            with nc.Block() as block:
                @block.sync
                def _(sp):
                    sp.dma_start(gain[:], d["norm_final"].partition_broadcast(P)).then_inc(sem("last_gain_loaded"), 16)

                    def body(e, b, n, first, last):
                        if not (isinstance(e, int) and e < 2):
                            sp.wait_ge(sem("up_done"), e - 1)
                        sp.dma_start(w_gate[b][:], one(wg_v, e)).then_inc(sem(f"w_gate_loaded{b}"), 16)
                        sp.dma_start(w_up[b][:], one(wu_v, e)).then_inc(sem(f"w_up_loaded{b}"), 16)
                        if not (isinstance(e, int) and e < 2):
                            sp.wait_ge(sem("down_done"), e - 1)
                        sp.dma_start(w_down[b][:], one(wd_v, e)).then_inc(sem(f"w_down_loaded{b}"), 16)
                    run_pairs(sp, body, NE)

                    def more(n):
                        sp.wait_ge(sem("down_done"), n + NE - 1)
                        sp.wait_ge(sem("up_done"), n + NE - 1)
                        e = sp.value_load(extra[0:1, bass.ds(n, 1)], min_val=0, max_val=NE - 1)
                        sp.dma_start(w_gate[0][:], one(wg_v, e)).then_inc(sem("more_w_loaded"), 16)
                        sp.dma_start(w_up[0][:], one(wu_v, e)).then_inc(sem("more_w_loaded"), 16)
                        sp.dma_start(w_down[0][:], one(wd_v, e)).then_inc(sem("more_w_loaded"), 16)
                        sp.wait_ge(sem("y_evacuated"), n + NE)
                        sp.dma_start(y_dram[bass.ds((n + (NE - 1)) * P, P), :], y_out[0][:]).then_inc(sem("more_y_stored"), 16)
                        sp.wait_ge(sem("more_y_stored"), n * 16)
                    over_extra(sp, more)
                    sp.sem_inc(sem("more_over"), 1)

                    for t in range(NTR):
                        b = t % 2
                        if t >= 2:
                            sp.wait_ge(sem("out_ready"), t - 1)
                        sp.dma_start(h_in[b][:], h2_dram[(t + 1) * P:(t + 2) * P, :]).then_inc(sem(f"h_last_loaded{b}"), 16)
                    sp.wait_ge(sem("out_stored0"), 16 * NTR // 2)
                    sp.wait_ge(sem("out_stored1"), 16 * NTR // 2)

                @block.gpsimd
                def _(pool):
                    for e in range(NE):
                        b = e % 2
                        if e >= 2:
                            pool.wait_ge(sem("x_turned"), e - 1)
                        pool.indirect_dma_start(x_rows[b][:], None, u2_dram, bass.IndirectOffsetOnAxis(ap=slot_row[:, e:e + 1], axis=0)
                                                ).then_inc(sem(f"x_rows_loaded{b}"), 16)

                    def more(n):
                        pool.wait_ge(sem("x_rows_loaded1"), 16 * NE // 2)
                        pool.wait_ge(sem("more_row_ready"), n)
                        pool.indirect_dma_start(x_rows[0][:], None, u2_dram, bass.IndirectOffsetOnAxis(ap=more_row[:, 0:1], axis=0)
                                                ).then_inc(sem("more_x_loaded"), 16)
                    over_extra(pool, more)

                    pool.wait_ge(sem("y_stored0"), 16 * NE // 2)
                    pool.wait_ge(sem("y_stored1"), 16 * NE // 2)
                    pool.wait_ge(sem("more_over"), 1)
                    def bring(t):
                        b = t % 2
                        if t >= 2:
                            pool.wait_ge(sem(f"out_stored{b}"), 16 * (t // 2))
                        for j in range(2):
                            pool.indirect_dma_start(y_in[j][b][:], None, y_dram,
                                                    bass.IndirectOffsetOnAxis(ap=slots[:, j, t:t + 1], axis=0)
                                                    ).then_inc(sem(f"y_in_loaded{b}"), 16)
                    bring(0)
                    for t in range(NTR):
                        if t + 1 < NTR:
                            bring(t + 1)
                        pool.wait_ge(sem("rms_in"), t + 1)
                        pool.tensor_tensor(rms[:, 2, t % 2:t % 2 + 1], rms[:, 1, t % 2:t % 2 + 1], half[:, 0:1], ALU.pow
                                           ).then_inc(sem("rms_ready"), 1)

                @block.scalar
                def _(act):
                    def body(e, b, n, first, last):
                        act.wait_ge(sem("x_turned"), e + 1)
                        act.activation(x_t[b][:, 0:4, :], ps[:, 4, :], ACT.Copy).then_inc(sem("x_t0_ready"), 1)
                        if not first:
                            finish(e - 1, 1 - b, n - 1 + b)
                        act.wait_ge(sem("gate_done"), e + 1)
                        act.activation(act_t[:], ps[:, 0, :], ACT.Tanh, scale=0.5).then_inc(sem("act_t_ready"), 1)
                        if last:
                            finish(e, b, n)

                    def finish(e, b, n):
                        act.wait_ge(sem("hid_turned"), e + 1)
                        act.activation(hid_t[:], ps[:, 2, :], ACT.Copy).then_inc(sem("hid_t_ready"), 1)
                        act.wait_ge(sem("down_done"), e + 1)
                        if not (isinstance(e, int) and e < 2):
                            act.wait_ge(sem(f"y_stored{b}"), 16 * n)
                        act.activation(y_out[b][:], ps[:, 6:8, :].rearrange("p a c -> p (a c)"), ACT.Copy).then_inc(sem("y_evacuated"), 1)
                        act.wait_ge(sem("y_evacuated"), e + 1)
                        act.dma_start(y_dram[bass.ds(e * P, P), :], y_out[b][:]).then_inc(sem(f"y_stored{b}"), 16)
                    run_pairs(act, body, NE)
                    act.wait_ge(sem("y_stored0"), 16 * NE // 2)

                    def more(n):
                        act.wait_ge(sem("x_turned"), n + NE)
                        act.activation(x_t[0][:, 0:4, :], ps[:, 4, :], ACT.Copy).then_inc(sem("x_t0_ready"), 1)
                        act.wait_ge(sem("gate_done"), n + NE)
                        act.activation(act_t[:], ps[:, 0, :], ACT.Tanh, scale=0.5).then_inc(sem("act_t_ready"), 1)
                        act.wait_ge(sem("hid_turned"), n + NE)
                        act.activation(hid_t[:], ps[:, 2, :], ACT.Copy).then_inc(sem("hid_t_ready"), 1)
                        act.wait_ge(sem("down_done"), n + NE)
                        act.activation(y_out[0][:], ps[:, 6:8, :].rearrange("p a c -> p (a c)"), ACT.Copy).then_inc(sem("y_evacuated"), 1)
                    over_extra(act, more)

                    for t in range(NTR):
                        b = t % 2
                        act.wait_ge(sem("h3_ready"), t + 1)
                        act.activation(y_in[0][b][:], h_in[b][:], ACT.Square, scale=D ** -0.5, accum_out=rms[:, 0, b:b + 1]
                                       ).then_inc(sem("last_mean_square"), 1)
                        act.wait_ge(sem("out_ready"), t + 1)
                        act.dma_start(out[t * P:(t + 1) * P, :], y_in[1][b][:]).then_inc(sem(f"out_stored{b}"), 16)

                @block.vector
                def _(dve):
                    def body(e, b, n, first, last):
                        dve.wait_ge(sem("x_turned"), e + 1)
                        dve.tensor_copy(x_t[b][:, 4:8, :], ps[:, 5, :]).then_inc(sem("x_t1_ready"), 1)
                        dve.wait_ge(sem("act_t_ready"), e + 1)
                        if not is_first(e):
                            dve.wait_ge(sem("hid_turned"), e)
                        dve.scalar_tensor_tensor(hid[:], act_t[:], 1.0, ps[:, 0, :], ALU.add, ALU.mult).then_inc(sem("hid_half"), 1)
                        dve.wait_ge(sem("hid_half"), e + 1)
                        dve.wait_ge(sem("up_done"), e + 1)
                        dve.scalar_tensor_tensor(hid[:], hid[:], 0.5, ps[:, 1, :], ALU.mult, ALU.mult).then_inc(sem("hid_ready"), 1)
                    run_pairs(dve, body, NE)

                    def more(n):
                        dve.tensor_copy(more_row[:], slot_row[:, bass.ds(n + (NE - 1), 1)]).then_inc(sem("more_row_ready"), 1)
                        body(n + (NE - 1), 0, 0, False, False)
                    over_extra(dve, more)

                    for t in range(NTR):
                        b = t % 2
                        c = rms[:, :, b]
                        dve.wait_ge(sem(f"h_last_loaded{b}"), 16 * (t // 2 + 1))
                        dve.wait_ge(sem(f"y_in_loaded{b}"), 32 * (t // 2 + 1))
                        for j in range(2):
                            dve.scalar_tensor_tensor(h_in[b][:], y_in[j][b][:], weight[:, j, t:t + 1], h_in[b][:], ALU.mult, ALU.add
                                                     ).then_inc(sem("h3_ready" if j else "h3_first"), 1)
                            dve.wait_ge(sem("h3_ready" if j else "h3_first"), t + 1)
                        dve.wait_ge(sem("last_mean_square"), t + 1)
                        dve.tensor_scalar(rms[:, 1, b:b + 1], rms[:, 0, b:b + 1], 1e-6, None, ALU.add, ALU.bypass
                                          ).then_inc(sem("rms_in"), 1)
                        dve.wait_ge(sem("rms_ready"), t + 1)
                        if t == 0:
                            dve.wait_ge(sem("last_gain_loaded"), 16)
                        dve.scalar_tensor_tensor(y_in[1][b][:], h_in[b][:], rms[:, 2, b:b + 1], gain[:], ALU.mult, ALU.mult
                                                 ).then_inc(sem("out_ready"), 1)

                @block.tensor
                def _(pe):
                    def turn_x(e, b):
                        if not is_first(e):
                            pe.wait_ge(sem("x_t0_ready"), e)
                            pe.wait_ge(sem("x_t1_ready"), e)
                        for k in range(KD):
                            mm = pe.transpose(ps[:, 4 + k // 4, (k % 4) * P:(k % 4 + 1) * P], x_rows[b][:, k * P:(k + 1) * P], ident)
                        mm.then_inc(sem("x_turned"), 1)

                    def product(bank, w, b):
                        for k in range(KD):
                            mm = pe.matmul(ps[:, bank, :], x_t[b][:, k, :], w[:, k, :], start=(k == 0), stop=(k == KD - 1))
                        return mm

                    def turn_hid(e):
                        pe.wait_ge(sem("hid_ready"), e + 1)
                        for k in range(KE):
                            mm = pe.transpose(ps[:, 2, k * P:(k + 1) * P], hid[:, k * P:(k + 1) * P], ident)
                        mm.then_inc(sem("hid_turned"), 1)

                    def down(e, b):
                        pe.wait_ge(sem("hid_t_ready"), e + 1)
                        if not is_first(e):
                            pe.wait_ge(sem("y_evacuated"), e)
                        for n in range(2):
                            for k in range(KE):
                                mm = pe.matmul(ps[:, 6 + n, :], hid_t[:, k, :], w_down[b][:, k, n * 512:(n + 1) * 512],
                                               start=(k == 0), stop=(k == KE - 1))
                        mm.then_inc(sem("down_done"), 1)

                    def gate(e, b):
                        pe.wait_ge(sem("x_t0_ready"), e + 1)
                        pe.wait_ge(sem("x_t1_ready"), e + 1)
                        if not is_first(e):
                            pe.wait_ge(sem("hid_ready"), e)
                        product(0, w_gate[b], b).then_inc(sem("gate_done"), 1)

                    def body(e, b, n, first, last):
                        pe.wait_ge(sem(f"w_gate_loaded{b}"), 16 * (n + 1))
                        gate(e, b)
                        if not first:
                            turn_hid(e - 1)
                        pe.wait_ge(sem(f"w_up_loaded{b}"), 16 * (n + 1))
                        product(1, w_up[b], b).then_inc(sem("up_done"), 1)
                        if not last:
                            pe.wait_ge(sem(f"x_rows_loaded{1 - b}"), 16 * (n + 1 + b))
                            turn_x(e + 1, 1 - b)
                        if not first:
                            pe.wait_ge(sem(f"w_down_loaded{1 - b}"), 16 * (n + b))
                            down(e - 1, 1 - b)
                        if last:
                            turn_hid(e)
                            pe.wait_ge(sem(f"w_down_loaded{b}"), 16 * (n + 1))
                            down(e, b)
                    pe.wait_ge(sem("x_rows_loaded0"), 16)
                    turn_x(0, 0)
                    run_pairs(pe, body, NE)

                    def more(n):
                        e = n + (NE - 1)
                        pe.wait_ge(sem("more_x_loaded"), n * 16)
                        turn_x(e, 0)
                        pe.wait_ge(sem("more_w_loaded"), n * 48)
                        gate(e, 0)
                        product(1, w_up[0], 0).then_inc(sem("up_done"), 1)
                        turn_hid(e)
                        down(e, 0)
                    over_extra(pe, more)


_NAMES = ['x', 'meta_tokens', 'norm_mix', 'w_in', 'shift_mu', 'decay_w0', 'decay_up', 'iclr_a0', 'iclr_up', 'gate_up',
          'k_k', 'k_a', 'r_k', 'ln_w_a', 'ln_b_a', 'gn_w_b', 'w_out', 'norm_ffn', 'router_group_w', 'router_group_b',
          'router_expert_w', 'router_expert_b', 'moe_w_gate', 'moe_w_up', 'moe_w_down', 'norm_final']


def kernel(**inputs):
    import concourse.bacc as bacc
    from concourse.bass_utils import run_bass_kernel_spmd

    nc = bacc.Bacc("TRN2", target_bir_lowering=False, num_devices=1)
    table, rotation = shape_constants()
    arrays = {"consts": table, "rotation": rotation}
    for name in _NAMES:
        a = np.ascontiguousarray(inputs[name])
        if name not in ("meta_tokens", "norm_final"):
            a = a[0]
        arrays[name] = a
    data = {}
    for name, a in arrays.items():
        data[name] = nc.dram_tensor("in_" + name, a.shape, mybir.dt.from_np(a.dtype), kind="ExternalInput").ap()
    out = nc.dram_tensor("out_rows", (SEQ, D), F32, kind="ExternalOutput").ap()
    layer(nc, data, out)
    r = run_bass_kernel_spmd(nc, [{"in_" + n: a for n, a in arrays.items()}], core_ids=[0])
    return r.results[0]["out_rows"].reshape(1, SEQ, D)
```

```python
from contextlib import ExitStack
import math

import numpy as np

import concourse.bass as bass
from concourse import mybir

F32, F32R, I32 = mybir.dt.float32, mybir.dt.float32r, mybir.dt.int32
ACT = mybir.ActivationFunctionType
ALU = mybir.AluOpType
X = mybir.AxisListType.X

P = 128
D = 1024
KD = D // P
SEQ = 1024
N_META = 16
NT = SEQ // P + 1
PAD = P - N_META
ROWS = NT * P
C = 64
DA, HA, HEAD_A = 512, 8, 64
DB, HB, HEAD_B = 512, 4, 128
PA, PB = 3 * DA + 256, 4 * DB
PIN = PA + PB
GROUP_COLS = 480
NGRP = PIN // GROUP_COLS
N_GROUPS, PER_GROUP, NE = 4, 8, 32
NR = N_GROUPS + NE
DE = 512
KE = DE // P
DECAY = math.exp(-0.5)
EXTRA = (2 * SEQ - 1) // P
ROW_PARAMS = ("decay_w0", "iclr_a0", "k_k", "k_a", "r_k", "ln_w_a", "ln_b_a", "gn_w_b")
NBLK = NE + EXTRA
SUB = 16

CONST_PARTS = [
    ("ident", P), ("cum_in", P), ("cum_ex", P), ("after", P), ("chunk_of", 2),
    ("lt_sub", C), ("gt_sub", C), ("gt_off", C), ("lt", C), ("le", C), ("ident_c", C),
    ("before", P), ("ones", P),
    ("ret_mask", HB * C), ("q_decay", HB), ("k_decay", HB), ("r_decay", HB),
    ("group_prio", N_GROUPS), ("expert_prio", NE), ("slot_base", NE), ("before_e", NE * NE),
    ("thresholds", 8), ("block_no", EXTRA),
]
CONST_AT, _n = {}, 0
for _name, _w in CONST_PARTS:
    CONST_AT[_name] = (_n, _n + _w)
    _n += _w
NCONST = _n


def shape_constants():
    c = {}
    p = np.arange(P)[:, None]
    q = np.arange(P)[None, :]
    same = p // C == q // C
    c["ident"] = p == q
    c["cum_in"] = same & (p <= q)
    c["cum_ex"] = same & (p < q)
    c["after"] = same & (p > q)
    c["chunk_of"] = p // C == np.arange(2)[None, :]
    s = p % C
    t = np.arange(C)[None, :]
    sub = s // SUB == t // SUB
    c["lt_sub"] = (s < t) & sub
    c["gt_sub"] = (s > t) & sub
    c["gt_off"] = (s > t) & ~sub
    c["lt"] = s < t
    c["le"] = s <= t
    c["ident_c"] = s == t
    c["before"] = p < q
    c["ones"] = np.ones((P, P))
    lg = np.log1p(-np.exp2(-5.0 - np.arange(HB)))
    scale = HEAD_B ** -0.5
    rel = t - s
    c["ret_mask"] = np.concatenate([np.where(rel >= 0, np.exp(g * np.maximum(rel, 0)), 0.0) * scale for g in lg], 1)
    c["q_decay"] = np.exp(lg[None, :] * (s + 1))
    c["k_decay"] = np.exp(lg[None, :] * (C - 1 - s)) * scale
    c["r_decay"] = np.exp(lg * C)[None, :] + np.zeros((P, 1))
    c["group_prio"] = np.arange(N_GROUPS, 0, -1)[None, :] + np.zeros((P, 1))
    c["expert_prio"] = np.arange(NE, 0, -1)[None, :] + np.zeros((P, 1))
    c["slot_base"] = np.arange(NE)[None, :] * P + np.zeros((P, 1))
    e = np.arange(NE)
    c["before_e"] = (e[None, :] < e[:, None]).reshape(1, -1) + np.zeros((P, 1))
    c["thresholds"] = (np.arange(8) + 1)[None, :] * P + np.zeros((P, 1))
    c["block_no"] = np.arange(EXTRA)[None, :] + np.zeros((P, 1))
    table = np.zeros((P, NCONST), np.float32)
    for name, (a, b) in CONST_AT.items():
        table[:, a:b] = c[name]
    pos = np.maximum(np.arange(ROWS) - PAD, 0).astype(np.float32)
    inv = (np.float32(10000.0) ** (-np.arange(0, HEAD_B, 2, dtype=np.float32) / np.float32(HEAD_B))).astype(np.float32)
    ang = (pos[:, None] * inv[None, :]).astype(np.float32)
    rot = np.concatenate([np.cos(ang.astype(np.float64)), np.sin(ang.astype(np.float64))], 1).astype(np.float32)
    return table, rot


class Turn:
    def __init__(self, i, after):
        self.i, self.after = i, after
        self.has_before = not (isinstance(i, int) and i == 0)

    def lead(self, eng):
        if not isinstance(self.i, int):
            eng.wait_ge(self.loaded, 16)


def layer(nc, d, out):
    with ExitStack() as top:
        sems = {}

        def sem(name):
            if name not in sems:
                sems[name] = nc.alloc_semaphore(name=name)
            return sems[name]

        def free_sems():
            names = [n for n in sems if n != "consts_loaded"]
            nc.clear_and_free_semaphores([sems.pop(n) for n in names])
            nc.all_engine_barrier()

        def tile(stack, name, shape, dt=F32):
            return stack.enter_context(nc.sbuf_tensor(name, shape, dt))

        scr = lambda name, shape, dt=F32: nc.dram_tensor(name, shape, dt, kind="Internal").ap()
        z_dram = scr("z_rows", (ROWS + 1, PIN))
        h2_dram = scr("h2_rows", (ROWS, D))
        u2_dram = scr("u2_rows", (ROWS, D))
        y_dram = scr("y_slots", (NBLK * P, D))
        slot_row_dram = scr("slot_rows", (NBLK * P, 1))

        ps = top.enter_context(nc.psum_tensor("ps", [P, 8, 512], F32))
        consts = tile(top, "consts", [P, NCONST])
        logits = tile(top, "logits", [P, NT, NR])
        half = tile(top, "minus_half", [P, 8])

        def cst(name):
            a, b = CONST_AT[name]
            return consts[:, a:b]

        ident = cst("ident")

        Turn.loaded = sem("consts_loaded")

        def two_names(stack, name, shape, dt, other, other_shape, other_dt=F32):
            at = -(-nc.sbuf_base // 32) * 32
            first = tile(stack, name, shape, dt)
            assert nc.sbuf_base == at + 4 * math.prod(shape[1:])
            return first, nc.alloc_sbuf_tensor_at(other, other_shape, other_dt, offset=at)

        with ExitStack() as mixing:
            row_params, norm_work = two_names(mixing, "row_params", [P, len(ROW_PARAMS), DA], F32,
                                              "norm_work", [P, 4, D])
            rows = {n: row_params[:, i, :] for i, n in enumerate(ROW_PARAMS)}
            gain_ffn = tile(mixing, "norm_ffn_rows", [P, D])
            router_b = tile(mixing, "router_b", [P, NR])
            w_out, router_w = tile(mixing, "w_out", [P, KD, D]), tile(mixing, "router_w", [P, KD, NR])
            project(nc, d, locals())
            free_sems()
            mix(nc, d, locals())
        free_sems()
        dispatch_and_experts(nc, d, out, locals())


def project(nc, d, env):
    sem, tile, ps, ident, z_dram, consts, half = (env[k] for k in ("sem", "tile", "ps", "ident", "z_dram", "consts", "half"))
    y_dram, two_names, norm_work, rows, gain_ffn, router_b, w_out, router_w = (env[k] for k in (
        "y_dram", "two_names", "norm_work", "rows", "gain_ffn", "router_b", "w_out", "router_w"))
    with ExitStack() as s:
        u_hi = tile(s, "u_hi", [P, KD, ROWS], F32R)
        u_lo = tile(s, "u_lo", [P, KD, ROWS], F32R)
        h_in = [norm_work[:, b, :] for b in range(2)]
        u = [norm_work[:, 2 + b, :] for b in range(2)]
        gain = tile(s, "norm_mix_rows", [P, D])
        stat = tile(s, "stat", [P, 3, 2])
        shape = [P, KD, GROUP_COLS]
        w_lo, w_raw = zip(*(two_names(s, f"w_lo{b}", shape, F32R, f"w_raw{b}", shape) for b in range(2)))
        w_hi = [tile(s, f"w_hi{b}", shape, F32R) for b in range(2)]
        z_out = [tile(s, f"z_out{b}", [P, GROUP_COLS]) for b in range(3)]
        zero_row = u[1]
        w_view = d["w_in"].rearrange("(k p) n -> p k n", p=P)
        x = d["x"]

        def run_groups(eng, body):
            with eng.Fori(0, NGRP // 2 - 1) as i:
                body(2 * i + 1, 1, i, False)
                body(2 * i + 2, 0, i + 1, False)
            body(NGRP - 1, 1, NGRP // 2 - 1, True)

        with nc.Block() as block:
            @block.sync
            def _(sp):
                def store(g, t):
                    sp.wait_ge(sem("z_evacuated"), g * NT + t + 1)
                    sp.dma_start(z_dram[1 + t * P:1 + (t + 1) * P, bass.ds(g * GROUP_COLS, GROUP_COLS)],
                                 z_out[t % 3][:]).then_inc(sem(f"z_stored{t % 3}"), 16)

                sp.dma_start(gain[:], d["norm_mix"].partition_broadcast(P)).then_inc(sem("gain_loaded"), 16)
                sp.wait_ge(sem("h0_zeroed"), 1)
                sp.dma_start(h_in[0][PAD:P, :], d["meta_tokens"]).then_inc(sem("h_loaded0"), 16)
                sp.dma_start(h_in[1], x[0:P, :]).then_inc(sem("h_loaded1"), 16)
                sp.dma_start(consts[:], d["consts"]).then_inc(sem("consts_loaded"), 16)
                sp.dma_start(w_raw[0][:], w_view[:, :, 0:GROUP_COLS]).then_inc(sem("w_loaded0"), 16)
                for t in range(2, NT):
                    sp.wait_ge(sem("u_ready"), t - 1)
                    sp.dma_start(h_in[t % 2], x[(t - 1) * P:t * P, :]).then_inc(sem(f"h_loaded{t % 2}"), 16)
                    if t == 3:
                        sp.dma_start(w_raw[1][:], w_view[:, :, GROUP_COLS:2 * GROUP_COLS]).then_inc(sem("w_loaded1"), 16)
                    if t >= 3:
                        store(0, t - 3)
                for t in range(NT - 3, NT):
                    store(0, t)
                sp.wait_ge(sem("zero_row_ready"), 1)
                for i in range(PIN // 960):
                    sp.dma_start(z_dram[0:1, i * 960:(i + 1) * 960], zero_row[0:1, 0:960]).then_inc(sem("zero_stored"), 16)

                params = [(w_out[:, k, :], d["w_out"][k * P:(k + 1) * P, :]) for k in range(KD)]
                params += [(rows[name], d[name].partition_broadcast(P)) for name in ROW_PARAMS]
                params += [
                    (gain_ffn[:], d["norm_ffn"].partition_broadcast(P)),
                    (router_b[:, 0:N_GROUPS], d["router_group_b"].partition_broadcast(P)),
                    (router_b[:, N_GROUPS:NR], d["router_expert_b"].partition_broadcast(P)),
                    (router_w[:, :, 0:N_GROUPS], d["router_group_w"].rearrange("(k p) n -> p k n", p=P)),
                    (router_w[:, :, N_GROUPS:NR], d["router_expert_w"].rearrange("(k p) n -> p k n", p=P))]
                assert EXTRA % (NGRP // 2 - 1) == 0
                zero_share = EXTRA // (NGRP // 2 - 1)

                def group(g, b, n, last):
                    if not last:
                        sp.wait_ge(sem("z_ready"), g * NT)
                        sp.dma_start(w_raw[1 - b][:], w_view[:, :, bass.ds((g + 1) * GROUP_COLS, GROUP_COLS)]
                                     ).then_inc(sem(f"w_loaded{1 - b}"), 16)
                    else:
                        sp.wait_ge(sem("zero_stored"), 16 * (PIN // 960 + EXTRA))
                    for t in range(NT):
                        store(g, t)
                        if last:
                            for dst, src in params[t::NT]:
                                sp.dma_start(dst, src).then_inc(sem("mix_params"), 16)
                        elif b == 1 and t < zero_share:
                            sp.dma_start(y_dram[bass.ds((n * zero_share + NE + t) * P, P), :], zero_row
                                         ).then_inc(sem("zero_stored"), 16)
                run_groups(sp, group)
                for r in range(3):
                    sp.wait_ge(sem(f"z_stored{r}"), 16 * (NT // 3) * NGRP)
                sp.wait_ge(sem("mix_params"), 16 * len(params))

            @block.scalar
            def _(act):
                def square(t):
                    b = t % 2
                    act.wait_ge(sem(f"h_loaded{b}"), 16 * (t // 2 + 1))
                    if t >= 2:
                        act.wait_ge(sem("u_ready"), t - 1)
                        act.wait_ge(sem("u_turned"), t - 1)
                    act.activation(u[b], h_in[b], ACT.Square, scale=D ** -0.5,
                                   accum_out=stat[:, 0, b:b + 1]).then_inc(sem("mean_square"), 1)

                def high(t):
                    b = t % 2
                    act.wait_ge(sem("u_turned"), t + 1)
                    act.activation(u_hi[:, :, t * P:(t + 1) * P],
                                   ps[:, 2 * b:2 * b + 2, :].rearrange("p a (k t) -> p (a k) t", t=P),
                                   ACT.Copy).then_inc(sem("u_hi_ready"), 1)

                def split(g, b, n):
                    act.wait_ge(sem(f"w_loaded{b}"), 16 * (n + 1))
                    if not (isinstance(g, int) and g < 2):
                        act.wait_ge(sem("z_ready"), (g - 1) * NT)
                    act.activation(w_hi[b][:], w_raw[b][:], ACT.Copy).then_inc(sem("w_hi_ready"), 1)

                def evacuate(g, t):
                    act.wait_ge(sem("z_ready"), g * NT + t + 1)
                    if not (isinstance(g, int) and g == 0 and t < 3):
                        act.wait_ge(sem(f"z_stored{t % 3}"), 16 * (g * (NT // 3) + t // 3))
                    act.activation(z_out[t % 3][:], ps[:, 4 + t % 3, 0:GROUP_COLS], ACT.Copy
                                   ).then_inc(sem("z_evacuated"), 1)
                square(0)
                square(1)
                high(0)
                split(0, 0, 0)
                for t in range(NT):
                    if t + 2 < NT:
                        square(t + 2)
                    if t + 1 < NT:
                        high(t + 1)
                    if t == 3:
                        split(1, 1, 0)
                    evacuate(0, t)

                def group(g, b, n, last):
                    evacuate(g, 0)
                    evacuate(g, 1)
                    if not last:
                        split(g + 1, 1 - b, n + b)
                    for t in range(2, NT):
                        evacuate(g, t)
                run_groups(act, group)

            @block.gpsimd
            def _(pool):
                pool.memset(half[:], -0.5).then_inc(sem("half_ready"), 1)
                pool.wait_ge(sem("half_ready"), 1)
                for t in range(NT):
                    b = t % 2
                    pool.wait_ge(sem("mean_eps"), t + 1)
                    pool.tensor_tensor(stat[:, 2, b:b + 1], stat[:, 1, b:b + 1], half[:, 0:1], ALU.pow
                                       ).then_inc(sem("rstd_ready"), 1)

            @block.vector
            def _(dve):
                dve.memset(h_in[0], 0.0).then_inc(sem("h0_zeroed"), 1)
                dve.wait_ge(sem("gain_loaded"), 16)

                def norm(t):
                    b = t % 2
                    dve.wait_ge(sem("mean_square"), t + 1)
                    dve.tensor_scalar(stat[:, 1, b:b + 1], stat[:, 0, b:b + 1], 1e-6, None, ALU.add
                                      ).then_inc(sem("mean_eps"), 1)
                    dve.wait_ge(sem("rstd_ready"), t + 1)
                    dve.scalar_tensor_tensor(u[b], h_in[b], stat[:, 2, b:b + 1], gain[:], ALU.mult, ALU.mult
                                             ).then_inc(sem("u_ready"), 1)

                def low_rows(t):
                    b = t % 2
                    dve.wait_ge(sem("u_hi_ready"), t + 1)
                    dve.tensor_tensor(u_lo[:, :, t * P:(t + 1) * P],
                                      ps[:, 2 * b:2 * b + 2, :].rearrange("p a (k t) -> p (a k) t", t=P),
                                      u_hi[:, :, t * P:(t + 1) * P].bitcast(F32), ALU.subtract
                                      ).then_inc(sem("u_lo_ready"), 1)

                def low(g, b):
                    dve.wait_ge(sem("w_hi_ready"), g + 1)
                    dve.tensor_tensor(w_lo[b][:], w_raw[b][:], w_hi[b][:].bitcast(F32), ALU.subtract
                                      ).then_inc(sem("w_lo_ready"), 1)
                norm(0)
                norm(1)
                low_rows(0)
                low(0, 0)
                for t in range(1, NT):
                    low_rows(t)
                    if t + 1 < NT:
                        norm(t + 1)
                    if t == 5:
                        low(1, 1)
                dve.wait_ge(sem("u_turned"), NT)
                dve.memset(zero_row, 0.0).then_inc(sem("zero_row_ready"), 1)
                with dve.Fori(1, NGRP // 2) as i:
                    low(2 * i, 0)
                    low(2 * i + 1, 1)

            @block.tensor
            def _(pe):
                pe.wait_ge(sem("consts_loaded"), 16)

                def turn(t):
                    b = t % 2
                    if t >= 2:
                        pe.wait_ge(sem("u_lo_ready"), t - 1)
                    pe.wait_ge(sem("u_ready"), t + 1)
                    for k in range(KD):
                        last = pe.transpose(ps[:, 2 * b + k // 4, (k % 4) * P:(k % 4 + 1) * P],
                                            u[b][:, k * P:(k + 1) * P], ident)
                    last.then_inc(sem("u_turned"), 1)

                def products(g, b, t):
                    if not (isinstance(g, int) and g == 0 and t < 3):
                        pe.wait_ge(sem("z_evacuated"), g * NT + t - 2)
                    acc = ps[:, 4 + t % 3, 0:GROUP_COLS]
                    for k in range(KD):
                        for a, w, n3 in ((u_hi, w_hi, 0), (u_hi, w_lo, 1), (u_lo, w_hi, 2)):
                            mm = pe.matmul(acc, a[:, k, t * P:(t + 1) * P], w[b][:, k, :],
                                           start=(k == 0 and n3 == 0), stop=(k == KD - 1 and n3 == 2))
                    mm.then_inc(sem("z_ready"), 1)

                turn(0)
                turn(1)
                pe.wait_ge(sem("w_hi_ready"), 1)
                pe.wait_ge(sem("w_lo_ready"), 1)
                for t in range(NT):
                    pe.wait_ge(sem("u_hi_ready"), t + 1)
                    pe.wait_ge(sem("u_lo_ready"), t + 1)
                    products(0, 0, t)
                    if t + 2 < NT:
                        turn(t + 2)

                def group(g, b, n, last):
                    pe.wait_ge(sem("w_hi_ready"), g + 1)
                    pe.wait_ge(sem("w_lo_ready"), g + 1)
                    for t in range(NT):
                        products(g, b, t)
                run_groups(pe, group)


def mix(nc, d, env):
    sem, tile, ps, ident, cst = (env[k] for k in ("sem", "tile", "ps", "ident", "cst"))
    rows, gain, router_b, w_out, router_w = (env[k] for k in ("rows", "gain_ffn", "router_b", "w_out", "router_w"))
    z_dram, h2_dram, u2_dram, consts, half, logits = (
        env[k] for k in ("z_dram", "h2_dram", "u2_dram", "consts", "half", "logits"))
    with ExitStack() as s:
        def sb(name, *shape):
            return tile(s, name, [P, *shape])

        mu = sb("mu", PA)
        lora_up, gate_up = sb("lora_up", DA), sb("gate_up", DA)
        z_cur, z_prev, z_ret = sb("z_cur", PA), sb("z_prev", PA), sb("z_ret", PB)
        rot, h_in = sb("rot", 2 * C), sb("h_res", D)
        zs = sb("zs", PA)
        r, k, v = (zs[:, i * DA:(i + 1) * DA] for i in range(3))

        lora_t, gate_t = sb("lora_t", P), sb("gate_t", P)
        log_w, iclr, gate, kk, k2, b_row, e_in, e_neg, e_ex, e_after, r_d, k_d, b_d, a_d, r_t, a_t, tmp = (
            sb(n, DA) for n in ("log_w", "iclr", "gate", "kk", "k2", "b_row", "e_in", "e_neg", "e_ex", "e_after",
                                "r_d", "k_d", "b_d", "a_d", "r_t", "a_t", "tmp"))
        after_pair, turned_pair = sb("after_pair", D), sb("turned_pair", D)
        k_h, b_h = after_pair[:, 0:DA], after_pair[:, DA:D]
        k_t, b_t = turned_pair[:, 0:DA], turned_pair[:, DA:D]
        stat = sb("mix_stat", 10, HA)
        decay_c = sb("decay_c", HA)
        ld_t, ld, lo = e_in, e_neg, e_ex
        ak_t, rb_t, rk_t = sb("ak_t", DA), sb("rb_t", DA), sb("rk_t", DA)
        l2, l2_t, l4, l4_t, l8 = log_w, kk, b_row, r_d, k_d
        inv = sb("inv", DA)
        x_m, x_t, x2_t, x_p, q_m = e_after, e_in, e_neg, lo, b_d
        z0, w_m = sb("z0", 2, DA), sb("w_m", 2, DA)
        diag_c = iclr[:].rearrange("p (c k) -> p c k", c=2)
        m_t = sb("m_t", 2, DA // 2)
        n_m = sb("n_m", 2, DA // 2)
        state = [sb(f"state{i}", DA // 2) for i in range(2)]
        rz_t, y = l4_t, inv
        bonus = sb("bonus", DA)

        z_cos, z_sin, qk = sb("z_cos", D), sb("z_sin", D), sb("qk", D)
        q_t, kr_t, k_dec, s_t = sb("q_t", DB), sb("kr_t", DB), sb("k_dec", DB), sb("s_t", HB * C)
        memory = [sb(f"memory{i}", DB) for i in range(2)]
        memory_d = a_t
        in_s, y_ret, ret_gate = sb("in_s", DB), sb("y_ret", DB), sb("ret_gate", DB)
        ret_tmp = tmp
        mixed_t = z_cos[:].rearrange("p (k t) -> p k t", t=P)
        h2, u2 = after_pair, z_sin
        u2_t = h_in[:].rearrange("p (k t) -> p k t", t=P)

        def heads(ap, n=HA):
            return ap.rearrange("p (h c) -> p h c", h=n)

        def per_head(small, n=HA):
            return small.unsqueeze(2).to_broadcast([P, n, DA // n])

        def parity(ap):
            return ap.rearrange("p (q a c) -> p a q c", a=2, c=C)

        def bank_pair(b, at=0):
            return ps[:, b:b + 2, at:at + 256].rearrange("p a (q c) -> p a q c", c=C)

        def all_heads(mask):
            return mask.unsqueeze(1).to_broadcast([P, HA, C])

        def all_pairs(mask):
            return mask.unsqueeze(1).unsqueeze(1).to_broadcast([P, 2, 4, C])

        def run(eng, body):
            body(Turn(0, 1))
            with eng.Fori(2, NT) as v_:
                body(Turn(v_ - 1, v_))
            body(Turn(NT - 1, NT))

        def at(t, n=P):
            return slice(t.i * n, (t.i + 1) * n) if isinstance(t.i, int) else bass.ds(t.i * n, n)

        with nc.Block() as block:
            @block.sync
            def _(sp):
                sp.wait_ge(sem("h_res_zeroed"), 1)

                def store(n):
                    sp.wait_ge(sem("h2_ready"), n)
                    sp.dma_start(h2_dram[bass.ds((n - 1) * P, P), :], h2[:]).then_inc(sem("h2_stored"), 16)
                    sp.wait_ge(sem("u2_ready"), n)
                    sp.dma_start(u2_dram[bass.ds((n - 1) * P, P), :], u2[:]).then_inc(sem("u2_stored"), 16)

                def body(t):
                    if t.has_before:
                        sp.wait_ge(sem("zs_ready"), t.i)
                        sp.wait_ge(sem("zs_k_ready"), t.i)
                    sp.dma_start(z_cur[:], z_dram[bass.ds(t.i * P + 1, P), 0:PA]).then_inc(sem("z_cur_loaded"), 16)
                    sp.dma_start(z_prev[:], z_dram[bass.ds(t.i * P, P), 0:PA]).then_inc(sem("z_prev_loaded"), 16)
                    if t.has_before:
                        sp.wait_ge(sem("mixed_b_ready"), t.i)
                    sp.dma_start(z_ret[:], z_dram[bass.ds(t.i * P + 1, P), PA:PIN]).then_inc(sem("z_ret_loaded"), 16)
                    sp.dma_start(rot[:], d["rotation"][bass.ds(t.i * P, P), :]).then_inc(sem("rot_loaded"), 16)
                    if isinstance(t.i, int) and t.i == 0:
                        sp.dma_start(h_in[PAD:P, :], d["meta_tokens"]).then_inc(sem("h_res_loaded"), 16)
                    else:
                        store(t.i)
                        sp.wait_ge(sem("router_done"), t.i)
                        sp.dma_start(h_in[:], d["x"][bass.ds((t.i - 1) * P, P), :]).then_inc(sem("h_res_loaded"), 16)
                run(sp, body)
                store(NT)
                sp.wait_ge(sem("h2_stored"), 16 * NT)
                sp.wait_ge(sem("u2_stored"), 16 * NT)

            @block.gpsimd
            def _(pool):
                for ap in (state[0], memory[0]):
                    pool.memset(ap[:], 0.0).then_inc(sem("states_zeroed"), 1)
                pool.wait_ge(sem("mu_loaded"), 16)

                def head_a_rstd(n):
                    pool.wait_ge(sem("head_a_rstd_in"), n)
                    pool.tensor_tensor(stat[:, 4, :], stat[:, 3, :], half[:, 0:HA], ALU.pow).then_inc(sem("head_a_rstd"), 1)

                def h2_rstd(n):
                    pool.wait_ge(sem("h2_rstd_in"), n)
                    pool.tensor_tensor(stat[:, 7, 1:2], stat[:, 7, 0:1], half[:, 0:1], ALU.pow).then_inc(sem("h2_rstd"), 1)

                def r_and_v(ap):
                    return ap[:, 0:4 * DA].rearrange("p (a c) -> p a c", c=2 * DA)[:, :, 0:DA]

                def body(t):
                    pool.wait_ge(sem("z_cur_loaded"), t.after * 16)
                    pool.wait_ge(sem("z_prev_loaded"), t.after * 16)
                    pool.tensor_tensor(z_prev[:], z_prev[:], z_cur[:], ALU.subtract).then_inc(sem("shift_diff"), 1)
                    pool.wait_ge(sem("shift_diff"), t.after)
                    pool.tensor_tensor(z_prev[:], z_prev[:], mu[:], ALU.mult).then_inc(sem("shift_scaled"), 1)
                    pool.wait_ge(sem("shift_scaled"), t.after)
                    if t.has_before:
                        pool.wait_ge(sem("y0_done"), t.i)
                        pool.wait_ge(sem("bonus_ready"), t.i)
                    pool.tensor_tensor(zs[:, 0:DA], z_prev[:, 0:DA], z_cur[:, 0:DA], ALU.add).then_inc(sem("zs_r_ready"), 1)
                    pool.tensor_tensor(v, z_prev[:, 2 * DA:3 * DA], z_cur[:, 2 * DA:3 * DA], ALU.add).then_inc(sem("zs_ready"), 1)
                    if t.has_before:
                        head_a_rstd(t.i)
                    pool.wait_ge(sem("kk_rnorm_in"), t.after)
                    pool.tensor_tensor(stat[:, 1, :], stat[:, 0, :], half[:, 0:HA], ALU.pow).then_inc(sem("kk_rnorm"), 1)
                    pool.wait_ge(sem("decay_c_ready"), t.after)
                    pool.wait_ge(sem("b_d_ready"), t.after)
                    pool.tensor_tensor(diag_c.rearrange("p c (q k) -> p c q k", k=C),
                                       all_pairs(cst("ident_c")),
                                       decay_c[:].rearrange("p (q c) -> p c q", c=2).unsqueeze(3).to_broadcast([P, 2, 4, C]),
                                       ALU.mult).then_inc(sem("diag_c_ready"), 1)
                    if t.has_before:
                        h2_rstd(t.i)
                    pool.wait_ge(sem("z_ret_loaded"), t.after * 16)
                    pool.wait_ge(sem("rot_loaded"), t.after * 16)
                    if t.has_before:
                        pool.wait_ge(sem("proj_done"), t.i)
                        pool.wait_ge(sem("u2_turned1"), t.i)
                        pool.wait_ge(sem("u2_stored"), t.i * 16)
                    zq = z_ret[:, 0:D].rearrange("p (h c) -> p h c", c=C)
                    halves = lambda ap: ap[:].rearrange("p (h a c) -> p h a c", a=2, c=C)
                    pool.tensor_tensor(z_cos[:].rearrange("p (h c) -> p h c", c=C), zq,
                                       rot[:, 0:C].unsqueeze(1).to_broadcast([P, 16, C]), ALU.mult
                                       ).then_inc(sem("rot_product"), 1)
                    pool.tensor_tensor(z_sin[:].rearrange("p (h c) -> p h c", c=C), zq,
                                       rot[:, C:2 * C].unsqueeze(1).to_broadcast([P, 16, C]), ALU.mult
                                       ).then_inc(sem("rot_product"), 1)
                    pool.wait_ge(sem("rot_product"), t.after * 2)
                    pool.tensor_tensor(halves(qk)[:, :, 0, :], halves(z_cos)[:, :, 0, :], halves(z_sin)[:, :, 1, :],
                                       ALU.subtract).then_inc(sem("rot_first"), 1)
                    pool.tensor_tensor(halves(qk)[:, :, 1, :], halves(z_sin)[:, :, 0, :], halves(z_cos)[:, :, 1, :],
                                       ALU.add).then_inc(sem("qk_ready"), 1)
                    pool.wait_ge(sem("rot_first"), t.after)
                    pool.wait_ge(sem("qk_ready"), t.after)
                    pool.tensor_tensor(heads(k_dec[:], HB), heads(qk[:, DB:D], HB), per_head(cst("k_decay"), HB), ALU.mult
                                       ).then_inc(sem("k_dec_ready"), 1)
                    pool.wait_ge(sem("head_b_rstd_in"), t.after)
                    pool.tensor_tensor(stat[:, 6, 0:HB], stat[:, 5, 0:HB], half[:, 0:HB], ALU.pow).then_inc(sem("head_b_rstd"), 1)
                run(pool, body)
                head_a_rstd(NT)
                h2_rstd(NT)

            @block.scalar
            def _(act):
                load = lambda dst, src: act.dma_start(dst, src).then_inc(sem("lora_up_loaded"), 16)
                act.dma_start(mu[:], d["shift_mu"].partition_broadcast(P)).then_inc(sem("mu_loaded"), 16)
                load(lora_up[0:C, :], d["decay_up"])
                load(lora_up[C:P, :], d["iclr_up"])
                load(gate_up[:], d["gate_up"])
                act.wait_ge(sem("consts_loaded"), 16)

                def mixed_t0(n):
                    act.wait_ge(sem("mixed_turned0"), n)
                    act.activation(mixed_t[:, 0:4, :], ps[:, 3, :], ACT.Copy).then_inc(sem("mixed_t0_ready"), 1)

                def mean_square(n):
                    act.wait_ge(sem("h2_ready"), n)
                    act.activation(z0[:].rearrange("p a c -> p (a c)"), h2[:], ACT.Square,
                                   scale=D ** -0.5, accum_out=stat[:, 7, 2:3]).then_inc(sem("h2_mean_square"), 1)

                def u2_t0(n):
                    act.wait_ge(sem("u2_turned0"), n)
                    act.activation(u2_t[:, 0:4, :], ps[:, 6, :], ACT.Copy).then_inc(sem("u2_t0_ready"), 1)

                def body(t):
                    act.wait_ge(sem("lora_turned"), t.after)
                    act.activation(lora_t[0:C, :], ps[0:C, 4, 0:P], ACT.Tanh).then_inc(sem("lora_tanh"), 1)
                    act.activation(lora_t[C:P, :], ps[C:P, 4, 0:P], ACT.Copy).then_inc(sem("lora_t_ready"), 1)
                    act.activation(gate_t[:], ps[:, 4, P:2 * P], ACT.Tanh, scale=0.5).then_inc(sem("gate_tanh"), 1)
                    act.wait_ge(sem("decay_in"), t.after)
                    act.activation(log_w[:], log_w[:], ACT.Tanh, scale=0.5).then_inc(sem("decay_tanh"), 1)
                    act.wait_ge(sem("iclr_in"), t.after)
                    act.activation(iclr[:], iclr[:], ACT.Tanh, scale=0.5).then_inc(sem("iclr_tanh"), 1)
                    if t.has_before:
                        mixed_t0(t.i)
                    act.wait_ge(sem("cum_in_done"), t.after)
                    act.activation(e_in[:], ps[:, 0, :], ACT.Exp).then_inc(sem("e_in_ready"), 1)
                    act.activation(e_neg[:], ps[:, 0, :], ACT.Exp, scale=-1.0).then_inc(sem("e_neg_ready"), 1)
                    act.wait_ge(sem("cum_ex_done"), t.after)
                    act.activation(e_ex[:], ps[:, 1, :], ACT.Exp).then_inc(sem("e_ex_ready"), 1)
                    act.wait_ge(sem("chunk_sum_done"), t.after)
                    act.activation(decay_c[:], ps[:, 2, 0:HA], ACT.Exp).then_inc(sem("decay_c_ready"), 1)
                    act.wait_ge(sem("after_done"), t.after)
                    act.activation(e_after[:], ps[:, 5, :], ACT.Exp).then_inc(sem("e_after_ready"), 1)
                    act.wait_ge(sem("gate_up_done"), t.after)
                    if t.has_before:
                        act.wait_ge(sem("mixed_a_ready"), t.i)
                    act.activation(gate[:], ps[:, 4, :], ACT.Copy).then_inc(sem("gate_ready"), 1)
                    act.wait_ge(sem("b_turned"), t.after)
                    act.activation(b_t[:], ps[:, 1, :], ACT.Copy).then_inc(sem("b_t_ready"), 1)
                    act.wait_ge(sem("k_turned"), t.after)
                    act.activation(k_t[:], ps[:, 2, :], ACT.Copy).then_inc(sem("k_t_ready"), 1)
                    if t.has_before:
                        mean_square(t.i)
                        u2_t0(t.i)
                    act.wait_ge(sem("l2_t_done"), t.after)
                    act.activation(l2_t[:], ps[:, 5, :], ACT.Copy).then_inc(sem("l2_t_ready"), 1)
                    act.wait_ge(sem("l4_done"), t.after)
                    act.wait_ge(sem("b_h_ready"), t.after)
                    act.activation(l4[:], ps[:, 0, :], ACT.Copy).then_inc(sem("l4_ready"), 1)
                    act.wait_ge(sem("l4_t_done"), t.after)
                    act.activation(l4_t[:], ps[:, 1, :], ACT.Copy).then_inc(sem("l4_t_ready"), 1)
                    act.wait_ge(sem("q_m_done"), t.after)
                    act.activation(q_m[:], ps[:, 5, :], ACT.Copy).then_inc(sem("q_m_ready"), 1)
                    act.wait_ge(sem("l8_done"), t.after)
                    act.activation(l8[:], ps[:, 3, :], ACT.Copy).then_inc(sem("l8_ready"), 1)
                    act.wait_ge(sem("z_ret_loaded"), t.after * 16)
                    act.activation(ret_gate[:], z_ret[:, 3 * DB:4 * DB], ACT.Tanh, scale=0.5).then_inc(sem("ret_tanh"), 1)
                    act.wait_ge(sem("q_turned"), t.after)
                    act.activation(q_t[:], ps[:, 6, :], ACT.Copy).then_inc(sem("q_t_ready"), 1)
                    act.wait_ge(sem("kr_turned"), t.after)
                    act.activation(kr_t[:], ps[:, 7, :], ACT.Copy).then_inc(sem("kr_t_ready"), 1)
                    act.wait_ge(sem("x_t_done"), t.after)
                    act.activation(x_t[:], ps[:, 0, :], ACT.Copy).then_inc(sem("x_t_ready"), 1)
                    act.wait_ge(sem("z0_a_done"), t.after)
                    act.activation(z0[:, 0, :], ps[:, 4, :], ACT.Copy).then_inc(sem("z0_a_ready"), 1)
                    act.wait_ge(sem("x2_t_done"), t.after)
                    act.activation(x2_t[:], ps[:, 2, :], ACT.Copy).then_inc(sem("x2_t_ready"), 1)
                    act.wait_ge(sem("inner_done"), t.after)
                    act.activation(in_s[:], ps[:, 6, :], ACT.Copy).then_inc(sem("in_s_ready"), 1)
                    act.wait_ge(sem("y_keys_done"), t.after)
                    act.activation(y[:], ps[:, 6, :], ACT.Copy).then_inc(sem("y_keys_ready"), 1)
                    act.wait_ge(sem("n_m_done"), t.after)
                    act.activation(n_m[:], ps[:, 0:2, 0:256], ACT.Copy).then_inc(sem("n_m_ready"), 1)
                    act.wait_ge(sem("mixed_turned1"), t.after)
                    act.activation(mixed_t[:, 4:8, :], ps[:, 7, :], ACT.Copy).then_inc(sem("mixed_t1_ready"), 1)
                run(act, body)
                mixed_t0(NT)
                mean_square(NT)
                u2_t0(NT)

            @block.vector
            def _(dve):
                dve.memset(h_in[:], 0.0).then_inc(sem("h_res_zeroed"), 1)
                dve.wait_ge(sem("states_zeroed"), 2)

                OWN, OWN_END = 30, 8

                def centre(y_, n, tmp_, mean, var, done):
                    w = DA // n
                    done(dve.tensor_reduce(mean, heads(y_[:], n), X, ALU.add))
                    done(dve.tensor_scalar(mean, mean, 1.0 / w, None, ALU.mult, ALU.bypass))
                    done(dve.tensor_tensor(heads(y_[:], n), heads(y_[:], n), per_head(mean, n), ALU.subtract))
                    done(dve.tensor_tensor(tmp_[:], y_[:], y_[:], ALU.mult))
                    done(dve.tensor_reduce(var, heads(tmp_[:], n), X, ALU.add))

                def end_steps(n):
                    n_own = [0]

                    def own(ins):
                        n_own[0] += 1
                        ins.then_inc(sem("dve_end"), 1)
                        dve.wait_ge(sem("dve_end"), (n - 1) * OWN_END + n_own[0])

                    def centre_a():
                        dve.wait_ge(sem("y0_done"), n)
                        dve.wait_ge(sem("y_keys_ready"), n)
                        dve.tensor_tensor(y[:], y[:], ps[:, 0, :], ALU.add).then_inc(sem("y0_ready"), 1)
                        dve.wait_ge(sem("y0_ready"), n)
                        dve.wait_ge(sem("y1_done"), n)
                        own(dve.tensor_tensor(parity(y[:]), parity(y[:]), bank_pair(2), ALU.add))
                        dve.wait_ge(sem("s2_done"), n)
                        dve.tensor_tensor(state[0][:], n_m[:, 1, :], ps[:, 5, 0:256], ALU.add).then_inc(sem("state0_ready"), 1)
                        centre(y, HA, tmp, stat[:, 2, :], stat[:, 3, :], own)
                        dve.tensor_scalar(stat[:, 3, :], stat[:, 3, :], 1.0 / HEAD_A, 64e-5, ALU.mult, ALU.add
                                          ).then_inc(sem("head_a_rstd_in"), 1)

                    def gate_a():
                        dve.wait_ge(sem("head_a_rstd"), n)
                        own(dve.tensor_tensor(heads(y[:]), heads(y[:]), per_head(stat[:, 4, :]), ALU.mult))
                        own(dve.tensor_tensor(y[:], y[:], gate[:], ALU.mult))
                        dve.tensor_tensor(y[:], y[:], bonus[:], ALU.add).then_inc(sem("mixed_a_ready"), 1)

                    def residual():
                        dve.wait_ge(sem("h_res_loaded"), n * 16)
                        dve.wait_ge(sem("proj_done"), n)
                        dve.tensor_tensor(h2[:], h_in[:], ps[:, 6:8, :].rearrange("p a c -> p (a c)"), ALU.add).then_inc(sem("h2_ready"), 1)

                    def mean_eps():
                        dve.wait_ge(sem("h2_mean_square"), n)
                        dve.tensor_scalar(stat[:, 7, 0:1], stat[:, 7, 2:3], 1e-6, None, ALU.add, ALU.bypass).then_inc(sem("h2_rstd_in"), 1)

                    def norm():
                        dve.wait_ge(sem("h2_ready"), n)
                        dve.wait_ge(sem("h2_rstd"), n)
                        dve.scalar_tensor_tensor(u2[:], h2[:], stat[:, 7, 1:2], gain[:], ALU.mult, ALU.mult).then_inc(sem("u2_ready"), 1)

                    def u2_t1():
                        dve.wait_ge(sem("u2_turned1"), n)
                        dve.tensor_copy(u2_t[:, 4:8, :], ps[:, 7, :]).then_inc(sem("u2_t1_ready"), 1)

                    def logits_of():
                        dve.wait_ge(sem("router_done"), n)
                        dve.tensor_tensor(logits[:, bass.ds(n - 1, 1), :].rearrange("p a c -> p (a c)"), ps[:, 6, 0:NR],
                                          router_b[:], ALU.add).then_inc(sem("logits_ready"), 1)
                        assert n_own[0] == OWN_END, n_own[0]
                    return centre_a, gate_a, residual, mean_eps, norm, u2_t1, logits_of

                def body(t):
                    n_own = [0]

                    def own(ins):
                        n_own[0] += 1
                        ins.then_inc(sem("dve_own"), 1)
                        dve.wait_ge(sem("dve_own"), t.i * OWN + n_own[0])

                    if t.has_before:
                        centre_a, gate_a, residual, mean_eps, norm, u2_t1, logits_of = end_steps(t.i)
                    dve.wait_ge(sem("shift_scaled"), t.after)
                    if t.has_before:
                        dve.wait_ge(sem("y0_done"), t.i)
                    dve.tensor_tensor(zs[:, 3 * DA:PA], z_prev[:, 3 * DA:PA], z_cur[:, 3 * DA:PA], ALU.add).then_inc(sem("zs_lora_ready"), 1)
                    dve.tensor_tensor(k, z_prev[:, DA:2 * DA], z_cur[:, DA:2 * DA], ALU.add).then_inc(sem("zs_k_ready"), 1)
                    if t.has_before:
                        centre_a()
                    dve.wait_ge(sem("gate_tanh"), t.after)
                    dve.tensor_scalar(gate_t[:], gate_t[:], 0.5, 0.5, ALU.mult, ALU.add).then_inc(sem("gate_t_ready"), 1)
                    dve.wait_ge(sem("decay_up_done"), t.after)
                    dve.tensor_tensor(log_w[:], ps[:, 0, :], rows["decay_w0"], ALU.add).then_inc(sem("decay_in"), 1)
                    dve.wait_ge(sem("iclr_up_done"), t.after)
                    dve.tensor_tensor(iclr[:], ps[:, 1, :], rows["iclr_a0"], ALU.add).then_inc(sem("iclr_in"), 1)
                    if t.has_before:
                        gate_a()
                    dve.wait_ge(sem("zs_k_ready"), t.after)
                    own(dve.tensor_tensor(kk[:], k, rows["k_k"], ALU.mult))
                    dve.wait_ge(sem("decay_tanh"), t.after)
                    dve.tensor_scalar(log_w[:], log_w[:], -0.5 * DECAY, -0.5 * DECAY, ALU.mult, ALU.add).then_inc(sem("log_w_ready"), 1)
                    own(dve.tensor_tensor(tmp[:], kk[:], kk[:], ALU.mult))
                    own(dve.tensor_reduce(stat[:, 0, :], heads(tmp[:]), X, ALU.add))
                    dve.tensor_scalar(stat[:, 0, :], stat[:, 0, :], 1e-24, None, ALU.max, ALU.bypass).then_inc(sem("kk_rnorm_in"), 1)
                    dve.wait_ge(sem("iclr_tanh"), t.after)
                    own(dve.tensor_scalar(iclr[:], iclr[:], 0.5, 0.5, ALU.mult, ALU.add))
                    own(dve.scalar_tensor_tensor(k2[:], iclr[:], -1.0, rows["k_a"], ALU.add, ALU.mult))
                    own(dve.scalar_tensor_tensor(k2[:], k2[:], 1.0, k, ALU.add, ALU.mult))
                    dve.wait_ge(sem("kk_rnorm"), t.after)
                    own(dve.tensor_tensor(heads(kk[:]), heads(kk[:]), per_head(stat[:, 1, :]), ALU.mult))
                    dve.wait_ge(sem("e_ex_ready"), t.after)
                    dve.scalar_tensor_tensor(a_d[:], kk[:], -1.0, e_ex[:], ALU.mult, ALU.mult).then_inc(sem("a_d_ready"), 1)
                    own(dve.tensor_tensor(b_row[:], kk[:], iclr[:], ALU.mult))
                    dve.wait_ge(sem("e_neg_ready"), t.after)
                    dve.tensor_tensor(b_d[:], b_row[:], e_neg[:], ALU.mult).then_inc(sem("b_d_ready"), 1)
                    dve.tensor_tensor(k_d[:], k2[:], e_neg[:], ALU.mult).then_inc(sem("k_d_ready"), 1)
                    dve.wait_ge(sem("e_in_ready"), t.after)
                    dve.wait_ge(sem("zs_r_ready"), t.after)
                    dve.tensor_tensor(r_d[:], r, e_in[:], ALU.mult).then_inc(sem("r_d_ready"), 1)
                    dve.wait_ge(sem("a_turned"), t.after)
                    dve.tensor_copy(a_t[:], ps[:, 0, :]).then_inc(sem("a_t_ready"), 1)
                    dve.wait_ge(sem("r_turned"), t.after)
                    dve.tensor_copy(r_t[:], ps[:, 3, :]).then_inc(sem("r_t_ready"), 1)
                    if t.has_before:
                        residual()
                        mean_eps()
                    dve.wait_ge(sem("g_ab_done"), t.after)
                    dve.tensor_tensor(parity(ld_t[:]), bank_pair(4), all_pairs(cst("lt_sub")), ALU.mult).then_inc(sem("ld_t_ready"), 1)
                    dve.tensor_tensor(parity(ld[:]), bank_pair(4, 256), all_pairs(cst("gt_sub")), ALU.mult).then_inc(sem("ld_ready"), 1)
                    dve.tensor_tensor(parity(lo[:]), bank_pair(4, 256), all_pairs(cst("gt_off")), ALU.mult).then_inc(sem("lo_ready"), 1)
                    if t.has_before:
                        norm()
                    dve.wait_ge(sem("g_ak_done"), t.after)
                    own(dve.tensor_tensor(parity(ak_t[:]), bank_pair(0), all_pairs(cst("lt")), ALU.mult))
                    dve.tensor_tensor(parity(rb_t[:]), bank_pair(0, 256), all_pairs(cst("le")), ALU.mult).then_inc(sem("rb_t_ready"), 1)
                    dve.wait_ge(sem("g_rk_done"), t.after)
                    dve.tensor_tensor(parity(rk_t[:]), bank_pair(2), all_pairs(cst("le")), ALU.mult).then_inc(sem("rk_t_ready"), 1)
                    if t.has_before:
                        u2_t1()
                    dve.wait_ge(sem("e_after_ready"), t.after)
                    if t.has_before:
                        dve.wait_ge(sem("u2_ready"), t.i)
                        dve.wait_ge(sem("h2_stored"), t.i * 16)
                    dve.tensor_tensor(k_h[:], k2[:], e_after[:], ALU.mult).then_inc(sem("k_h_ready"), 1)
                    dve.tensor_tensor(b_h[:], b_row[:], e_after[:], ALU.mult).then_inc(sem("b_h_ready"), 1)
                    dve.wait_ge(sem("l2_done"), t.after)
                    dve.tensor_copy(l2[:], ps[:, 4, :]).then_inc(sem("l2_ready"), 1)
                    dve.wait_ge(sem("ld_t_ready"), t.after)
                    own(dve.tensor_tensor(heads(inv[:]), heads(ld_t[:]), all_heads(cst("ident_c")), ALU.add))
                    dve.wait_ge(sem("l2_t_ready"), t.after)
                    own(dve.tensor_tensor(inv[:], inv[:], l2_t[:], ALU.add))
                    if t.has_before:
                        logits_of()
                    dve.wait_ge(sem("l3_t_done"), t.after)
                    dve.tensor_tensor(inv[:], inv[:], ps[:, 2, :], ALU.add).then_inc(sem("inv_3"), 1)
                    dve.wait_ge(sem("zs_ready"), t.after)
                    own(dve.tensor_tensor(tmp[:], r, k2[:], ALU.mult))
                    own(dve.tensor_tensor(tmp[:], tmp[:], rows["r_k"], ALU.mult))
                    own(dve.tensor_reduce(stat[:, 8, :], heads(tmp[:]), X, ALU.add))
                    own(dve.tensor_tensor(heads(bonus[:]), heads(v), per_head(stat[:, 8, :]), ALU.mult))
                    dve.wait_ge(sem("inv_3"), t.after)
                    dve.wait_ge(sem("inv4_done"), t.after)
                    dve.tensor_tensor(inv[:], inv[:], ps[:, 4, :], ALU.add).then_inc(sem("inv_4"), 1)
                    own(dve.tensor_tensor(bonus[:], bonus[:], rows["ln_b_a"], ALU.add))
                    dve.wait_ge(sem("gate_ready"), t.after)
                    dve.tensor_tensor(bonus[:], bonus[:], gate[:], ALU.mult).then_inc(sem("bonus_ready"), 1)
                    dve.wait_ge(sem("inv_4"), t.after)
                    dve.wait_ge(sem("inv8_done"), t.after)
                    dve.tensor_tensor(inv[:], inv[:], ps[:, 5, :], ALU.add).then_inc(sem("inv_ready"), 1)
                    dve.wait_ge(sem("bonus_ready"), t.after)
                    own(dve.tensor_tensor(gate[:], gate[:], rows["ln_w_a"], ALU.mult))
                    own(dve.tensor_tensor(heads(memory_d[:], HB), heads(memory[0][:], HB), per_head(cst("r_decay"), HB), ALU.mult))
                    dve.wait_ge(sem("scores_done"), t.after)
                    dve.tensor_tensor(s_t[:], ps[:, 6, 0:HB * C], cst("ret_mask"), ALU.mult).then_inc(sem("s_t_ready"), 1)
                    dve.wait_ge(sem("kv0_done"), t.after)
                    dve.tensor_tensor(memory[1][:], memory_d[:], ps[:, 7, :], ALU.add).then_inc(sem("memory1_ready"), 1)
                    dve.wait_ge(sem("x_m_done"), t.after)
                    dve.tensor_copy(x_m[:], ps[:, 1, :]).then_inc(sem("x_m_ready"), 1)
                    dve.wait_ge(sem("z0_q_done"), t.after)
                    dve.tensor_copy(z0[:, 1, :], ps[:, 5, :]).then_inc(sem("z0_q_ready"), 1)
                    dve.wait_ge(sem("x_t_ready"), t.after)
                    dve.wait_ge(sem("x2_t_ready"), t.after)
                    own(dve.tensor_tensor(x_p[:], x_t[:], x2_t[:], ALU.add))
                    dve.wait_ge(sem("memory1_ready"), t.after)
                    own(dve.tensor_tensor(heads(memory_d[:], HB), heads(memory[1][:], HB), per_head(cst("r_decay"), HB), ALU.mult))
                    dve.wait_ge(sem("x3_t_done"), t.after)
                    dve.tensor_tensor(x_p[:], x_p[:], ps[:, 3, :], ALU.add).then_inc(sem("x_p_ready"), 1)
                    dve.wait_ge(sem("cross_done"), t.after)
                    own(dve.tensor_tensor(heads(ret_tmp[:], HB), heads(ps[:, 7, :], HB), per_head(cst("q_decay"), HB), ALU.mult))
                    dve.wait_ge(sem("in_s_ready"), t.after)
                    own(dve.tensor_tensor(y_ret[:], ret_tmp[:], in_s[:], ALU.add))
                    dve.wait_ge(sem("kv1_done"), t.after)
                    dve.tensor_tensor(memory[0][:], memory_d[:], ps[:, 6, :], ALU.add).then_inc(sem("memory0_ready"), 1)
                    centre(y_ret, HB, ret_tmp, stat[:, 9, 0:HB], stat[:, 5, 0:HB], own)
                    dve.tensor_scalar(stat[:, 5, 0:HB], stat[:, 5, 0:HB], 1.0 / HEAD_B, 1e-5, ALU.mult, ALU.add
                                      ).then_inc(sem("head_b_rstd_in"), 1)
                    dve.wait_ge(sem("z0_a_ready"), t.after)
                    dve.wait_ge(sem("z0_q_ready"), t.after)
                    dve.wait_ge(sem("w_done"), t.after)
                    dve.tensor_tensor(w_m[:], z0[:], ps[:, 0:2, :], ALU.add).then_inc(sem("w_m_ready"), 1)
                    dve.wait_ge(sem("head_b_rstd"), t.after)
                    own(dve.tensor_tensor(heads(y_ret[:], HB), heads(y_ret[:], HB), per_head(stat[:, 6, 0:HB], HB), ALU.mult))
                    own(dve.tensor_tensor(y_ret[:], y_ret[:], rows["gn_w_b"], ALU.mult))
                    dve.wait_ge(sem("m_t_done"), t.after)
                    dve.wait_ge(sem("diag_c_ready"), t.after)
                    dve.tensor_tensor(m_t[:], diag_c, ps[:, 4:6, 0:256], ALU.add).then_inc(sem("m_t_ready"), 1)
                    dve.wait_ge(sem("ret_tanh"), t.after)
                    own(dve.scalar_tensor_tensor(ret_gate[:], ret_gate[:], 1.0, z_ret[:, 3 * DB:4 * DB], ALU.add, ALU.mult))
                    dve.scalar_tensor_tensor(y_ret[:], ret_gate[:], 0.5, y_ret[:], ALU.mult, ALU.mult).then_inc(sem("mixed_b_ready"), 1)
                    dve.wait_ge(sem("rz_done"), t.after)
                    dve.tensor_tensor(rz_t[:].rearrange("p (q c k) -> p c q k", c=2, k=C), r_t[:].rearrange("p (q c k) -> p c q k", c=2, k=C), ps[:, 2:4, 0:256].rearrange("p c (q k) -> p c q k", k=C), ALU.add).then_inc(sem("rz_t_ready"), 1)
                    dve.wait_ge(sem("s1_done"), t.after)
                    dve.wait_ge(sem("n_m_ready"), t.after)
                    dve.tensor_tensor(state[1][:], n_m[:, 0, :], ps[:, 4, 0:256], ALU.add).then_inc(sem("state1_ready"), 1)
                    assert n_own[0] == OWN, n_own[0]
                run(dve, body)
                for step in end_steps(NT):
                    step()

            @block.tensor
            def _(pe):
                pe.wait_ge(sem("lora_up_loaded"), 16 * 3)

                def turn4(bank, src):
                    for j in range(4):
                        tr = pe.transpose(ps[:, bank, j * P:(j + 1) * P], src[:, j * P:(j + 1) * P], ident)
                    return tr

                def full(bank, lhs, rhs):
                    return pe.matmul(ps[:, bank, :], lhs, rhs, start=True, stop=True)

                def chunks(bank, pairs):
                    for h in range(HA):
                        for c in range(2):
                            p_ = slice(c * C, (c + 1) * C)
                            f = slice(h * C, (h + 1) * C)
                            for n, (lhs, rhs) in enumerate(pairs):
                                mm = pe.matmul(ps[p_, bank, f], lhs[p_, f], rhs[p_, f],
                                               start=(n == 0), stop=(n == len(pairs) - 1))
                    return mm

                def cross(banks, at_, lhs, rhs):
                    for a in range(2):
                        for q in range(4):
                            for c in range(2):
                                f = slice(q * P + c * C, q * P + (c + 1) * C)
                                mm = pe.matmul(ps[c * C:(c + 1) * C, banks + a, at_ + q * C:at_ + (q + 1) * C],
                                               lhs[a * C:(a + 1) * C, f], rhs[a * C:(a + 1) * C, f], start=True, stop=True)
                    return mm

                def to_features(banks, pairs):
                    for c in range(2):
                        p_ = slice(c * C, (c + 1) * C)
                        for h in range(HA):
                            a, q = h % 2, h // 2
                            f = slice(h * C, (h + 1) * C)
                            for n, (lhs, rhs) in enumerate(pairs):
                                mm = pe.matmul(ps[a * C:(a + 1) * C, banks + c, q * C:(q + 1) * C], lhs[p_, f], rhs[p_, f],
                                               start=(n == 0), stop=(n == len(pairs) - 1))
                    return mm

                def advance(bank, m, st):
                    for a in range(2):
                        p_ = slice(a * C, (a + 1) * C)
                        for q in range(4):
                            f = slice(q * C, (q + 1) * C)
                            mm = pe.matmul(ps[p_, bank, f], m[p_, f], st[p_, f], start=True, stop=True)
                    return mm

                def project_out(n, ks):
                    for k_ in ks:
                        mm = pe.matmul(ps[:, 6 + n, :], mixed_t[:, k_, :], w_out[:, k_, n * 512:(n + 1) * 512],
                                       start=(k_ == 4), stop=(k_ == 3))
                    return mm

                def end_steps(n, lead):
                    def retention_rows(cols, ks):
                        lead()
                        pe.wait_ge(sem("mixed_t1_ready"), n)
                        pe.wait_ge(sem("memory0_ready"), n)
                        pe.wait_ge(sem("y_keys_ready"), n)
                        project_out(cols, ks)

                    def turn_rwkv_rows():
                        lead()
                        pe.wait_ge(sem("mixed_a_ready"), n)
                        turn4(3, y).then_inc(sem("mixed_turned0"), 1)

                    def rwkv_rows():
                        lead()
                        pe.wait_ge(sem("mixed_t0_ready"), n)
                        project_out(0, range(4))
                        project_out(1, range(4)).then_inc(sem("proj_done"), 1)

                    def turn_u2():
                        lead()
                        pe.wait_ge(sem("u2_ready"), n)
                        turn4(6, u2[:, 0:512]).then_inc(sem("u2_turned0"), 1)
                        turn4(7, u2[:, 512:D]).then_inc(sem("u2_turned1"), 1)

                    def route():
                        lead()
                        pe.wait_ge(sem("u2_t0_ready"), n)
                        pe.wait_ge(sem("u2_t1_ready"), n)
                        for k_ in range(KD):
                            mm = pe.matmul(ps[:, 6, 0:NR], u2_t[:, k_, :], router_w[:, k_, :], start=(k_ == 0), stop=(k_ == KD - 1))
                        mm.then_inc(sem("router_done"), 1)
                    return retention_rows, turn_rwkv_rows, rwkv_rows, turn_u2, route

                def body(t):
                    if t.has_before:
                        retention_rows, turn_rwkv_rows, rwkv_rows, turn_u2, route = end_steps(t.i, lambda: t.lead(pe))
                    t.lead(pe)
                    pe.wait_ge(sem("zs_lora_ready"), t.after)
                    pe.transpose(ps[:, 4, 0:P], zs[:, 3 * DA:3 * DA + P], ident)
                    pe.transpose(ps[:, 4, P:2 * P], zs[:, 3 * DA + P:3 * DA + 2 * P], ident).then_inc(sem("lora_turned"), 1)
                    if t.has_before:
                        retention_rows(0, range(4, 5))
                    t.lead(pe)
                    pe.wait_ge(sem("lora_tanh"), t.after)
                    pe.wait_ge(sem("lora_t_ready"), t.after)
                    if t.has_before:
                        pe.wait_ge(sem("y0_ready"), t.i)
                    full(0, lora_t[0:C, :], lora_up[0:C, :]).then_inc(sem("decay_up_done"), 1)
                    full(1, lora_t[C:P, :], lora_up[C:P, :]).then_inc(sem("iclr_up_done"), 1)
                    if t.has_before:
                        retention_rows(0, range(5, 8))
                    t.lead(pe)
                    pe.wait_ge(sem("gate_t_ready"), t.after)
                    full(4, gate_t[:], gate_up[:]).then_inc(sem("gate_up_done"), 1)
                    if t.has_before:
                        retention_rows(1, range(4, 5))
                        turn_rwkv_rows()
                        retention_rows(1, range(5, 6))
                    t.lead(pe)
                    pe.wait_ge(sem("log_w_ready"), t.after)
                    pe.wait_ge(sem("iclr_in"), t.after)
                    full(0, cst("cum_in"), log_w[:]).then_inc(sem("cum_in_done"), 1)
                    full(1, cst("cum_ex"), log_w[:]).then_inc(sem("cum_ex_done"), 1)
                    for q in range(4):
                        mm = pe.matmul(ps[:, 2, 2 * q:2 * q + 2], log_w[:, q * P:(q + 1) * P], cst("chunk_of"),
                                       start=True, stop=True)
                    mm.then_inc(sem("chunk_sum_done"), 1)
                    full(5, cst("after"), log_w[:]).then_inc(sem("after_done"), 1)
                    if t.has_before:
                        retention_rows(1, range(6, 8))
                        t.lead(pe)
                        pe.wait_ge(sem("mixed_t0_ready"), t.i)
                    t.lead(pe)
                    pe.wait_ge(sem("a_d_ready"), t.after)
                    pe.wait_ge(sem("e_neg_ready"), t.after)
                    turn4(0, a_d).then_inc(sem("a_turned"), 1)
                    t.lead(pe)
                    pe.wait_ge(sem("b_d_ready"), t.after)
                    pe.wait_ge(sem("e_ex_ready"), t.after)
                    turn4(1, b_d).then_inc(sem("b_turned"), 1)
                    t.lead(pe)
                    pe.wait_ge(sem("k_d_ready"), t.after)
                    pe.wait_ge(sem("decay_c_ready"), t.after)
                    turn4(2, k_d).then_inc(sem("k_turned"), 1)
                    t.lead(pe)
                    pe.wait_ge(sem("r_d_ready"), t.after)
                    turn4(3, r_d).then_inc(sem("r_turned"), 1)
                    if t.has_before:
                        rwkv_rows()
                    t.lead(pe)
                    pe.wait_ge(sem("b_t_ready"), t.after)
                    pe.wait_ge(sem("a_t_ready"), t.after)
                    pe.wait_ge(sem("gate_ready"), t.after)
                    pe.wait_ge(sem("e_after_ready"), t.after)
                    cross(4, 0, b_t, a_t)
                    cross(4, 256, a_t, b_t).then_inc(sem("g_ab_done"), 1)
                    t.lead(pe)
                    pe.wait_ge(sem("k_t_ready"), t.after)
                    pe.wait_ge(sem("r_t_ready"), t.after)
                    cross(0, 0, k_t, a_t)
                    cross(0, 256, b_t, r_t).then_inc(sem("g_ak_done"), 1)
                    cross(2, 0, k_t, r_t).then_inc(sem("g_rk_done"), 1)
                    if t.has_before:
                        turn_u2()
                    t.lead(pe)
                    pe.wait_ge(sem("ld_t_ready"), t.after)
                    pe.wait_ge(sem("ld_ready"), t.after)
                    pe.wait_ge(sem("lo_ready"), t.after)
                    chunks(4, [(ld_t, ld)]).then_inc(sem("l2_done"), 1)
                    chunks(5, [(ld, ld_t)]).then_inc(sem("l2_t_done"), 1)
                    if t.has_before:
                        route()
                    t.lead(pe)
                    pe.wait_ge(sem("l2_ready"), t.after)
                    pe.wait_ge(sem("l2_t_ready"), t.after)
                    pe.wait_ge(sem("rb_t_ready"), t.after)
                    pe.wait_ge(sem("rk_t_ready"), t.after)
                    chunks(0, [(l2_t, l2)]).then_inc(sem("l4_done"), 1)
                    chunks(1, [(l2, l2_t)]).then_inc(sem("l4_t_done"), 1)
                    chunks(2, [(l2, ld_t)]).then_inc(sem("l3_t_done"), 1)
                    t.lead(pe)
                    pe.wait_ge(sem("zs_ready"), t.after)
                    chunks(5, [(ak_t, v)]).then_inc(sem("q_m_done"), 1)
                    t.lead(pe)
                    pe.wait_ge(sem("l4_ready"), t.after)
                    pe.wait_ge(sem("l4_t_ready"), t.after)
                    chunks(3, [(l4_t, l4)]).then_inc(sem("l8_done"), 1)
                    t.lead(pe)
                    pe.wait_ge(sem("inv_3"), t.after)
                    chunks(4, [(l4, inv)]).then_inc(sem("inv4_done"), 1)
                    if t.has_before:
                        t.lead(pe)
                        pe.wait_ge(sem("logits_ready"), t.i)
                    t.lead(pe)
                    pe.wait_ge(sem("qk_ready"), t.after)
                    turn4(6, qk[:, 0:DB]).then_inc(sem("q_turned"), 1)
                    turn4(7, qk[:, DB:D]).then_inc(sem("kr_turned"), 1)
                    t.lead(pe)
                    pe.wait_ge(sem("inv_4"), t.after)
                    pe.wait_ge(sem("l8_ready"), t.after)
                    pe.wait_ge(sem("q_m_ready"), t.after)
                    chunks(5, [(l8, inv)]).then_inc(sem("inv8_done"), 1)
                    t.lead(pe)
                    pe.wait_ge(sem("q_t_ready"), t.after)
                    pe.wait_ge(sem("kr_t_ready"), t.after)
                    pe.wait_ge(sem("k_dec_ready"), t.after)

                    def key_values(bank, c):
                        p_ = slice(c * C, (c + 1) * C)
                        for h in range(HB):
                            mm = pe.matmul(ps[:, bank, h * P:(h + 1) * P], k_dec[p_, h * P:(h + 1) * P],
                                           z_ret[p_, 2 * DB + h * P:2 * DB + (h + 1) * P], start=True, stop=True)
                        return mm
                    for c in range(2):
                        for h in range(HB):
                            f = slice(h * P + c * C, h * P + (c + 1) * C)
                            mm = pe.matmul(ps[c * C:(c + 1) * C, 6, h * C:(h + 1) * C], kr_t[:, f], q_t[:, f], start=True, stop=True)
                    mm.then_inc(sem("scores_done"), 1)
                    key_values(7, 0).then_inc(sem("kv0_done"), 1)
                    t.lead(pe)
                    pe.wait_ge(sem("inv_ready"), t.after)
                    chunks(0, [(lo, inv)]).then_inc(sem("x_t_done"), 1)
                    chunks(1, [(inv, lo)]).then_inc(sem("x_m_done"), 1)
                    chunks(4, [(inv, a_d)]).then_inc(sem("z0_a_done"), 1)
                    chunks(5, [(inv, q_m)]).then_inc(sem("z0_q_done"), 1)
                    t.lead(pe)
                    pe.wait_ge(sem("x_m_ready"), t.after)
                    pe.wait_ge(sem("x_t_ready"), t.after)
                    chunks(2, [(x_m, x_t)]).then_inc(sem("x2_t_done"), 1)
                    t.lead(pe)
                    pe.wait_ge(sem("s_t_ready"), t.after)
                    for c in range(2):
                        p_ = slice(c * C, (c + 1) * C)
                        for h in range(HB):
                            mm = pe.matmul(ps[p_, 6, h * P:(h + 1) * P], s_t[p_, h * C:(h + 1) * C],
                                           z_ret[p_, 2 * DB + h * P:2 * DB + (h + 1) * P], start=True, stop=True)
                    mm.then_inc(sem("inner_done"), 1)
                    t.lead(pe)
                    pe.wait_ge(sem("x2_t_ready"), t.after)
                    chunks(3, [(x_m, x2_t)]).then_inc(sem("x3_t_done"), 1)
                    t.lead(pe)
                    pe.wait_ge(sem("memory1_ready"), t.after)
                    for c in range(2):
                        for h in range(HB):
                            mm = pe.matmul(ps[c * C:(c + 1) * C, 7, h * P:(h + 1) * P], q_t[:, h * P + c * C:h * P + (c + 1) * C],
                                           memory[c][:, h * P:(h + 1) * P], start=True, stop=True)
                    mm.then_inc(sem("cross_done"), 1)
                    t.lead(pe)
                    pe.wait_ge(sem("in_s_ready"), t.after)
                    key_values(6, 1).then_inc(sem("kv1_done"), 1)
                    t.lead(pe)
                    pe.wait_ge(sem("x_p_ready"), t.after)
                    pe.wait_ge(sem("z0_a_ready"), t.after)
                    pe.wait_ge(sem("z0_q_ready"), t.after)
                    chunks(0, [(x_p, z0[:, 0, :])])
                    chunks(1, [(x_p, z0[:, 1, :])]).then_inc(sem("w_done"), 1)
                    t.lead(pe)
                    pe.wait_ge(sem("memory0_ready"), t.after)
                    chunks(6, [(rk_t, v)]).then_inc(sem("y_keys_done"), 1)
                    t.lead(pe)
                    pe.wait_ge(sem("w_m_ready"), t.after)
                    pe.wait_ge(sem("k_h_ready"), t.after)
                    pe.wait_ge(sem("b_h_ready"), t.after)
                    wa, wq = w_m[:, 0, :], w_m[:, 1, :]
                    to_features(4, [(wa, b_h)]).then_inc(sem("m_t_done"), 1)
                    to_features(0, [(b_h, wq), (k_h, v)]).then_inc(sem("n_m_done"), 1)
                    to_features(2, [(wa, rb_t)]).then_inc(sem("rz_done"), 1)
                    t.lead(pe)
                    pe.wait_ge(sem("m_t_ready"), t.after)
                    if t.has_before:
                        pe.wait_ge(sem("state0_ready"), t.i)
                    advance(4, m_t[:, 0, :], state[0]).then_inc(sem("s1_done"), 1)
                    t.lead(pe)
                    pe.wait_ge(sem("mixed_b_ready"), t.after)
                    pe.wait_ge(sem("n_m_ready"), t.after)
                    turn4(7, y_ret).then_inc(sem("mixed_turned1"), 1)
                    chunks(0, [(rb_t, wq)]).then_inc(sem("y0_done"), 1)
                    t.lead(pe)
                    pe.wait_ge(sem("state1_ready"), t.after)
                    pe.wait_ge(sem("rz_t_ready"), t.after)
                    advance(5, m_t[:, 1, :], state[1]).then_inc(sem("s2_done"), 1)
                    for a in range(2):
                        p_ = slice(a * C, (a + 1) * C)
                        for q in range(4):
                            for c in range(2):
                                mm = pe.matmul(ps[c * C:(c + 1) * C, 2 + a, q * C:(q + 1) * C],
                                               rz_t[p_, q * P + c * C:q * P + (c + 1) * C],
                                               state[c][p_, q * C:(q + 1) * C], start=True, stop=True)
                    mm.then_inc(sem("y1_done"), 1)
                run(pe, body)
                retention_rows, turn_rwkv_rows, rwkv_rows, turn_u2, route = end_steps(NT, lambda: None)
                retention_rows(0, range(4, 8))
                retention_rows(1, range(4, 8))
                turn_rwkv_rows()
                rwkv_rows()
                turn_u2()
                route()


def dispatch_and_experts(nc, d, out, env):
    sem, tile, ps, ident, cst = (env[k] for k in ("sem", "tile", "ps", "ident", "cst"))
    two_names = env["two_names"]
    h2_dram, u2_dram, y_dram, slot_row_dram, half, logits, free_sems = (
        env[k] for k in ("h2_dram", "u2_dram", "y_dram", "slot_row_dram", "half", "logits", "free_sems"))
    NTR = NT - 1
    BIG = 1e30
    with ExitStack() as outer:
        slots = tile(outer, "slots", [P, 2, NTR], I32)
        weight = tile(outer, "weight", [P, 2, NTR])
        slot_row = tile(outer, "slot_row", [P, NBLK], I32)
        extra = tile(outer, "extra", [1, 1 + EXTRA], I32)

        rows_at = -(-nc.sbuf_base // 32) * 32
        gate_lo, gate_raw = zip(*(two_names(outer, f"gate_lo{b}", [P, KD, DE], F32R, f"gate_raw{b}", [P, KD, DE]) for b in range(2)))
        up_lo, up_raw = zip(*(two_names(outer, f"up_lo{b}", [P, KD, DE], F32R, f"up_raw{b}", [P, KD, DE]) for b in range(2)))
        down_lo, down_raw = zip(*(two_names(outer, f"down_lo{b}", [P, KE, D], F32R, f"down_raw{b}", [P, KE, D]) for b in range(2)))
        wg_v = d["moe_w_gate"].rearrange("e (k p) n -> e p k n", p=P)
        wu_v = d["moe_w_up"].rearrange("e (k p) n -> e p k n", p=P)
        wd_v = d["moe_w_down"].rearrange("e (k p) n -> e p k n", p=P)

        def one(view, e):
            return (view[e:e + 1] if isinstance(e, int) else view[bass.ds(e, 1)]).rearrange("a p k n -> p (a k) n")

        with ExitStack() as s:
            def sb(name, *shape, dt=F32):
                return tile(s, name, [P, *shape], dt)

            g_max, g_pick, g_hot, g_exp = sb("g_max", NTR), sb("g_pick", NTR, N_GROUPS), sb("g_hot", NTR, N_GROUPS), sb("g_exp", NTR, N_GROUPS)
            g_prob, e_max, e_gap, e_ratio = sb("g_prob", NTR), sb("e_max", 2, NTR), sb("e_gap", NTR), sb("e_ratio", NTR)
            e_log, e_pick = sb("e_log", 2, NTR, NE), sb("e_pick", NTR, NE)
            hot, load, rank = sb("hot", 2, NTR, NE), sb("load", NTR + 1, NE), sb("rank", NTR, NE)
            both = sb("both", NTR, NE)
            count, over, more, more_before, more_end, base_gap = (sb(n, NE) for n in (
                "count", "over_unused", "more", "more_before", "more_end", "base_gap"))
            cmp_t, cmp_e, cmp_b = sb("cmp_t", NE, 8), sb("cmp_e", NE, NE), sb("cmp_b", EXTRA, NE)
            blk = sb("blk", EXTRA)
            r_of, s_of, g_of = sb("r_of", NTR), sb("s_of", NTR), sb("g_of", NTR)
            slot_f = sb("slot_f", 2, NTR)
            row_id = sb("row_id", NTR, dt=I32)
            row_f = sb("row_f", NTR)
            blank = sb("blank", NBLK)
            by_block = tile(s, "by_block", [NBLK, P])

            gl = logits[:, 1:NT, 0:N_GROUPS]
            el = logits[:, 1:NT, N_GROUPS:NR]

            with nc.Block() as block:
                @block.vector
                def _(dve):
                    n = [0]

                    def step(ins, name=None):
                        if name:
                            ins.then_inc(sem(name), 1)
                            dve.wait_ge(sem(name), 1)
                        else:
                            n[0] += 1
                            ins.then_inc(sem("route_step"), 1)
                            dve.wait_ge(sem("route_step"), n[0])

                    def tt(dst, a, b, op, name=None):
                        step(dve.tensor_tensor(dst, a, b, op), name)

                    def red(dst, a, op, name=None):
                        step(dve.tensor_reduce(dst, a, X, op), name)

                    def over_last(ap, w):
                        return ap.unsqueeze(2).to_broadcast([P, NTR, w])

                    def first_of_max(dst, pick, top, values, prio, w):
                        red(top, values, ALU.max)
                        tt(pick, values, over_last(top, w), ALU.is_equal)
                        tt(pick, pick, prio.unsqueeze(1).to_broadcast([P, NTR, w]), ALU.mult)
                        red(s_of[:], pick, ALU.max)
                        tt(dst, pick, over_last(s_of[:], w), ALU.is_equal)

                    dve.memset(blank[:], 0.0).then_inc(sem("blank_ready"), 1)
                    dve.wait_ge(sem("blank_ready"), 1)
                    dve.wait_ge(sem("row_id_ready"), 1)
                    dve.tensor_copy(row_f[:], row_id[:]).then_inc(sem("row_f_ready"), 1)
                    dve.wait_ge(sem("row_f_ready"), 1)
                    first_of_max(g_hot[:], g_pick[:], g_max[:], gl, cst("group_prio"), N_GROUPS)
                    tt(g_exp[:], gl, over_last(g_max[:], N_GROUPS), ALU.subtract, "g_exp_in")
                    step(dve.tensor_scalar(g_pick[:], g_hot[:], BIG, -BIG, ALU.mult, ALU.add))
                    tt(e_log[:, 0].rearrange("p t (g e) -> p t g e", g=N_GROUPS), el.rearrange("p t (g e) -> p t g e", g=N_GROUPS),
                       g_pick[:].unsqueeze(3).to_broadcast([P, NTR, N_GROUPS, PER_GROUP]), ALU.add)
                    first_of_max(hot[:, 0], e_pick[:], e_max[:, 0], e_log[:, 0], cst("expert_prio"), NE)
                    step(dve.scalar_tensor_tensor(e_log[:, 1], hot[:, 0], -3.0 * BIG, e_log[:, 0], ALU.mult, ALU.add))
                    first_of_max(hot[:, 1], e_pick[:], e_max[:, 1], e_log[:, 1], cst("expert_prio"), NE)
                    tt(e_gap[:], e_max[:, 1], e_max[:, 0], ALU.subtract, "e_gap_ready")
                    dve.wait_ge(sem("g_exp_ready"), 1)
                    red(g_prob[:], g_exp[:], ALU.add)
                    dve.wait_ge(sem("e_ratio_ready"), 1)
                    step(dve.tensor_scalar(e_gap[:], e_ratio[:], 1.0, None, ALU.add, ALU.bypass))
                    tt(g_prob[:], g_prob[:], e_gap[:], ALU.mult)
                    step(dve.reciprocal(weight[:, 0], g_prob[:]))
                    tt(weight[:, 1], weight[:, 0], e_ratio[:], ALU.mult)
                    tt(both[:], hot[:, 0], hot[:, 1], ALU.add)
                    step(dve.memset(load[:, 0], 0.0))
                    for j in range(NTR):
                        tt(load[:, j + 1], load[:, j], both[:, j], ALU.add, "load_ready" if j == NTR - 1 else None)
                    dve.wait_ge(sem("rank_done"), 1)
                    step(dve.tensor_copy(rank[:].rearrange("p t e -> p (t e)"), ps[:, 0, 0:NTR * NE]))
                    step(dve.tensor_copy(count[:], ps[:, 1, 0:NE]))
                    tt(cmp_t[:], count[:].unsqueeze(2).to_broadcast([P, NE, 8]),
                       cst("thresholds").unsqueeze(1).to_broadcast([P, NE, 8]), ALU.is_gt)
                    red(more[:], cmp_t[:], ALU.add)
                    tt(cmp_e[:], cst("before_e").rearrange("p (a b) -> p a b", a=NE),
                       more[:].unsqueeze(1).to_broadcast([P, NE, NE]), ALU.mult)
                    red(more_before[:], cmp_e[:], ALU.add)
                    tt(more_end[:], more_before[:], more[:], ALU.add)
                    tt(cmp_b[:], more_end[:].unsqueeze(1).to_broadcast([P, EXTRA, NE]),
                       cst("block_no").unsqueeze(2).to_broadcast([P, EXTRA, NE]), ALU.is_le)
                    red(blk[:], cmp_b[:], ALU.add)
                    step(dve.tensor_scalar(blk[:], blk[:], float(NE - 1), None, ALU.min, ALU.bypass))
                    step(dve.tensor_copy(extra[0:1, 1:1 + EXTRA], blk[0:1, :]))
                    dve.tensor_copy(extra[0:1, 0:1], more_end[0:1, NE - 1:NE]).then_inc(sem("extra_ready"), 1)
                    dve.wait_ge(sem("extra_ready"), 1)
                    step(dve.tensor_scalar(base_gap[:], more_before[:], float(P), float((NE - 1) * P), ALU.mult, ALU.add))
                    tt(base_gap[:], base_gap[:], cst("slot_base"), ALU.subtract)
                    for j in range(2):
                        for dst, table in ((r_of, rank[:]), (s_of, cst("slot_base").unsqueeze(1).to_broadcast([P, NTR, NE])),
                                           (g_of, base_gap[:].unsqueeze(1).to_broadcast([P, NTR, NE]))):
                            tt(e_pick[:], hot[:, j], table, ALU.mult)
                            red(dst[:], e_pick[:], ALU.add)
                        tt(s_of[:], s_of[:], r_of[:], ALU.add)
                        step(dve.tensor_scalar(r_of[:], r_of[:], float(P), None, ALU.is_ge, ALU.bypass))
                        tt(g_of[:], g_of[:], r_of[:], ALU.mult)
                        tt(slot_f[:, j], s_of[:], g_of[:], ALU.add)
                    dve.tensor_copy(slots[:], slot_f[:]).then_inc(sem("slots_ready"), 1)
                    dve.wait_ge(sem("slots_ready"), 1)
                    dve.wait_ge(sem("slot_rows_turned"), 1)
                    dve.tensor_copy(slot_row[:], ps[:, 2, 0:NBLK]).then_inc(sem("slot_row_ready"), 1)
                    dve.wait_ge(sem("slot_row_ready"), 1)

                @block.scalar
                def _(act):
                    act.wait_ge(sem("g_exp_in"), 1)
                    act.activation(g_exp[:], g_exp[:], ACT.Exp).then_inc(sem("g_exp_ready"), 1)
                    act.wait_ge(sem("e_gap_ready"), 1)
                    act.activation(e_ratio[:], e_gap[:], ACT.Exp).then_inc(sem("e_ratio_ready"), 1)

                @block.tensor
                def _(pe):
                    pe.wait_ge(sem("load_ready"), 1)
                    flat = lambda ap: ap.rearrange("p t e -> p (t e)")
                    pe.matmul(ps[:, 0, 0:NTR * NE], cst("before"), flat(both[:]), start=True, stop=False)
                    pe.matmul(ps[:, 0, 0:NTR * NE], cst("ones"), flat(load[:, 0:NTR]), start=False, stop=True)
                    pe.matmul(ps[:, 1, 0:NE], cst("ones"), load[:, NTR], start=True, stop=True).then_inc(sem("rank_done"), 1)
                    pe.wait_ge(sem("by_block_loaded"), 16)
                    pe.transpose(ps[:, 2, 0:NBLK], by_block[:], ident[0:NBLK, 0:NBLK]).then_inc(sem("slot_rows_turned"), 1)

                @block.gpsimd
                def _(pool):
                    pool.iota(row_id[:], [[P, NTR]], base=P, channel_multiplier=1).then_inc(sem("row_id_ready"), 1)
                    pool.wait_ge(sem("blank_stored"), 16)
                    pool.wait_ge(sem("row_f_ready"), 1)
                    pool.wait_ge(sem("slots_ready"), 1)
                    for j in range(2):
                        for t in range(NTR):
                            pool.indirect_dma_start(slot_row_dram, bass.IndirectOffsetOnAxis(ap=slots[:, j, t:t + 1], axis=0),
                                                    row_f[:, t:t + 1], None).then_inc(sem("slot_rows_stored"), 16)

                @block.sync
                def _(sp):
                    sp.wait_ge(sem("blank_ready"), 1)
                    sp.dma_start(slot_row_dram.rearrange("(b p) o -> p (b o)", p=P), blank[:],
                                 allow_slow_non_contiguous=True).then_inc(sem("blank_stored"), 16)
                    for e in range(2):
                        sp.dma_start(gate_raw[e][:], one(wg_v, e)).then_inc(sem("first_w_loaded"), 16)
                        sp.dma_start(up_raw[e][:], one(wu_v, e)).then_inc(sem("first_w_loaded"), 16)
                        sp.dma_start(down_raw[e][:], one(wd_v, e)).then_inc(sem("first_w_loaded"), 16)
                    sp.wait_ge(sem("slot_rows_stored"), 16 * 2 * NTR)
                    sp.dma_start(by_block[:], slot_row_dram.rearrange("(b p) o -> b (p o)", p=P)).then_inc(sem("by_block_loaded"), 16)
                    sp.wait_ge(sem("slot_row_ready"), 1)
                    sp.wait_ge(sem("first_w_loaded"), 16 * 6)
        free_sems()

        with ExitStack() as s:
            def sb(name, *shape):
                return tile(s, name, [P, *shape])

            h_at = -(-nc.sbuf_base // 32) * 32
            gate_hi, up_hi = tile(s, "gate_hi", [P, KD, DE], F32R), tile(s, "up_hi", [P, KD, DE], F32R)
            down_hi = tile(s, "down_hi", [P, KE, D], F32R)
            assert NTR * D <= 2 * KD * DE and 2 * NTR * D <= 4 * KD * DE
            h_in = nc.alloc_sbuf_tensor_at("h_last", [P, NTR, D], F32, offset=h_at)
            y_in = nc.alloc_sbuf_tensor_at("y_last", [P, 2, NTR, D], F32, offset=rows_at)
            matrices = {"gate": (gate_raw, gate_lo, gate_hi, 6), "up": (up_raw, up_lo, up_hi, 6),
                        "down": (down_raw, down_lo, down_hi, 3)}
            x_rows = [sb(f"x_rows{b}", D) for b in range(2)]
            x_hi, x_lo = (tile(s, n, [P, KD, P], F32R) for n in ("x_hi", "x_lo"))
            hid_hi, hid_lo = (tile(s, n, [P, KE, P], F32R) for n in ("hid_hi", "hid_lo"))
            act_t, hid = sb("act_t", DE), sb("hid", DE)
            y_out = [sb(f"y_out{b}", D) for b in range(2)]
            more_row = tile(s, "more_row", [P, 1], I32)
            gain = sb("norm_final_rows", D)
            rms = sb("rms", 3, NTR)

            def run_pairs(eng, body, count):
                body(0, 0, 0, True, False)
                body(1, 1, 0, False, False)
                with eng.Fori(1, count // 2 - 1) as i:
                    body(2 * i, 0, i, False, False)
                    body(2 * i + 1, 1, i, False, False)
                body(count - 2, 0, count // 2 - 1, False, False)
                body(count - 1, 1, count // 2 - 1, False, True)

            def over_extra(eng, body):
                total = eng.value_load(extra[0:1, 0:1], min_val=0, max_val=EXTRA)
                with eng.If(total > 0):
                    with eng.Fori(1, total + 1) as n:
                        body(n)

            def is_first(e):
                return isinstance(e, int) and e == 0

            with nc.Block() as block:
                @block.sync
                def _(sp):
                    sp.dma_start(gain[:], d["norm_final"].partition_broadcast(P)).then_inc(sem("last_gain_loaded"), 16)

                    for b in range(2):
                        sp.sem_inc(sem(f"w_gate_loaded{b}"), 16)
                        sp.sem_inc(sem(f"w_up_loaded{b}"), 16)
                        sp.sem_inc(sem(f"w_down_loaded{b}"), 16)

                    def gate_up(e, b):
                        sp.wait_ge(sem("gate_done"), e - 1)
                        sp.dma_start(gate_raw[b][:], one(wg_v, e)).then_inc(sem(f"w_gate_loaded{b}"), 16)
                        sp.wait_ge(sem("up_done"), e - 1)
                        sp.dma_start(up_raw[b][:], one(wu_v, e)).then_inc(sem(f"w_up_loaded{b}"), 16)

                    def down(e, b):
                        sp.wait_ge(sem("down_done"), e - 1)
                        sp.dma_start(down_raw[b][:], one(wd_v, e)).then_inc(sem(f"w_down_loaded{b}"), 16)
                    gate_up(2, 0)
                    gate_up(3, 1)
                    down(2, 0)
                    with sp.Fori(2, NE // 2) as i:
                        gate_up(2 * i, 0)
                        down(2 * i - 1, 1)
                        gate_up(2 * i + 1, 1)
                        down(2 * i, 0)
                    down(NE - 1, 1)

                    def more(n):
                        sp.wait_ge(sem("down_done"), n + NE - 1)
                        sp.wait_ge(sem("up_done"), n + NE - 1)
                        e = sp.value_load(extra[0:1, bass.ds(n, 1)], min_val=0, max_val=NE - 1)
                        sp.dma_start(gate_raw[0][:], one(wg_v, e)).then_inc(sem("more_w_loaded"), 16)
                        sp.dma_start(up_raw[0][:], one(wu_v, e)).then_inc(sem("more_w_loaded"), 16)
                        sp.dma_start(down_raw[0][:], one(wd_v, e)).then_inc(sem("more_w_loaded"), 16)
                        sp.wait_ge(sem("y_evacuated"), n + NE)
                        sp.dma_start(y_dram[bass.ds((n + (NE - 1)) * P, P), :], y_out[0][:]).then_inc(sem("more_y_stored"), 16)
                        sp.wait_ge(sem("more_y_stored"), n * 16)
                    over_extra(sp, more)
                    sp.sem_inc(sem("more_over"), 1)

                    sp.wait_ge(sem("up_done"), NE)
                    for t in range(NTR):
                        sp.dma_start(h_in[:, t, :], h2_dram[(t + 1) * P:(t + 2) * P, :]).then_inc(sem(f"h_last_loaded{t}"), 16)
                    sp.wait_ge(sem("out_stored"), 16 * NTR)

                @block.gpsimd
                def _(pool):
                    def bring_x(e):
                        if e >= 2:
                            pool.wait_ge(sem("x_turned"), e - 1)
                        pool.indirect_dma_start(x_rows[e % 2][:], None, u2_dram, bass.IndirectOffsetOnAxis(ap=slot_row[:, e:e + 1], axis=0)
                                                ).then_inc(sem(f"x_rows_loaded{e % 2}"), 16)

                    def low(name, e):
                        raw, lo, hi, cut = matrices[name]
                        pool.wait_ge(sem(f"{name}_hi_ready"), e + 1)
                        pool.tensor_tensor(lo[e % 2][:, cut:, :], raw[e % 2][:, cut:, :], hi[:, cut:, :].bitcast(F32),
                                           ALU.subtract).then_inc(sem(f"{name}_lo2_ready"), 1)
                    bring_x(0)
                    bring_x(1)
                    low("gate", 0)
                    for e in range(NE):
                        if e + 2 < NE:
                            bring_x(e + 2)
                        low("up", e)
                        if e >= 1:
                            low("down", e - 1)
                        if e + 1 < NE:
                            low("gate", e + 1)
                    low("down", NE - 1)

                    def more(n):
                        pool.wait_ge(sem("x_rows_loaded1"), 16 * NE // 2)
                        pool.wait_ge(sem("more_row_ready"), n)
                        pool.indirect_dma_start(x_rows[0][:], None, u2_dram, bass.IndirectOffsetOnAxis(ap=more_row[:, 0:1], axis=0)
                                                ).then_inc(sem("more_x_loaded"), 16)
                    over_extra(pool, more)

                    pool.wait_ge(sem("y_stored0"), 16 * NE // 2)
                    pool.wait_ge(sem("y_stored1"), 16 * NE // 2)
                    pool.wait_ge(sem("more_over"), 1)
                    for t in range(NTR):
                        for j in range(2):
                            pool.indirect_dma_start(y_in[:, j, t, :], None, y_dram,
                                                    bass.IndirectOffsetOnAxis(ap=slots[:, j, t:t + 1], axis=0)
                                                    ).then_inc(sem(f"y_in_loaded{t}"), 16)
                    for t in range(NTR):
                        pool.wait_ge(sem("rms_in"), t + 1)
                        pool.tensor_tensor(rms[:, 2, t:t + 1], rms[:, 1, t:t + 1], half[:, 0:1], ALU.pow
                                           ).then_inc(sem("rms_ready"), 1)

                @block.scalar
                def _(act):
                    def high(name, e, b):
                        raw, lo, hi, cut = matrices[name]
                        if not is_first(e):
                            act.wait_ge(sem(f"{name}_done"), e)
                        act.activation(hi[:], raw[b][:], ACT.Copy).then_inc(sem(f"{name}_hi_ready"), 1)

                    def turned_x(e):
                        act.wait_ge(sem("x_turned"), e + 1)
                        act.activation(x_hi[:], ps[:, 4:6, :].rearrange("p a (k t) -> p (a k) t", t=P), ACT.Copy
                                       ).then_inc(sem("x_hi_ready"), 1)

                    def gated(e):
                        act.wait_ge(sem("gate_done"), e + 1)
                        act.activation(act_t[:], ps[:, 0, :], ACT.Tanh, scale=0.5).then_inc(sem("act_t_ready"), 1)

                    def turned_hid(e):
                        act.wait_ge(sem("hid_turned"), e + 1)
                        act.activation(hid_hi[:], ps[:, 2, :].rearrange("p (k t) -> p k t", t=P), ACT.Copy
                                       ).then_inc(sem("hid_hi_ready"), 1)

                    def finish(e, b, n):
                        act.wait_ge(sem("down_done"), e + 1)
                        if not (isinstance(e, int) and e < 2):
                            act.wait_ge(sem(f"y_stored{b}"), 16 * n)
                        act.activation(y_out[b][:], ps[:, 6:8, :].rearrange("p a c -> p (a c)"), ACT.Copy).then_inc(sem("y_evacuated"), 1)
                        act.wait_ge(sem("y_evacuated"), e + 1)
                        act.dma_start(y_dram[bass.ds(e * P, P), :], y_out[b][:]).then_inc(sem(f"y_stored{b}"), 16)

                    def body(e, b, n, first, last):
                        if not (isinstance(e, int) and e < 2):
                            finish(e - 2, b, n - 1)
                        if not first:
                            act.wait_ge(sem(f"w_down_loaded{1 - b}"), 16 * (n + b))
                            high("down", e - 1, 1 - b)
                        gated(e)
                        if not first:
                            turned_hid(e - 1)
                        if not last:
                            act.wait_ge(sem(f"w_gate_loaded{1 - b}"), 16 * (n + b + 1))
                            high("gate", e + 1, 1 - b)
                            turned_x(e + 1)
                            act.wait_ge(sem(f"w_up_loaded{1 - b}"), 16 * (n + b + 1))
                            high("up", e + 1, 1 - b)
                    act.wait_ge(sem("w_gate_loaded0"), 16)
                    high("gate", 0, 0)
                    act.wait_ge(sem("w_up_loaded0"), 16)
                    high("up", 0, 0)
                    turned_x(0)
                    run_pairs(act, body, NE)
                    finish(NE - 2, 0, NE // 2 - 1)
                    act.wait_ge(sem("w_down_loaded1"), 16 * (NE // 2))
                    high("down", NE - 1, 1)
                    turned_hid(NE - 1)
                    finish(NE - 1, 1, NE // 2 - 1)
                    act.wait_ge(sem("y_stored0"), 16 * NE // 2)

                    def more(n):
                        e = n + (NE - 1)
                        act.wait_ge(sem("more_w_loaded"), n * 48)
                        for name in ("gate", "up", "down"):
                            high(name, e, 0)
                        turned_x(e)
                        gated(e)
                        turned_hid(e)
                        act.wait_ge(sem("down_done"), n + NE)
                        act.activation(y_out[0][:], ps[:, 6:8, :].rearrange("p a c -> p (a c)"), ACT.Copy).then_inc(sem("y_evacuated"), 1)
                    over_extra(act, more)

                    for t in range(NTR):
                        act.wait_ge(sem("h3_ready"), t + 1)
                        act.activation(y_in[:, 0, t, :], h_in[:, t, :], ACT.Square, scale=D ** -0.5, accum_out=rms[:, 0, t:t + 1]
                                       ).then_inc(sem("last_mean_square"), 1)
                        if t >= 1:
                            act.wait_ge(sem("out_ready"), t)
                            act.dma_start(out[(t - 1) * P:t * P, :], y_in[:, 1, t - 1, :]).then_inc(sem("out_stored"), 16)
                    act.wait_ge(sem("out_ready"), NTR)
                    act.dma_start(out[(NTR - 1) * P:NTR * P, :], y_in[:, 1, NTR - 1, :]).then_inc(sem("out_stored"), 16)

                @block.vector
                def _(dve):
                    def low(name, e, b, whole=False):
                        raw, lo, hi, cut = matrices[name]
                        cut = None if whole else cut
                        dve.wait_ge(sem(f"{name}_hi_ready"), e + 1)
                        dve.tensor_tensor(lo[b][:, :cut, :], raw[b][:, :cut, :], hi[:, :cut, :].bitcast(F32),
                                          ALU.subtract).then_inc(sem(f"{name}_lo_ready"), 1)

                    def turned_x(e):
                        dve.wait_ge(sem("x_hi_ready"), e + 1)
                        dve.tensor_tensor(x_lo[:], ps[:, 4:6, :].rearrange("p a (k t) -> p (a k) t", t=P), x_hi[:].bitcast(F32),
                                          ALU.subtract).then_inc(sem("x_lo_ready"), 1)

                    def turned_hid(e):
                        dve.wait_ge(sem("hid_hi_ready"), e + 1)
                        dve.tensor_tensor(hid_lo[:], ps[:, 2, :].rearrange("p (k t) -> p k t", t=P), hid_hi[:].bitcast(F32),
                                          ALU.subtract).then_inc(sem("hid_lo_ready"), 1)

                    def half_hid(e):
                        dve.wait_ge(sem("act_t_ready"), e + 1)
                        if not is_first(e):
                            dve.wait_ge(sem("hid_turned"), e)
                        dve.scalar_tensor_tensor(hid[:], act_t[:], 1.0, ps[:, 0, :], ALU.add, ALU.mult).then_inc(sem("hid_half"), 1)

                    def whole_hid(e):
                        dve.wait_ge(sem("hid_half"), e + 1)
                        dve.wait_ge(sem("up_done"), e + 1)
                        dve.scalar_tensor_tensor(hid[:], hid[:], 0.5, ps[:, 1, :], ALU.mult, ALU.mult).then_inc(sem("hid_ready"), 1)

                    def body(e, b, n, first, last):
                        low("up", e, b)
                        if not first:
                            low("down", e - 1, 1 - b)
                            turned_hid(e - 1)
                        half_hid(e)
                        if not last:
                            low("gate", e + 1, 1 - b)
                            turned_x(e + 1)
                        whole_hid(e)
                    low("gate", 0, 0)
                    turned_x(0)
                    run_pairs(dve, body, NE)
                    low("down", NE - 1, 1)
                    turned_hid(NE - 1)

                    def more(n):
                        e = n + (NE - 1)
                        dve.tensor_copy(more_row[:], slot_row[:, bass.ds(n + (NE - 1), 1)]).then_inc(sem("more_row_ready"), 1)
                        for name in ("gate", "up", "down"):
                            low(name, e, 0, whole=True)
                        turned_x(e)
                        half_hid(e)
                        whole_hid(e)
                        turned_hid(e)
                    over_extra(dve, more)

                    def add_rows(t):
                        dve.wait_ge(sem(f"h_last_loaded{t}"), 16)
                        dve.wait_ge(sem(f"y_in_loaded{t}"), 32)
                        for j in range(2):
                            dve.scalar_tensor_tensor(h_in[:, t, :], y_in[:, j, t, :], weight[:, j, t:t + 1], h_in[:, t, :], ALU.mult, ALU.add
                                                     ).then_inc(sem("h3_ready" if j else "h3_first"), 1)
                            dve.wait_ge(sem("h3_ready" if j else "h3_first"), t + 1)

                    def last_norm(t):
                        dve.wait_ge(sem("rms_ready"), t + 1)
                        dve.scalar_tensor_tensor(y_in[:, 1, t, :], h_in[:, t, :], rms[:, 2, t:t + 1], gain[:], ALU.mult, ALU.mult
                                                 ).then_inc(sem("out_ready"), 1)
                    dve.wait_ge(sem("last_gain_loaded"), 16)
                    add_rows(0)
                    for t in range(NTR):
                        dve.wait_ge(sem("last_mean_square"), t + 1)
                        dve.tensor_scalar(rms[:, 1, t:t + 1], rms[:, 0, t:t + 1], 1e-6, None, ALU.add, ALU.bypass
                                          ).then_inc(sem("rms_in"), 1)
                        if t + 1 < NTR:
                            add_rows(t + 1)
                        last_norm(t)

                @block.tensor
                def _(pe):
                    def turn_x(e, b):
                        if not is_first(e):
                            pe.wait_ge(sem("x_hi_ready"), e)
                            pe.wait_ge(sem("x_lo_ready"), e)
                        for k in range(KD):
                            mm = pe.transpose(ps[:, 4 + k // 4, (k % 4) * P:(k % 4 + 1) * P], x_rows[b][:, k * P:(k + 1) * P], ident)
                        mm.then_inc(sem("x_turned"), 1)

                    def product(bank, a_hi, a_lo, hi, lo, ks, cols=slice(None)):
                        for k in range(ks):
                            for i, (a, w) in enumerate(((a_hi, hi), (a_hi, lo), (a_lo, hi))):
                                mm = pe.matmul(ps[:, bank, :], a[:, k, :], w[:, k, cols],
                                               start=(k == 0 and i == 0), stop=(k == ks - 1 and i == 2))
                        return mm

                    def gate(e, b):
                        pe.wait_ge(sem("x_hi_ready"), e + 1)
                        pe.wait_ge(sem("x_lo_ready"), e + 1)
                        pe.wait_ge(sem("gate_hi_ready"), e + 1)
                        pe.wait_ge(sem("gate_lo_ready"), e + 1)
                        if not is_first(e):
                            pe.wait_ge(sem("hid_half"), e)
                        product(0, x_hi, x_lo, gate_hi, gate_lo[b], KD).then_inc(sem("gate_done"), 1)

                    def up(e, b):
                        pe.wait_ge(sem("up_hi_ready"), e + 1)
                        pe.wait_ge(sem("up_lo_ready"), e + 1)
                        if not is_first(e):
                            pe.wait_ge(sem("hid_ready"), e)
                        product(1, x_hi, x_lo, up_hi, up_lo[b], KD).then_inc(sem("up_done"), 1)

                    def turn_hid(e):
                        pe.wait_ge(sem("hid_ready"), e + 1)
                        for k in range(KE):
                            mm = pe.transpose(ps[:, 2, k * P:(k + 1) * P], hid[:, k * P:(k + 1) * P], ident)
                        mm.then_inc(sem("hid_turned"), 1)

                    def down(e, b):
                        pe.wait_ge(sem("hid_hi_ready"), e + 1)
                        pe.wait_ge(sem("hid_lo_ready"), e + 1)
                        pe.wait_ge(sem("down_hi_ready"), e + 1)
                        pe.wait_ge(sem("down_lo_ready"), e + 1)
                        if not is_first(e):
                            pe.wait_ge(sem("y_evacuated"), e)
                        product(6, hid_hi, hid_lo, down_hi, down_lo[b], KE, slice(0, 512))
                        product(7, hid_hi, hid_lo, down_hi, down_lo[b], KE, slice(512, D)).then_inc(sem("down_done"), 1)

                    def body(e, b, n, first, last):
                        pe.wait_ge(sem("gate_lo2_ready"), e + 1)
                        gate(e, b)
                        if not first:
                            turn_hid(e - 1)
                        pe.wait_ge(sem("up_lo2_ready"), e + 1)
                        up(e, b)
                        if not last:
                            pe.wait_ge(sem(f"x_rows_loaded{1 - b}"), 16 * (n + 1 + b))
                            turn_x(e + 1, 1 - b)
                        if not first:
                            pe.wait_ge(sem("down_lo2_ready"), e)
                            down(e - 1, 1 - b)
                        if last:
                            turn_hid(e)
                            pe.wait_ge(sem("down_lo2_ready"), e + 1)
                            down(e, b)
                    pe.wait_ge(sem("x_rows_loaded0"), 16)
                    turn_x(0, 0)
                    run_pairs(pe, body, NE)

                    def more(n):
                        e = n + (NE - 1)
                        pe.wait_ge(sem("more_x_loaded"), n * 16)
                        turn_x(e, 0)
                        gate(e, 0)
                        up(e, 0)
                        turn_hid(e)
                        down(e, 0)
                    over_extra(pe, more)


_NAMES = ['x', 'meta_tokens', 'norm_mix', 'w_in', 'shift_mu', 'decay_w0', 'decay_up', 'iclr_a0', 'iclr_up', 'gate_up',
          'k_k', 'k_a', 'r_k', 'ln_w_a', 'ln_b_a', 'gn_w_b', 'w_out', 'norm_ffn', 'router_group_w', 'router_group_b',
          'router_expert_w', 'router_expert_b', 'moe_w_gate', 'moe_w_up', 'moe_w_down', 'norm_final']


def kernel(**inputs):
    import concourse.bacc as bacc
    from concourse.bass_utils import run_bass_kernel_spmd

    nc = bacc.Bacc("TRN2", target_bir_lowering=False, num_devices=1)
    table, rotation = shape_constants()
    arrays = {"consts": table, "rotation": rotation}
    for name in _NAMES:
        a = np.ascontiguousarray(inputs[name])
        if name not in ("meta_tokens", "norm_final"):
            a = a[0]
        arrays[name] = a
    data = {}
    for name, a in arrays.items():
        data[name] = nc.dram_tensor("in_" + name, a.shape, mybir.dt.from_np(a.dtype), kind="ExternalInput").ap()
    out = nc.dram_tensor("out_rows", (SEQ, D), F32, kind="ExternalOutput").ap()
    layer(nc, data, out)
    r = run_bass_kernel_spmd(nc, [{"in_" + n: a for n, a in arrays.items()}], core_ids=[0])
    return r.results[0]["out_rows"].reshape(1, SEQ, D)
```
